# Optimizing a Trainium2 kernel written in Bass

```python
import math
import jax, jax.numpy as jnp
from jax import lax
import numpy as np

D_MODEL = 1024
BATCH = 1
SEQ = 512
DEPTH = 2

CHUNK = 64
GLA_HEADS = 4
GLA_DK = 64
GLA_DV = 128
GLA_GATE_RANK = 16
GLA_TAU = 16.0
SB_HEADS = 8
SB_DIM = 64
SB_BLOCK = 128
C_HEADS = 16
C_KV_HEADS = 4
C_DIM = 64
SWA_WINDOW = 128
N_WIN_CHUNKS = SWA_WINDOW // CHUNK
T5_BUCKETS = 32
T5_MAX_DIST = 128
D_FF = 2816
CONV_WIDTH = 3
EPS = 1e-6

AB_SPLITS = [GLA_HEADS * GLA_DK, GLA_HEADS * GLA_DK, GLA_HEADS * GLA_DV,
             GLA_HEADS * GLA_DV, GLA_GATE_RANK,
             SB_HEADS * SB_DIM, SB_HEADS * SB_DIM, SB_HEADS * SB_DIM]
AB_IN = sum(AB_SPLITS)
AB_OUT_IN = GLA_HEADS * GLA_DV + SB_HEADS * SB_DIM
C_SPLITS = [C_HEADS * C_DIM, C_KV_HEADS * C_DIM, C_KV_HEADS * C_DIM]
C_IN = sum(C_SPLITS)

kernel_name = "hybrid_gla_stickbreak_swa_convffn"

def rms_norm(x, g):
    xf = x.astype(jnp.float32)
    y = xf * lax.rsqrt(jnp.mean(xf * xf, axis=-1, keepdims=True) + EPS)
    return (y * g.astype(jnp.float32)).astype(x.dtype)

def split_cols(t, sizes):
    return jnp.split(t, np.cumsum(sizes)[:-1].tolist(), axis=-1)

def gla_chunk_causal(q, k, v, log_a):
    B, T, H, K = q.shape
    V = v.shape[-1]
    n_chunks = T // CHUNK
    f = lambda t: t.astype(jnp.float32).reshape(B, n_chunks, CHUNK, H, t.shape[-1])
    q, k, v, log_a = f(q), f(k), f(v), f(log_a)
    cum = jnp.cumsum(log_a, axis=2)
    total = cum[:, :, -1]
    kv = jnp.einsum('bclhk,bclhv->bchkv', k * jnp.exp(total[:, :, None] - cum), v)

    def step(state, inp):
        decay, kv_c = inp
        state = decay[..., None] * state + kv_c
        return state, state

    _, states = lax.scan(step, jnp.zeros((B, H, K, V), jnp.float32),
                         (jnp.moveaxis(jnp.exp(total), 1, 0), jnp.moveaxis(kv, 1, 0)))
    states = jnp.moveaxis(states, 0, 1)
    o = jnp.einsum('bclhk,bchkv->bclhv', q, states)
    return o.reshape(B, T, H, V)

def stick_breaking(q, k, v):
    B, T, H, Dh = q.shape
    n_blocks = T // SB_BLOCK
    scale = Dh ** -0.5
    qb = q.reshape(B, n_blocks, SB_BLOCK, H, Dh).transpose(1, 0, 3, 2, 4)
    kpos = jnp.arange(T)

    def block(args):
        qi, i = args
        z = jnp.einsum('bhqd,bkhd->bhqk', qi, k).astype(jnp.float32) * scale
        qpos = i * SB_BLOCK + jnp.arange(SB_BLOCK)
        mask = kpos[None, :] < qpos[:, None]
        log_beta = jax.nn.log_sigmoid(z)
        log_1m = jnp.where(mask, jax.nn.log_sigmoid(-z), 0.0)
        suffix = lax.cumsum(log_1m, axis=3, reverse=True) - log_1m
        w = jnp.where(mask, jnp.exp(log_beta + suffix), 0.0)
        return jnp.einsum('bhqk,bkhd->bqhd', w.astype(v.dtype), v)

    out = lax.map(block, (qb, jnp.arange(n_blocks)))
    return out.transpose(1, 0, 2, 3, 4).reshape(B, T, H, Dh)

def t5_bucket(rel):
    nb = T5_BUCKETS // 2
    max_exact = nb // 2
    n = np.abs(rel)
    large = max_exact + (np.log(np.maximum(n, 1) / max_exact)
                         / math.log(T5_MAX_DIST / max_exact) * (nb - max_exact)).astype(np.int32)
    large = np.minimum(large, nb - 1)
    return (np.where(rel > 0, nb, 0) + np.where(n < max_exact, n, large)).astype(np.int32)

def band_keys(t, n_chunks):
    parts = []
    for off in range(N_WIN_CHUNKS - 1, -1, -1):
        parts.append(jnp.pad(t, ((0, 0), (off, 0), (0, 0), (0, 0), (0, 0)))[:, :n_chunks])
    return jnp.concatenate(parts, axis=2)

def swa_gqa_sinks(q, k, v, sinks, rel_bias):
    B, T, Hq, Dh = q.shape
    Hkv = k.shape[2]
    G = Hq // Hkv
    L = CHUNK
    W = N_WIN_CHUNKS * L
    n_chunks = T // L
    qc = q.reshape(B, n_chunks, L, Hkv, G, Dh)
    kw = band_keys(k.reshape(B, n_chunks, L, Hkv, Dh), n_chunks)
    vw = band_keys(v.reshape(B, n_chunks, L, Hkv, Dh), n_chunks)
    s = jnp.einsum('bcqhgd,bckhd->bchgqk', qc, kw).astype(jnp.float32) * (Dh ** -0.5)
    rel = np.arange(W)[None, :] - ((N_WIN_CHUNKS - 1) * L + np.arange(L)[:, None])
    bias = rel_bias.astype(jnp.float32)[t5_bucket(rel)]
    bias = bias.transpose(2, 0, 1).reshape(Hkv, G, L, W)
    offs = (N_WIN_CHUNKS - 1) - np.arange(W) // L
    valid = (np.arange(n_chunks)[:, None] - offs[None, :]) >= 0
    s = jnp.where(valid[None, :, None, None, None, :], s + bias, -1e30)
    sink = jnp.broadcast_to(sinks.astype(jnp.float32).reshape(1, 1, Hkv, G, 1, 1),
                            s.shape[:-1] + (1,))
    p = jax.nn.softmax(jnp.concatenate([s, sink], axis=-1), axis=-1)[..., :-1]
    o = jnp.einsum('bchgqk,bckhd->bcqhgd', p.astype(v.dtype), vw)
    return o.reshape(B, T, Hq, Dh)

def mixer_gla_sb(h, w_in, w_gate2, b_gate, gla_norm, w_out):
    B, T, _ = h.shape
    qa, ka, va, ra, ga, qb, kb, vb = split_cols(h @ w_in, AB_SPLITS)
    log_a = jax.nn.log_sigmoid((ga @ w_gate2 + b_gate).astype(jnp.float32)) / GLA_TAU
    hd = lambda t, n: t.reshape(B, T, n, -1)
    o_a = gla_chunk_causal(hd(qa, GLA_HEADS) * (GLA_DK ** -0.5), hd(ka, GLA_HEADS),
                           hd(va, GLA_HEADS), hd(log_a, GLA_HEADS))
    o_a = o_a * lax.rsqrt(jnp.mean(o_a * o_a, axis=-1, keepdims=True) + EPS)
    o_a = o_a.reshape(B, T, -1) * gla_norm.astype(jnp.float32)
    o_a = (o_a * jax.nn.silu(ra.astype(jnp.float32))).astype(h.dtype)
    o_b = stick_breaking(hd(qb, SB_HEADS), hd(kb, SB_HEADS), hd(vb, SB_HEADS))
    return jnp.concatenate([o_a, o_b.reshape(B, T, -1).astype(h.dtype)], axis=-1) @ w_out

def mixer_swa(h, w_qkv, sinks, w_out, rel_bias):
    B, T, _ = h.shape
    q, k, v = split_cols(h @ w_qkv, C_SPLITS)
    o = swa_gqa_sinks(q.reshape(B, T, C_HEADS, C_DIM), k.reshape(B, T, C_KV_HEADS, C_DIM),
                      v.reshape(B, T, C_KV_HEADS, C_DIM), sinks, rel_bias)
    return o.reshape(B, T, -1) @ w_out

def conv_ffn(h, w_up, conv_w, conv_b, w_down):
    T = h.shape[1]
    u = h @ w_up
    up = jnp.pad(u, ((0, 0), (CONV_WIDTH - 1, 0), (0, 0)))
    c = conv_b + sum(up[:, i:i + T] * conv_w[i] for i in range(CONV_WIDTH))
    g, val = jnp.split(c, 2, axis=-1)
    return (jax.nn.gelu(g) * val) @ w_down

def setup_inputs(seed: int = 0) -> dict:
    key = jax.random.key(seed)
    ks = jax.random.split(key, 20)
    n_even = (DEPTH + 1) // 2
    n_odd = DEPTH // 2
    f32 = jnp.float32

    def w(k, shape, fan_in):
        return jax.random.normal(k, shape, f32) * fan_in ** -0.5

    def gain(k, shape):
        return 1.0 + 0.05 * jax.random.normal(k, shape, f32)

    return {
        "x": jax.random.normal(ks[0], (BATCH, SEQ, D_MODEL), f32),
        "norm_mix": gain(ks[1], (DEPTH, D_MODEL)),
        "norm_ffn": gain(ks[2], (DEPTH, D_MODEL)),
        "norm_final": gain(ks[3], (D_MODEL,)),
        "ab_w_in": w(ks[4], (n_even, D_MODEL, AB_IN), D_MODEL),
        "ab_w_gate2": w(ks[5], (n_even, GLA_GATE_RANK, GLA_HEADS * GLA_DK), GLA_GATE_RANK),
        "ab_b_gate": 0.1 * jax.random.normal(ks[6], (n_even, GLA_HEADS * GLA_DK), f32),
        "ab_gla_norm": gain(ks[7], (n_even, GLA_HEADS * GLA_DV)),
        "ab_w_out": w(ks[8], (n_even, AB_OUT_IN, D_MODEL), AB_OUT_IN),
        "c_w_qkv": w(ks[9], (n_odd, D_MODEL, C_IN), D_MODEL),
        "c_sinks": 0.5 * jax.random.normal(ks[10], (n_odd, C_HEADS), f32),
        "c_w_out": w(ks[11], (n_odd, C_HEADS * C_DIM, D_MODEL), C_HEADS * C_DIM),
        "rel_bias": 0.5 * jax.random.normal(ks[12], (T5_BUCKETS, C_HEADS), f32),
        "ffn_w_up": w(ks[13], (DEPTH, D_MODEL, 2 * D_FF), D_MODEL),
        "ffn_conv_w": w(ks[14], (DEPTH, CONV_WIDTH, 2 * D_FF), CONV_WIDTH),
        "ffn_conv_b": 0.01 * jax.random.normal(ks[15], (DEPTH, 2 * D_FF), f32),
        "ffn_w_down": w(ks[16], (DEPTH, D_FF, D_MODEL), D_FF),
    }

def reference(x, norm_mix, norm_ffn, norm_final, ab_w_in, ab_w_gate2, ab_b_gate,
              ab_gla_norm, ab_w_out, c_w_qkv, c_sinks, c_w_out, rel_bias,
              ffn_w_up, ffn_conv_w, ffn_conv_b, ffn_w_down):
    for layer in range(DEPTH):
        i = layer // 2
        h = rms_norm(x, norm_mix[layer])
        if layer % 2 == 0:
            x = x + mixer_gla_sb(h, ab_w_in[i], ab_w_gate2[i], ab_b_gate[i],
                                 ab_gla_norm[i], ab_w_out[i])
        else:
            x = x + mixer_swa(h, c_w_qkv[i], c_sinks[i], c_w_out[i], rel_bias)
        h = rms_norm(x, norm_ffn[layer])
        x = x + conv_ffn(h, ffn_w_up[layer], ffn_conv_w[layer], ffn_conv_b[layer],
                         ffn_w_down[layer])
    return rms_norm(x, norm_final)


_drawn_inputs = setup_inputs


def setup_inputs(seed=0):
    import zlib

    import numpy as np

    out = dict(_drawn_inputs(seed))
    spreads = {}
    factors = {'ab_b_gate': 2.734, 'c_sinks': 8.0, 'ffn_conv_b': 5.589}
    for name, (base, spread) in spreads.items():
        noise = np.random.default_rng([zlib.crc32(name.encode()), seed]).standard_normal(out[name].shape)
        drawn = base * np.exp(spread * noise) if base else spread * noise
        out[name] = __import__('jax').numpy.asarray(drawn.astype(out[name].dtype))
    for name, factor in factors.items():
        out[name] = (out[name] * factor).astype(out[name].dtype)
    return out
```

```python
from contextlib import ExitStack

import numpy as np

import concourse.bass as bass
from concourse import mybir

F32 = mybir.dt.float32
F32R = mybir.dt.float32r
BF16 = mybir.dt.bfloat16
ACT = mybir.ActivationFunctionType
ALU = mybir.AluOpType
AX = mybir.AxisListType

P = 128
T = 512
D = 1024
KC = D // P
TT = T // P
LAYERS = 2
CHUNK = 64
NCH = T // CHUNK
GH, GK, GV = 4, 64, 128
RANK = 16
TAU = 16.0
SH, SD = 8, 64
CH, CKV, CD = 16, 4, 64
DFF = 2816
FC = DFF // P
EPS = 1e-6
NEG = -1e30
RAW = 4
SPL = 2
UC = KC * P

MIX0 = ([("ra", i) for i in range(4)]
        + [("qb", 0), ("kb", 0), ("qb", 1), ("kb", 1), ("qb", 2), ("kb", 2)]
        + [("vb", i) for i in range(4)] + [("ka", 0), ("ka", 1), ("ga", 0)]
        + [("va", i) for i in range(4)]
        + [("qa", 0), ("qa", 1), ("qb", 3), ("kb", 3)])
N0 = len(MIX0)
MIX1 = [("k", 0), ("k", 1), ("v", 0), ("v", 1)] + [("q", i) for i in range(8)]
N1 = len(MIX1)
UP = 2 * FC
DN = (6, 6, 5, 5)
DOFF = (0, 6, 12, 17)
U_OUT0 = N0
U_UP0 = U_OUT0 + KC
U_DN0 = U_UP0 + UP
U_MIX1 = U_DN0 + 4 * KC
U_OUT1 = U_MIX1 + N1
U_UP1 = U_OUT1 + KC
U_DN1 = U_UP1 + UP
U_END = U_DN1 + 4 * KC

def mix0_order():
    fill = {0: [14, 15], 1: [16, 17], 2: [18, 19], 3: [20, 21], 4: [22, 23], 5: [24]}
    gla = {(5, 1): "gz", (6, 0): "gs", (6, 1): "gkv", (7, 1): "go"}
    seq = [("unit", 0), ("ssq", 0), ("unit", 1), ("rinv", 0)] + [("unit", u) for u in range(2, 14)]
    for h in range(SH):
        for half in range(2):
            if half < len(fill.get(h, [])):
                seq.append(("unit", fill[h][half]))
            if (h, half) in gla:
                seq.append((gla[h, half], 0))
            if half == 0:
                seq.append(("z", h))
                if h:
                    seq.append(("pv", h - 1))
        seq.append(("sfx", h))
    return seq + [("gn", 0), ("pv", SH - 1)]


def mix1_order():
    seq = [("unit", 0), ("ssq", 0), ("unit", 1), ("rinv", 0)] + [("unit", u) for u in range(2, 6)]
    for n in range(CH // 2):
        if n:
            seq.append(("t", n - 1))
        seq.append(("s", n))
        if 6 + n < N1:
            seq.append(("unit", 6 + n))
        if n:
            seq.append(("o", n - 1))
    return seq + [("t", CH // 2 - 1), ("o", CH // 2 - 1)]


SEQ0, SEQ1 = mix0_order(), mix1_order()


S_GAIN = 0
S_GLA = S_GAIN + 5 * KC
S_CONV = S_GLA + GH
S_SINK = S_CONV + LAYERS * UP * 4
S_END = S_SINK + CH // 2

ZOFF = (0, 512, 1024, 896)
ZW = (512, 384, 256, 128)
ZN = 1280


def trunk(nc, xT, w_mix0, w_mix1, w_up, w_down, small, wg2, bias, out):
    ctx = ExitStack()
    with ctx:
        def sb(name, shape, dt=F32, where=ctx):
            return where.enter_context(nc.sbuf_tensor(name, shape, dt))

        def sem(name):
            return ctx.enter_context(nc.semaphore(name))

        x = sb("x", [P, KC, T])
        h_hi = sb("h_hi", [P, KC, T], F32R)
        h_lo = sb("h_lo", [P, KC, T], F32R)
        w_raw = [sb(f"w_raw{r}", [P, UC]) for r in range(RAW)]
        w_hi = [sb(f"w_hi{s}", [P, UC], F32R) for s in range(SPL)]
        w_lo = [sb(f"w_lo{s}", [P, UC], F32R) for s in range(SPL)]
        par = sb("par", [P, S_END])
        rinv = sb("rinv", [P, T])
        rinv_col = sb("rinv_col", [P, TT])
        var_col = sb("var_col", [P, TT])
        mhalf = sb("mhalf", [P, TT])
        eps_col = sb("eps_col", [P, 1])
        gelu_warm = sb("gelu_warm", [P, 1])
        ssq = sb("ssq", [P, T])
        sq = sb("sq", [P, T])
        ident = sb("ident", [P, P])
        ones = sb("ones", [P, P])
        diag = sq

        m0 = ExitStack()

        def s0(name, shape, dt=F32):
            return sb(name, shape, dt, m0)

        ident_bf = s0("ident_bf", [P, P], BF16)
        negmask = s0("negmask", [P, P], BF16)
        negtri = s0("negtri", [P, P], F32R)
        negones = s0("negones", [P, P], F32R)
        tri_f = s0("tri_f", [P, P])
        tri16 = s0("tri16", [P, P])
        ind16 = s0("ind16", [P, 2])
        raT = s0("raT", [P, GH, T])
        qbT = s0("qbT", [P, SH // 2, T])
        kbT = s0("kbT", [P, SH // 2, T])
        vb = s0("vb", [P, TT, SH * SD])
        va = s0("va", [P, TT, GH * GV])
        ka = s0("ka", [P, TT, GH * GK])
        qaT = s0("qaT", [P, GH // 2, T])
        gaT = s0("gaT", [RANK + 1, T])
        wg2_sb = s0("wg2_sb", [RANK + 1, GH * GK])
        sbE = s0("sbE", [P, ZN])
        sbS = s0("sbS", [P, ZN])
        sbH = s0("sbH", [P, ZN], F32R)
        sbL = s0("sbL", [P, ZN], F32R)
        gE = s0("gE", [P, TT * GH * GK])
        gL = s0("gL", [P, TT * GH * GK])
        dec = s0("dec", [P, GH // 2, NCH])
        oc_hi = s0("oc_hi", [P, KC, T], F32R)
        oc_lo = s0("oc_lo", [P, KC, T], F32R)
        m0.close()
        st = [b[:, 0:2, :].rearrange("p a t -> p (a t)").rearrange("p (c v) -> p c v", c=NCH)
              for b in (qbT, kbT)]
        oF = va
        gq = [b[:, :].rearrange("p (a t) -> p a t", a=2) for b in (gE, gL)]

        m1 = ExitStack()

        def s1(name, shape, dt=F32):
            return sb(name, shape, dt, m1)

        q1 = s1("q1", [P, KC // 2, NCH, 2, CHUNK])
        k1 = s1("k1", [P, 2, CHUNK + T])
        v1 = s1("v1", [P, TT, CKV * CD])
        v1s = s1("v1s", [P, TT, CKV * CD])
        bias_sb = s1("bias_sb", [P, CH // 2, P])
        sc = s1("sc", [P, NCH, P])
        pr = s1("pr", [P, NCH, P])
        prT = s1("prT", [P, NCH, P])
        mx = s1("mx", [P, NCH])
        nm = s1("nm", [P, NCH])
        rs = s1("rs", [P, NCH])
        es = s1("es", [P, NCH])
        den = s1("den", [P, NCH])
        rd = s1("rd", [P, NCH])
        o1_hi = s1("o1_hi", [P, KC, T], F32R)
        o1_lo = s1("o1_lo", [P, KC, T], F32R)
        m1.close()

        y_hi = sb("y_hi", [P, FC, T], F32R)
        y_lo = sb("y_lo", [P, FC, T], F32R)
        us = [sb(f"us{k}", [P, 2 + T]) for k in range(2)]
        cv = [sb(f"cv{k}", [P, T]) for k in range(2)]

        ps = ctx.enter_context(nc.psum_tensor("ps", [P, 8, T], F32))
        zs = ps[:, 4:7, :].rearrange("p b t -> p (b t)")
        B_O = 7
        B_RES = 4
        B_SSQ, B_RINV = 6, 7
        B_SC, B_T, B_PV = 2, 4, 6

        w_loaded = [sem(f"w_loaded{r}") for r in range(RAW)]
        w_hi_ready = sem("w_hi_ready")
        w_lo_ready = sem("w_lo_ready")
        unit_done = sem("unit_done")
        x_loaded = [sem(f"x_loaded{i}") for i in range(4)]
        par_loaded = sem("par_loaded")
        wg2_loaded = sem("wg2_loaded")
        bias_loaded = sem("bias_loaded")
        consts = sem("consts")
        consts_dve = sem("consts_dve")
        sq_ready = sem("sq_ready")
        ssq_added = sem("ssq_added")
        hi_ready = sem("hi_ready")
        lo_ready = sem("lo_ready")
        x_updated = sem("x_updated")
        ssq_col = sem("ssq_col")
        var_ready = sem("var_ready")
        rcol_ready = sem("rcol_ready")
        diag_ready = sem("diag_ready")
        rbc_done = sem("rbc_done")
        rinv_ready = sem("rinv_ready")
        a_taken = sem("a_taken")
        b_taken = sem("b_taken")
        sb_z = sem("sb_z")
        sb_abs = sem("sb_abs")
        sb_e = sem("sb_e")
        sb_ln = sem("sb_ln")
        sb_sp = sem("sb_sp")
        sb_hi = sem("sb_hi")
        sb_lo = sem("sb_lo")
        sb_sum = sem("sb_sum")
        sb_w = sem("sb_w")
        sb_pv = sem("sb_pv")
        oc_hi_ready = sem("oc_hi_ready")
        oc_lo_ready = sem("oc_lo_ready")
        silu_done = sem("silu_done")
        g_z = sem("g_z")
        g_abs = sem("g_abs")
        g_e = sem("g_e")
        g_ln = sem("g_ln")
        g_log = sem("g_log")
        g_sum = sem("g_sum")
        g_exp = sem("g_exp")
        g_kd = sem("g_kd")
        g_kv = sem("g_kv")
        g_state = sem("g_state")
        g_o = sem("g_o")
        g_ocopy = sem("g_ocopy")
        g_osq = sem("g_osq")
        g_osum = sem("g_osum")
        g_lnv = sem("g_lnv")
        g_rms = sem("g_rms")
        g_norm = sem("g_norm")
        g_out = sem("g_out")
        c_pad = sem("c_pad")
        vs_loaded = [sem(f"vs_loaded{i}") for i in range(2)]
        c_s = sem("c_s")
        c_bias = sem("c_bias")
        c_mask = sem("c_mask")
        c_mx = sem("c_mx")
        c_nm = sem("c_nm")
        c_exp = sem("c_exp")
        c_den = sem("c_den")
        c_rd = sem("c_rd")
        c_p = sem("c_p")
        c_t = sem("c_t")
        c_tc = sem("c_tc")
        c_pv = sem("c_pv")
        o1_hi_ready = sem("o1_hi_ready")
        o1_lo_ready = sem("o1_lo_ready")
        u_scaled = sem("u_scaled")
        u_mid = sem("u_mid")
        conv1 = sem("conv1")
        conv2 = sem("conv2")
        gelu_done = sem("gelu_done")
        y_mul = sem("y_mul")
        yhi_ready = sem("yhi_ready")
        ylo_ready = sem("ylo_ready")
        halo = sem("halo")
        warmed = sem("warmed")
        out_ready = sem("out_ready")
        out_written = sem("out_written")

        def gain_at(n, c):
            return par[:, bass.ds(S_GAIN + n * KC + c, 1)]

        def blk(t, c):
            return t[:, bass.ds(c, 1), :].rearrange("p o t -> p (o t)")

        B_PARTS = {"vb": 4, "va": 4, "ka": 2, "v": 2}

        def a_before(units, u):
            return sum(n not in B_PARTS for n, _ in units[:u])

        def b_before(units, u):
            return TT * sum(n in B_PARTS and i == B_PARTS[n] - 1 for n, i in units[:u])

        A_MIX0, B_MIX0 = a_before(MIX0, N0), b_before(MIX0, N0)
        N_CONSTS = 16
        NADD = KC + 1

        o1_psum = ps[:, B_PV:B_PV + 2, :].rearrange("p b (c e q) -> p e (b c) q", e=2, q=CHUNK)

        def o1_tiles(t, g):
            return t[:, 2 * g:2 * g + 2, :].rearrange("p e (c q) -> p e c q", q=CHUNK)

        block = ctx.enter_context(nc.Block())

        @block.sync
        def _(sp):
            def unit(u, r, src, cols=UC):
                sp.wait_ge(w_lo_ready, u - (RAW - 1))
                sp.dma_start(w_raw[r][:, 0:cols], src).then_inc(w_loaded[r], 16)

            def one(t, i):
                return t[bass.ds(i, 1)].rearrange("o p c -> (o p) c")

            for u in range(RAW):
                sp.dma_start(w_raw[u][:, :], w_mix0[u]).then_inc(w_loaded[u], 16)
            with sp.Fori(1, U_UP0 // RAW) as i:
                for k in range(RAW):
                    unit(RAW * i + k, k, one(w_mix0, RAW * i + k))
            for u in range(U_UP0 // RAW * RAW, U_UP0):
                unit(u, u % RAW, w_mix0[u])

            def ffn(layer, u_up, u_dn):
                with sp.Fori(0, UP // RAW) as i:
                    for k in range(RAW):
                        unit(u_up + k + RAW * i, (u_up + k) % RAW, one(w_up, layer * UP + k + RAW * i))
                with sp.Fori(0, KC) as i:
                    for k in range(len(DN)):
                        src = w_down[bass.ds(layer * KC + i, 1), :, DOFF[k] * P:(DOFF[k] + DN[k]) * P]
                        unit(u_dn + k + RAW * i, (u_dn + k) % RAW,
                             src.rearrange("o p c -> (o p) c"), DN[k] * P)

            ffn(0, U_UP0, U_DN0)
            with sp.Fori(0, (N1 + KC) // RAW) as i:
                for k in range(RAW):
                    unit(U_MIX1 + k + RAW * i, (U_MIX1 + k) % RAW, one(w_mix1, k + RAW * i))
            ffn(1, U_UP1, U_DN1)
            for c in range(KC):
                sp.wait_ge(out_ready, c + 1)
                sp.dma_start(out[:, c * T:(c + 1) * T], x[:, c, :]).then_inc(out_written, 16)
            sp.wait_ge(out_written, 16 * KC)

        @block.gpsimd
        def _(pool):
            n = [0]

            def step(ins):
                ins.then_inc(consts, 1)
                n[0] += 1
                pool.wait_ge(consts, n[0])

            g = nc.gpsimd
            step(g.memset(mhalf[:, :], -0.5))
            step(g.memset(eps_col[:, :], EPS))
            step(g.memset(ones[:, :], 1.0))
            step(g.memset(ident[:, :], 0.0))
            step(g.affine_select(out=ident[:, :], in_=ident[:, :], compare_op=ALU.not_equal, fill=1.0,
                                 base=0, pattern=[[-1, P]], channel_multiplier=1))
            step(g.memset(gaT[:, :], 1.0))
            step(g.memset(negmask[:, :], NEG))
            step(g.affine_select(out=negmask[:, :], in_=negmask[:, :], compare_op=ALU.is_ge, fill=0.0,
                                 base=0, pattern=[[-1, P]], channel_multiplier=1))
            step(g.memset(tri_f[:, :], -1.0))
            step(g.affine_select(out=tri_f[:, :], in_=tri_f[:, :], compare_op=ALU.is_ge, fill=0.0,
                                 base=0, pattern=[[-1, P]], channel_multiplier=1))
            step(g.memset(tri16[:, :], 1.0 / TAU))
            step(g.affine_select(out=tri16[:, :], in_=tri16[:, :], compare_op=ALU.is_gt, fill=0.0,
                                 base=0, pattern=[[-1, P]], channel_multiplier=1))
            step(g.memset(tri16[CHUNK:P, 0:CHUNK], 0.0))
            step(g.memset(ind16[:, :], 0.0))
            step(g.memset(ind16[0:CHUNK, 0:1], 1.0 / TAU))
            step(g.memset(ind16[CHUNK:P, 1:2], 1.0 / TAU))
            assert n[0] == N_CONSTS

            for norm in range(2 * LAYERS + 1):
                pool.wait_ge(var_ready, norm + 1)
                g.tensor_tensor(rinv_col[:, :], var_col[:, :], mhalf[:, :], ALU.pow).then_inc(rcol_ready, 1)

        @block.scalar
        def _(act):
            s = nc.scalar

            def hi(u, gen, r, cols=UC):
                act.wait_ge(w_loaded[r], 16 * gen + 16)
                act.wait_ge(unit_done, u - (SPL - 1))
                s.activation(w_hi[r % SPL][:, 0:cols], w_raw[r][:, 0:cols], ACT.Copy).then_inc(w_hi_ready, 1)

            def hi_static(u, cols=UC):
                if u < U_END:
                    hi(u, u // RAW, u % RAW, cols)

            def norm_tile(norm, c, r, last=False):
                act.wait_ge(x_updated, r + 1)
                act.wait_ge(ssq_added, norm * NADD + 1 + c)
                s.activation(sq[:, :], blk(x, c), ACT.Square).then_inc(sq_ready, 1)
                if not last:
                    s.activation(blk(h_hi, c), blk(x, c), ACT.Copy, scale=gain_at(norm, c)).then_inc(hi_ready, 1)

            def rinv_copy(norm):
                act.wait_ge(rbc_done, norm + 1)
                s.activation(rinv[:, :], ps[:, B_RINV, :], ACT.Copy).then_inc(rinv_ready, 1)

            for i in range(4):
                act.dma_start(x[:, 2 * i:2 * i + 2, :],
                              xT[:, 2 * i * T:(2 * i + 2) * T].rearrange("p (c t) -> p c t", t=T)).then_inc(x_loaded[i], 16)
                if i == 0:
                    act.dma_start(par[:, :], small).then_inc(par_loaded, 16)
            act.dma_start(wg2_sb[:, :], wg2).then_inc(wg2_loaded, 16)

            act.wait_ge(par_loaded, 16)
            for c in range(KC):
                if c % 2 == 0:
                    act.wait_ge(x_loaded[c // 2], 16)
                act.wait_ge(ssq_added, 1 + c)
                s.activation(sq[:, :], x[:, c, :], ACT.Square).then_inc(sq_ready, 1)
                s.activation(h_hi[:, c, :], x[:, c, :], ACT.Copy, scale=gain_at(0, c)).then_inc(hi_ready, 1)
                if c < SPL:
                    act.wait_ge(w_loaded[c], 16)
                    s.activation(w_hi[c][:, :], w_raw[c][:, :], ACT.Copy).then_inc(w_hi_ready, 1)

            def b_evac(dst, bank0, n_cols):
                for tt in range(TT):
                    s.activation(dst[:, tt, :], ps[:, bank0 + tt, 0:n_cols], ACT.Copy,
                                 scale=rinv_col[:, tt:tt + 1]).then_inc(b_taken, 1)

            for name, i in SEQ0:
                if name == "unit":
                    hi_static(i + SPL)
                    n, part = MIX0[i]
                    if (n, part) == ("ra", 3):
                        act.wait_ge(a_taken, 4)
                        s.activation(raT[:, :, :], raT[:, :, :], ACT.Silu).then_inc(silu_done, 1)
                    if n in B_PARTS and part == B_PARTS[n] - 1:
                        b_evac({"vb": vb, "va": va, "ka": ka}[n], 0, {"vb": SH * SD, "va": GH * GV, "ka": GH * GK}[n])
                elif name == "rinv":
                    rinv_copy(0)
                elif name == "z":
                    act.wait_ge(sb_z, i + 1)
                    act.wait_ge(sb_sp, i)
                    s.activation(sbE[:, :], zs[:, 0:ZN], ACT.Abs).then_inc(sb_abs, 1)
                    act.wait_ge(sb_abs, i + 1)
                    s.activation(sbE[:, :], sbE[:, :], ACT.Exp, scale=-1.0).then_inc(sb_e, 1)
                    act.wait_ge(sb_e, i + 1)
                    s.activation(sbE[:, :], sbE[:, :], ACT.Ln, bias=1.0).then_inc(sb_ln, 1)
                elif name == "sfx":
                    act.wait_ge(sb_sum, i + 1)
                    s.activation(sbS[:, :], zs[:, 0:ZN], ACT.Exp).then_inc(sb_w, 1)
                elif name == "pv" and i % 2 == 1:
                    act.wait_ge(sb_pv, i + 1)
                    s.activation(oc_hi[:, GH + i // 2, :], ps[:, B_O, :], ACT.Copy).then_inc(oc_hi_ready, 1)
                elif name == "gz":
                    act.wait_ge(g_z, 1)
                    s.activation(gE[:, :], ps[:, 0:2, :].rearrange("p b t -> p (b t)"), ACT.Abs).then_inc(g_abs, 1)
                    act.wait_ge(g_abs, 1)
                    s.activation(gE[:, :], gE[:, :], ACT.Exp, scale=-1.0).then_inc(g_e, 1)
                    act.wait_ge(g_e, 1)
                    s.activation(gE[:, :], gE[:, :], ACT.Ln, bias=1.0).then_inc(g_ln, 1)
                elif name == "gs":
                    act.wait_ge(g_sum, 1)
                    s.activation(gE[:, :], ps[:, 2:4, :].rearrange("p b t -> p (b t)"), ACT.Exp).then_inc(g_exp, 1)
                    s.activation(dec[:, :, :].rearrange("p a c -> p (a c)"), ps[:, 0, 0:2 * NCH], ACT.Exp).then_inc(g_exp, 1)
                elif name == "go":
                    act.wait_ge(g_o, 1)
                    for h in range(GH):
                        s.activation(oF[:, h, :], ps[:, h, :], ACT.Copy).then_inc(g_ocopy, 1)
                elif name == "gn":
                    act.wait_ge(g_osum, 1)
                    act.wait_ge(consts, 2)
                    for p in range(2):
                        s.activation(gq[p], ps[:, 2 * p:2 * p + 2, :], ACT.Ln, scale=1.0 / GV,
                                     bias=eps_col[:, 0:1]).then_inc(g_lnv, 1)
                    for p in range(2):
                        act.wait_ge(g_lnv, p + 1)
                        s.activation(gq[p], gq[p], ACT.Exp, scale=-0.5).then_inc(g_rms, 1)
            for h in range(GH):
                act.wait_ge(g_out, h + 1)
                s.activation(oc_hi[:, h, :], oF[:, h, :], ACT.Copy).then_inc(oc_hi_ready, 1)

            def w_out(norm, u0, r0):
                for c in range(KC):
                    hi_static(u0 + c + SPL)
                    norm_tile(norm, c, r0 + c)

            def ffn(layer, norm, u_up, u_dn, r0, next_cols, last):
                act.wait_ge(warmed, layer)
                s.activation(gelu_warm[:, :], par[:, 0:1], ACT.Gelu_apprx_tanh).then_inc(warmed, 1)

                def up_hi(i, k, cols=UC):
                    hi(u_up + k + SPL + 4 * i, (u_up + k + SPL) // RAW + i, (u_up + k + SPL) % RAW, cols)

                def up_tile(i, k):
                    m = layer * UP + k + 4 * i
                    pair = layer * FC + k // 2 + 2 * i
                    taps = S_CONV + (layer * UP + k) * 4 + 16 * i
                    act.wait_ge(ylo_ready, pair)
                    act.wait_ge(u_scaled, m + 1)
                    s.activation(cv[k % 2][:, :], us[k % 2][:, 2:2 + T], ACT.Identity,
                                 bias=par[:, bass.ds(taps + 3, 1)],
                                 scale=par[:, bass.ds(taps + 2, 1)]).then_inc(u_mid, 1)
                    if k % 2 == 0:
                        act.wait_ge(conv2, m + 1)
                        s.activation(cv[0][:, :], cv[0][:, :], ACT.Gelu_apprx_tanh).then_inc(gelu_done, 1)
                    else:
                        act.wait_ge(y_mul, pair + 1)
                        s.activation(blk(y_hi, k // 2 + 2 * i), cv[1][:, :], ACT.Copy).then_inc(yhi_ready, 1)

                up_hi(0, 0)
                up_hi(0, 1)
                rinv_copy(norm)
                up_tile(0, 0)
                up_tile(0, 1)
                for k in (2, 3):
                    up_hi(0, k)
                    up_tile(0, k)
                with act.Fori(1, UP // 4 - 1) as i:
                    for k in range(4):
                        up_hi(i, k)
                        up_tile(i, k)
                for k in range(4):
                    up_hi(UP // 4 - 1, k, UC if k < 4 - SPL else DN[k - 4 + SPL] * P)
                    up_tile(UP // 4 - 1, k)

                def down_pair(i, ahead):
                    for j in range(2):
                        for kk in range(4 * j, 4 * j + 4):
                            if kk + SPL < 8 or ahead is not None:
                                cols = DN[(kk + SPL) % 4] * P if kk + SPL < 8 else ahead[kk + SPL - 8]
                                hi(u_dn + kk + SPL + 8 * i, (u_dn + kk + SPL) // RAW + 2 * i,
                                   (u_dn + kk + SPL) % RAW, cols)
                        norm_tile(norm + 1, j + 2 * i, r0 + j + 2 * i, last)

                with act.Fori(0, KC // 2 - 1) as i:
                    down_pair(i, [DN[k] * P for k in range(SPL)])
                down_pair(KC // 2 - 1, next_cols)

            w_out(1, U_OUT0, 0)
            ffn(0, 1, U_UP0, U_DN0, KC, [UC] * SPL, False)

            for name, i in SEQ1:
                if name == "unit":
                    hi_static(U_MIX1 + i + SPL)
                    if i == 0:
                        act.dma_start(bias_sb[:, :, :], bias.rearrange("p (n k) -> p n k", k=P)).then_inc(bias_loaded, 16)
                    if MIX1[i] == ("v", 1):
                        b_evac(v1, B_SC, CKV * CD)
                        act.wait_ge(b_taken, B_MIX0 + TT)
                        act.dma_start(v1s[0:CHUNK, 1:TT, :], v1[CHUNK:P, 0:TT - 1, :]).then_inc(vs_loaded[0], 16)
                        act.dma_start(v1s[CHUNK:P, :, :], v1[0:CHUNK, :, :]).then_inc(vs_loaded[1], 16)
                elif name == "rinv":
                    rinv_copy(2)
                elif name == "s":
                    act.wait_ge(c_nm, i + 1)
                    act.wait_ge(c_den, i)
                    act.wait_ge(c_t, i)
                    s.activation(es[:, :], nm[:, :], ACT.Exp, bias=par[:, S_SINK + i:S_SINK + i + 1])
                    for c in range(NCH):
                        ins = s.activation(pr[:, c, :], sc[:, c, :], ACT.Exp, bias=nm[:, c:c + 1],
                                           accum_out=rs[:, c:c + 1])
                    ins.then_inc(c_exp, 1)
                elif name == "t":
                    act.wait_ge(c_t, i + 1)
                    act.wait_ge(c_pv, i)
                    s.activation(prT[:, :, :].rearrange("p c k -> p (c k)"),
                                 ps[:, B_T:B_T + 2, :].rearrange("p b t -> p (b t)"), ACT.Copy).then_inc(c_tc, 1)
                elif name == "o" and i % 2 == 1:
                    act.wait_ge(c_pv, i + 1)
                    s.activation(o1_tiles(o1_hi, i // 2), o1_psum, ACT.Copy).then_inc(o1_hi_ready, 1)
            w_out(3, U_OUT1, 2 * KC)
            ffn(1, 3, U_UP1, U_DN1, 3 * KC, None, True)
            rinv_copy(2 * LAYERS)

        @block.vector
        def _(dve):
            v = nc.vector

            def lo(u, r, cols=UC):
                dve.wait_ge(w_hi_ready, u + 1)
                v.tensor_tensor(w_lo[r % SPL][:, 0:cols], w_raw[r][:, 0:cols],
                                w_hi[r % SPL][:, 0:cols].bitcast(F32), ALU.subtract).then_inc(w_lo_ready, 1)

            def lo_static(u, cols=UC):
                lo(u, u % RAW, cols)

            def add_sq(norm, c):
                dve.wait_ge(sq_ready, norm * KC + 1 + c)
                dve.wait_ge(ssq_added, norm * NADD + 1 + c)
                v.tensor_tensor(ssq[:, :], ssq[:, :], sq[:, :], ALU.add).then_inc(ssq_added, 1)

            def h_lo_part(norm, c):
                dve.wait_ge(hi_ready, norm * KC + 1 + c)
                v.scalar_tensor_tensor(blk(h_lo, c), blk(x, c), gain_at(norm, c),
                                       blk(h_hi, c).bitcast(F32), ALU.mult, ALU.subtract).then_inc(lo_ready, 1)

            def res_tile(norm, c, bank, r, units, last=False):
                dve.wait_ge(unit_done, units)
                v.tensor_tensor(blk(x, c), ps[:, bank, :], blk(x, c), ALU.add).then_inc(x_updated, 1)
                if not last:
                    dve.wait_ge(x_updated, r + 1)
                    h_lo_part(norm, c)
                add_sq(norm, c)

            def rms(norm):
                dve.wait_ge(ssq_col, norm + 1)
                v.tensor_scalar(var_col[:, :], ps[:, B_SSQ, 0:TT], 1.0 / D, EPS, ALU.mult, ALU.add).then_inc(var_ready, 1)
                if norm < 2 * LAYERS:
                    v.memset(ssq[:, :], 0.0).then_inc(ssq_added, 1)
                dve.wait_ge(rcol_ready, norm + 1)
                v.tensor_tensor(diag[:, :].rearrange("p (a t) -> p a t", a=TT),
                                ident[:, :].unsqueeze(1).broadcast_to([P, TT, P]),
                                rinv_col[:, :].unsqueeze(2).broadcast_to([P, TT, P]), ALU.mult).then_inc(diag_ready, 1)

            v.memset(ssq[:, :], 0.0).then_inc(ssq_added, 1)
            dve.wait_ge(par_loaded, 16)
            for c in range(KC):
                h_lo_part(0, c)
                add_sq(0, c)
                if c < SPL:
                    lo_static(c)
            dve.wait_ge(consts, N_CONSTS)
            v.tensor_copy(ident_bf[:, :], ident[:, :]).then_inc(consts_dve, 1)
            v.tensor_copy(negtri[:, :], tri_f[:, :]).then_inc(consts_dve, 1)
            v.tensor_scalar(negones[:, :], ones[:, :], -1.0, None, ALU.mult).then_inc(consts_dve, 1)

            def a_evac0(u):
                (n, i), a = MIX0[u], a_before(MIX0, u)
                dve.wait_ge(unit_done, u + 1)
                src = ps[:, a % 4, :]
                if n in ("ra", "kb"):
                    dst = (raT if n == "ra" else kbT)[:, i, :]
                    ins = v.tensor_tensor(dst, src, rinv[:, :], ALU.mult)
                elif n in ("qb", "qa"):
                    dst, width = (qbT, SD) if n == "qb" else (qaT, GK)
                    ins = v.scalar_tensor_tensor(dst[:, i, :], src, width ** -0.5, rinv[:, :], ALU.mult, ALU.mult)
                else:
                    ins = v.tensor_tensor(gaT[0:RANK, :], ps[0:RANK, a % 4, :], rinv[0:RANK, :], ALU.mult)
                ins.then_inc(a_taken, 1)

            for name, i in SEQ0:
                if name == "unit":
                    if i >= 2 and MIX0[i][0] not in B_PARTS:
                        a_evac0(i)
                    lo_static(i + SPL)
                elif name == "ssq":
                    rms(0)
                elif name == "rinv":
                    dve.wait_ge(rinv_ready, 1)
                    a_evac0(0)
                    a_evac0(1)
                elif name == "z":
                    dve.wait_ge(sb_ln, i + 1)
                    dve.wait_ge(sb_pv, i)
                    v.scalar_tensor_tensor(sbS[:, :], zs[:, 0:ZN], 0.0, sbE[:, :], ALU.max, ALU.add).then_inc(sb_sp, 1)
                    dve.wait_ge(sb_sp, i + 1)
                    v.tensor_copy(sbH[:, :], sbS[:, :]).then_inc(sb_hi, 1)
                    dve.wait_ge(sb_hi, i + 1)
                    v.tensor_tensor(sbL[:, :], sbS[:, :], sbH[:, :].bitcast(F32), ALU.subtract).then_inc(sb_lo, 1)
                elif name == "pv" and i % 2 == 1:
                    dve.wait_ge(oc_hi_ready, i // 2 + 1)
                    v.tensor_tensor(oc_lo[:, GH + i // 2, :], ps[:, B_O, :],
                                    oc_hi[:, GH + i // 2, :].bitcast(F32), ALU.subtract).then_inc(oc_lo_ready, 1)
                elif name == "gz":
                    gz = ps[:, 0:2, :].rearrange("p b t -> p (b t)")
                    dve.wait_ge(g_ln, 1)
                    v.scalar_tensor_tensor(gL[:, :], gz, 0.0, gE[:, :], ALU.min, ALU.subtract).then_inc(g_log, 1)
                elif name == "gs":
                    dve.wait_ge(g_exp, 2)
                    v.tensor_tensor(gL[:, :], gE[:, :], ka[:, :, :].rearrange("p a n -> p (a n)"),
                                    ALU.mult).then_inc(g_kd, 1)
                elif name == "gkv":
                    dve.wait_ge(g_kv, 1)
                    for c in range(NCH):
                        for p in range(GH // 2):
                            kv = ps[:, 2 * p + c % 2, (c // 2) * GV:(c // 2 + 1) * GV]
                            if c == 0:
                                v.tensor_copy(st[p][:, 0, :], kv).then_inc(g_state, 1)
                            else:
                                dve.wait_ge(g_state, 2 * c - 1 + p)
                                v.scalar_tensor_tensor(st[p][:, c, :], st[p][:, c - 1, :], dec[:, p, c:c + 1], kv,
                                                       ALU.mult, ALU.add).then_inc(g_state, 1)
                elif name == "go":
                    for h in range(GH):
                        dve.wait_ge(g_ocopy, h + 1)
                        v.tensor_tensor(gq[h // 2][:, h % 2, :], oF[:, h, :], oF[:, h, :], ALU.mult).then_inc(g_osq, 1)
            for p in range(2):
                dve.wait_ge(g_rms, p + 1)
                v.tensor_tensor(oF[:, 2 * p:2 * p + 2, :], oF[:, 2 * p:2 * p + 2, :], gq[p], ALU.mult).then_inc(g_norm, 1)
                dve.wait_ge(g_norm, p + 1)
                dve.wait_ge(silu_done, 1)
                for h in (2 * p, 2 * p + 1):
                    v.scalar_tensor_tensor(oF[:, h, :], oF[:, h, :], par[:, S_GLA + h:S_GLA + h + 1],
                                           raT[:, h, :], ALU.mult, ALU.mult).then_inc(g_out, 1)
            for h in range(GH):
                dve.wait_ge(oc_hi_ready, SH // 2 + h + 1)
                v.tensor_tensor(oc_lo[:, h, :], oF[:, h, :], oc_hi[:, h, :].bitcast(F32), ALU.subtract).then_inc(oc_lo_ready, 1)

            def w_out(norm, u0, r0):
                for c in range(KC):
                    res_tile(norm, c, B_RES + c % 2, r0 + c, u0 + c + 1)
                    lo_static(u0 + c + SPL)

            def ffn(layer, norm, u_up, u_dn, r0, next_cols, last):
                def up_lo(i, k, cols=UC):
                    lo(u_up + k + SPL + 4 * i, (u_up + k + SPL) % RAW, cols)

                def up_scale(i, k):
                    dve.wait_ge(unit_done, u_up + k + 1 + 4 * i)
                    v.tensor_tensor(us[k % 2][:, 2:2 + T], ps[:, k, :], rinv[:, :], ALU.mult).then_inc(u_scaled, 1)

                def up_conv(i, k):
                    m = layer * UP + k + 4 * i
                    pair = layer * FC + k // 2 + 2 * i
                    taps = S_CONV + (layer * UP + k) * 4 + 16 * i
                    dve.wait_ge(u_mid, m + 1)
                    v.scalar_tensor_tensor(cv[k % 2][:, :], us[k % 2][:, 1:1 + T], par[:, bass.ds(taps + 1, 1)],
                                           cv[k % 2][:, :], ALU.mult, ALU.add).then_inc(conv1, 1)
                    dve.wait_ge(conv1, m + 1)
                    v.scalar_tensor_tensor(cv[k % 2][:, :], us[k % 2][:, 0:T], par[:, bass.ds(taps, 1)],
                                           cv[k % 2][:, :], ALU.mult, ALU.add).then_inc(conv2, 1)
                    if k % 2 == 1:
                        dve.wait_ge(conv2, m + 1)
                        dve.wait_ge(gelu_done, pair + 1)
                        v.tensor_tensor(cv[1][:, :], cv[1][:, :], cv[0][:, :], ALU.mult).then_inc(y_mul, 1)
                        dve.wait_ge(yhi_ready, pair + 1)
                        p = k // 2 + 2 * i
                        v.tensor_tensor(blk(y_lo, p), cv[1][:, :], blk(y_hi, p).bitcast(F32),
                                        ALU.subtract).then_inc(ylo_ready, 1)

                up_lo(0, 0)
                for k in range(2):
                    v.memset(us[k][:, 0:2], 0.0).then_inc(halo, 1)
                rms(norm)
                up_lo(0, 1)
                dve.wait_ge(halo, 2 * (layer + 1))
                dve.wait_ge(rinv_ready, norm + 1)
                for k in range(2):
                    up_scale(0, k)
                    up_conv(0, k)
                for k in (2, 3):
                    up_scale(0, k)
                    up_lo(0, k)
                    up_conv(0, k)
                with dve.Fori(1, UP // 4 - 1) as i:
                    for k in range(4):
                        up_scale(i, k)
                        up_lo(i, k)
                        up_conv(i, k)
                for k in range(4):
                    up_scale(UP // 4 - 1, k)
                    up_lo(UP // 4 - 1, k, UC if k < 4 - SPL else DN[k - 4 + SPL] * P)
                    up_conv(UP // 4 - 1, k)

                def down_pair(i, ahead):
                    for j in range(2):
                        for kk in range(4 * j, 4 * j + 4):
                            if kk + SPL < 8 or ahead is not None:
                                cols = DN[(kk + SPL) % 4] * P if kk + SPL < 8 else ahead[kk + SPL - 8]
                                lo(u_dn + kk + SPL + 8 * i, (u_dn + kk + SPL) % RAW, cols)
                        res_tile(norm + 1, j + 2 * i, B_RES + j, r0 + j + 2 * i, u_dn + 4 * j + 4 + 8 * i, last)

                with dve.Fori(0, KC // 2 - 1) as i:
                    down_pair(i, [DN[k] * P for k in range(SPL)])
                down_pair(KC // 2 - 1, next_cols)

            w_out(1, U_OUT0, 0)
            ffn(0, 1, U_UP0, U_DN0, KC, [UC] * SPL, False)

            def a_evac1(i):
                n, part = MIX1[i]
                dve.wait_ge(unit_done, U_MIX1 + i + 1)
                src, scale = ps[:, a_before(MIX1, i) % 2, :], rinv[:, :]
                if n == "k":
                    dst = k1[:, part, CHUNK:CHUNK + T]
                else:
                    dst = q1[:, part // 2, :, part % 2, :]
                    src, scale = (t.rearrange("p (c q) -> p c q", q=CHUNK) for t in (src, scale))
                v.tensor_tensor(dst, src, scale, ALU.mult).then_inc(a_taken, 1)

            for name, i in SEQ1:
                if name == "unit":
                    if i >= 2 and MIX1[i][0] not in B_PARTS:
                        a_evac1(i)
                    lo_static(U_MIX1 + i + SPL)
                elif name == "ssq":
                    rms(2)
                    v.memset(k1[:, :, 0:CHUNK], 0.0).then_inc(c_pad, 1)
                    v.memset(v1s[0:CHUNK, 0, :], 0.0).then_inc(c_pad, 1)
                elif name == "rinv":
                    dve.wait_ge(rinv_ready, 3)
                    a_evac1(0)
                    a_evac1(1)
                elif name == "s":
                    dve.wait_ge(c_s, i + 1)
                    if i == 0:
                        dve.wait_ge(bias_loaded, 16)
                    dve.wait_ge(c_exp, i)
                    v.scalar_tensor_tensor(sc[:, :, :], ps[:, B_SC:B_SC + 2, :].rearrange("p b (c k) -> p (b c) k", k=P),
                                           CD ** -0.5, bias_sb[:, i, :].unsqueeze(1).broadcast_to([P, NCH, P]),
                                           ALU.mult, ALU.add).then_inc(c_bias, 1)
                    dve.wait_ge(c_bias, i + 1)
                    v.memset(sc[:, 0, 0:CHUNK], NEG).then_inc(c_mask, 1)
                    dve.wait_ge(c_mask, i + 1)
                    v.tensor_reduce(mx[:, :], sc[:, :, :], AX.X, ALU.max).then_inc(c_mx, 1)
                    dve.wait_ge(c_mx, i + 1)
                    v.tensor_scalar(nm[:, :], mx[:, :], par[:, S_SINK + i:S_SINK + i + 1], -1.0,
                                    ALU.max, ALU.mult).then_inc(c_nm, 1)
                    dve.wait_ge(c_exp, i + 1)
                    v.tensor_tensor(den[:, :], rs[:, :], es[:, :], ALU.add).then_inc(c_den, 1)
                    dve.wait_ge(c_den, i + 1)
                    v.reciprocal(rd[:, :], den[:, :]).then_inc(c_rd, 1)
                    dve.wait_ge(c_rd, i + 1)
                    v.tensor_tensor(pr[:, :, :], pr[:, :, :], rd[:, :].unsqueeze(2).broadcast_to([P, NCH, P]),
                                    ALU.mult).then_inc(c_p, 1)
                elif name == "o" and i % 2 == 1:
                    dve.wait_ge(o1_hi_ready, i // 2 + 1)
                    v.tensor_tensor(o1_tiles(o1_lo, i // 2), o1_psum, o1_tiles(o1_hi, i // 2).bitcast(F32),
                                    ALU.subtract).then_inc(o1_lo_ready, 1)
            w_out(3, U_OUT1, 2 * KC)
            ffn(1, 3, U_UP1, U_DN1, 3 * KC, None, True)

            rms(2 * LAYERS)
            dve.wait_ge(rinv_ready, 2 * LAYERS + 1)
            for c in range(KC):
                v.scalar_tensor_tensor(x[:, c, :], x[:, c, :], gain_at(2 * LAYERS, c), rinv[:, :],
                                       ALU.mult, ALU.mult).then_inc(out_ready, 1)

        @block.tensor
        def _(pe):
            mm = nc.tensor.matmul

            def three(dst, w, m, first, last):
                mm(dst, w[0], m[0], start=first, stop=False)
                mm(dst, w[0], m[1], start=False, stop=False)
                return mm(dst, w[1], m[0], start=False, stop=last)

            def w_blocks(r, c, n=P):
                return tuple(t[r % SPL][:, c * n:(c + 1) * n] for t in (w_hi, w_lo))

            def a_unit(u, r, bank, h_blocks=None):
                pe.wait_ge(w_lo_ready, u + 1)
                for c in range(KC):
                    if h_blocks is not None:
                        pe.wait_ge(lo_ready, h_blocks + c + 1)
                    ins = three(ps[:, bank, :], w_blocks(r, c), (h_hi[:, c, :], h_lo[:, c, :]),
                                c == 0, c == KC - 1)
                ins.then_inc(unit_done, 1)

            def b_unit(u, part, parts, bank0, n_cols):
                pe.wait_ge(w_lo_ready, u + 1)
                for k in range(KC // parts):
                    c = part * (KC // parts) + k
                    for tt in range(TT):
                        tok = slice(tt * P, (tt + 1) * P)
                        ins = three(ps[:, bank0 + tt, 0:n_cols], (h_hi[:, c, tok], h_lo[:, c, tok]),
                                    w_blocks(u % RAW, k, n_cols), c == 0, c == KC - 1)
                ins.then_inc(unit_done, 1)

            def ssq_mm(norm):
                if norm == 0:
                    pe.wait_ge(consts, N_CONSTS)
                pe.wait_ge(ssq_added, NADD * (norm + 1))
                for tt in range(TT):
                    ins = mm(ps[:, B_SSQ, tt:tt + 1], ssq[:, tt * P:(tt + 1) * P], ones[:, 0:1],
                             start=True, stop=True)
                ins.then_inc(ssq_col, 1)

            def rinv_mm(norm):
                pe.wait_ge(diag_ready, norm + 1)
                mm(ps[:, B_RINV, :], ones[:, :], diag[:, :], start=True, stop=True).then_inc(rbc_done, 1)

            def out_tiles(u0, r0, o_hi, o_lo):
                for c in range(KC):
                    pe.wait_ge(w_lo_ready, u0 + c + 1)
                    if c >= 2:
                        pe.wait_ge(x_updated, r0 + c - 1)
                    for k in range(KC):
                        ins = three(ps[:, B_RES + c % 2, :], w_blocks((u0 + c) % RAW, k),
                                    (o_hi[:, k, :], o_lo[:, k, :]), k == 0, k == KC - 1)
                    ins.then_inc(unit_done, 1)

            def ffn(layer, norm, u_up, u_dn, r0):
                def up(i, k):
                    pe.wait_ge(u_scaled, layer * UP + k - 3 + 4 * i)
                    a_unit(u_up + k + 4 * i, u_up + k, k)

                a_unit(u_up, u_up, 0, norm * KC)
                ssq_mm(norm)
                a_unit(u_up + 1, u_up + 1, 1)
                rinv_mm(norm)
                a_unit(u_up + 2, u_up + 2, 2)
                a_unit(u_up + 3, u_up + 3, 3)
                with pe.Fori(1, UP // 4) as i:
                    for k in range(4):
                        up(i, k)

                def down_pair(i, first):
                    for j in range(2):
                        if not (first and r0 == 0):
                            pe.wait_ge(x_updated, r0 + j - 1 + 2 * i)
                        for k in range(4):
                            kk = u_dn + 4 * j + k
                            pe.wait_ge(w_lo_ready, kk + 1 + 8 * i)
                            if first and j == 0:
                                pe.wait_ge(ylo_ready, layer * FC + DOFF[k] + DN[k])
                            for b in range(DN[k]):
                                c = DOFF[k] + b
                                ins = three(ps[:, B_RES + j, :], w_blocks(kk, b),
                                            (y_hi[:, c, :], y_lo[:, c, :]), c == 0, c == FC - 1)
                            ins.then_inc(unit_done, 1)

                down_pair(0, True)
                with pe.Fori(1, KC // 2) as i:
                    down_pair(i, False)

            for name, i in SEQ0:
                if name == "unit":
                    n, part = MIX0[i]
                    a = a_before(MIX0, i)
                    if n in B_PARTS:
                        if part == 0:
                            pe.wait_ge(a_taken, a)
                            pe.wait_ge(b_taken, b_before(MIX0, i))
                        b_unit(i, part, B_PARTS[n], 0, {"vb": SH * SD, "va": GH * GV, "ka": GH * GK}[n])
                    else:
                        if a >= 4:
                            pe.wait_ge(a_taken, a - 3)
                        pe.wait_ge(b_taken, b_before(MIX0, i))
                        a_unit(i, i, a % 4, 0 if i == 0 else None)
                elif name == "ssq":
                    ssq_mm(0)
                elif name == "rinv":
                    rinv_mm(0)
                elif name == "z":
                    j, rows = i // 2, slice(SD * (i % 2), SD * (i % 2) + SD)
                    kb_units = [u for u, n in enumerate(MIX0) if n == ("kb", j)]
                    pe.wait_ge(a_taken, a_before(MIX0, kb_units[0]) + 1)
                    pe.wait_ge(consts_dve, 3)
                    pe.wait_ge(sb_w, i)
                    for b in (0, 1, 3, 2):
                        mm(zs[:, ZOFF[b]:ZOFF[b] + ZW[b]], kbT[rows, j, b * P:(b + 1) * P],
                           qbT[rows, j, b * P:T], start=b != 3, stop=False, skip_group_check=True)
                    for b in range(TT):
                        ins = mm(zs[:, ZOFF[b]:ZOFF[b] + P], ident_bf[:, :], negmask[:, :],
                                 start=False, stop=False, skip_group_check=True)
                    ins.then_inc(sb_z, 1)
                elif name == "sfx":
                    pe.wait_ge(sb_lo, i + 1)
                    for b in range(TT):
                        for c in range(b, TT):
                            lhs = negtri if c == b else negones
                            dst = zs[:, ZOFF[b] + (c - b) * P:ZOFF[b] + ZW[b]]
                            for part in (sbH, sbL):
                                ins = mm(dst, lhs[:, :], part[:, ZOFF[c]:ZOFF[c] + ZW[c]],
                                         start=False, stop=c == TT - 1 and part is sbL, skip_group_check=True)
                    ins.then_inc(sb_sum, 1)
                elif name == "pv":
                    j, rows = i // 2, slice(SD * (i % 2), SD * (i % 2) + SD)
                    pe.wait_ge(sb_w, i + 1)
                    pe.wait_ge(oc_lo_ready, j)
                    for b in range(TT):
                        ins = mm(ps[rows, B_O, b * P:T], vb[:, b, i * SD:(i + 1) * SD],
                                 sbS[:, ZOFF[b]:ZOFF[b] + ZW[b]], start=b == 0, stop=b == TT - 1)
                    ins.then_inc(sb_pv, 1)
                elif name == "gz":
                    pe.wait_ge(wg2_loaded, 16)
                    pe.wait_ge(a_taken, A_MIX0)
                    pe.wait_ge(b_taken, B_MIX0)
                    for tt in range(TT):
                        ins = mm(ps[:, tt // 2, (tt % 2) * 256:(tt % 2) * 256 + GH * GK],
                                 gaT[:, tt * P:(tt + 1) * P], wg2_sb[:, :], start=True, stop=True)
                    ins.then_inc(g_z, 1)
                elif name == "gs":
                    pe.wait_ge(g_log, 1)
                    for tt in range(TT):
                        mm(ps[:, 2 + tt // 2, (tt % 2) * 256:(tt % 2) * 256 + GH * GK], tri16[:, :],
                           gL[:, tt * GH * GK:(tt + 1) * GH * GK], start=True, stop=True)
                        for p in range(GH // 2):
                            col = p * NCH + 2 * tt
                            ins = mm(ps[:, 0, col:col + 2], gL[:, tt * GH * GK + p * P:tt * GH * GK + (p + 1) * P],
                                     ind16[:, :], start=True, stop=True)
                    ins.then_inc(g_sum, 1)
                elif name == "gkv":
                    pe.wait_ge(g_kd, 1)
                    for h in range(GH):
                        for c in range(NCH):
                            tok = slice(CHUNK * (c % 2), CHUNK * (c % 2) + CHUNK)
                            col = (c // 2) * GH * GK + h * GK
                            ins = mm(ps[GK * (h % 2):GK * (h % 2) + GK, 2 * (h // 2) + c % 2,
                                        (c // 2) * GV:(c // 2 + 1) * GV],
                                     gL[tok, col:col + GK], va[tok, c // 2, h * GV:(h + 1) * GV], start=True, stop=True)
                    ins.then_inc(g_kv, 1)
                elif name == "go":
                    pe.wait_ge(g_state, 2 * NCH)
                    for h in range(GH):
                        rows = slice(GK * (h % 2), GK * (h % 2) + GK)
                        for c in range(NCH):
                            ins = mm(ps[:, h, c * CHUNK:(c + 1) * CHUNK], st[h // 2][rows, c, :],
                                     qaT[rows, h // 2, c * CHUNK:(c + 1) * CHUNK], start=True, stop=True)
                    ins.then_inc(g_o, 1)
                elif name == "gn":
                    pe.wait_ge(g_osq, GH)
                    for h in range(GH):
                        ins = mm(ps[:, h, :], ones[:, :], gq[h // 2][:, h % 2, :], start=True, stop=True)
                    ins.then_inc(g_osum, 1)
            pe.wait_ge(oc_lo_ready, KC)
            out_tiles(U_OUT0, 0, oc_hi, oc_lo)
            ffn(0, 1, U_UP0, U_DN0, KC)

            for name, i in SEQ1:
                if name == "unit":
                    n, part = MIX1[i]
                    a = a_before(MIX1, i)
                    if n == "v":
                        b_unit(U_MIX1 + i, part, B_PARTS[n], B_SC, CKV * CD)
                    else:
                        if a >= 2:
                            pe.wait_ge(a_taken, A_MIX0 + a - 1)
                        a_unit(U_MIX1 + i, U_MIX1 + i, a % 2, 2 * KC if i == 0 else None)
                elif name == "ssq":
                    ssq_mm(2)
                elif name == "rinv":
                    rinv_mm(2)
                elif name == "s":
                    g, hh = i // 2, i % 2
                    rows = slice(CD * hh, CD * hh + CD)
                    pe.wait_ge(a_taken, A_MIX0 + 2 + 2 * g + 2)
                    pe.wait_ge(c_pad, 2)
                    pe.wait_ge(b_taken, B_MIX0 + TT)
                    pe.wait_ge(c_bias, i)
                    for c in range(NCH):
                        ins = mm(ps[:, B_SC + c // 4, (c % 4) * P:(c % 4 + 1) * P],
                                 q1[rows, g, c, :, :].rearrange("k e q -> k (e q)"),
                                 k1[rows, g // 2, c * CHUNK:c * CHUNK + P], start=True, stop=True)
                    ins.then_inc(c_s, 1)
                elif name == "t":
                    pe.wait_ge(c_p, i + 1)
                    pe.wait_ge(c_tc, i)
                    for c in range(NCH):
                        ins = nc.tensor.transpose(ps[:, B_T + c // 4, (c % 4) * P:(c % 4 + 1) * P],
                                                  pr[:, c, :], ident[:, :])
                    ins.then_inc(c_t, 1)
                elif name == "o":
                    g, hh = i // 2, i % 2
                    kv = 2 * (g // 2) + hh
                    pe.wait_ge(c_tc, i + 1)
                    pe.wait_ge(o1_lo_ready, g)
                    for sem_v in vs_loaded:
                        pe.wait_ge(sem_v, 16)
                    for c in range(NCH):
                        vals = v1 if c % 2 else v1s
                        ins = mm(ps[CD * hh:CD * hh + CD, B_PV + c // 4, (c % 4) * P:(c % 4 + 1) * P],
                                 vals[:, c // 2, kv * CD:(kv + 1) * CD], prT[:, c, :], start=True, stop=True)
                    ins.then_inc(c_pv, 1)
            pe.wait_ge(o1_lo_ready, CH // 4)
            out_tiles(U_OUT1, 2 * KC, o1_hi, o1_lo)
            ffn(1, 3, U_UP1, U_DN1, 3 * KC)
            ssq_mm(2 * LAYERS)
            rinv_mm(2 * LAYERS)


def t5_bucket(rel):
    buckets, far = 32, 128
    nb = buckets // 2
    exact = nb // 2
    n = np.abs(rel)
    large = exact + (np.log(np.maximum(n, 1) / exact) / np.log(far / exact) * (nb - exact)).astype(np.int32)
    return (np.where(rel > 0, nb, 0) + np.where(n < exact, n, np.minimum(large, nb - 1))).astype(np.int32)


def stationary(w):
    k, n = w.shape
    return w.reshape(k // P, P, n // P, P).transpose(2, 1, 0, 3).reshape(n // P, P, k)


def moving(w):
    k, n = w.shape
    per = UC // n
    return w.reshape(k // (P * per), per, P, n).transpose(0, 2, 1, 3).reshape(-1, P, UC)


def columns(a):
    a = np.asarray(a)
    return np.moveaxis(a.reshape(*a.shape[:-1], a.shape[-1] // P, P), -1, 0).reshape(P, -1)


def kernel(x, norm_mix, norm_ffn, norm_final, ab_w_in, ab_w_gate2, ab_b_gate, ab_gla_norm, ab_w_out,
           c_w_qkv, c_sinks, c_w_out, rel_bias, ffn_w_up, ffn_conv_w, ffn_conv_b, ffn_w_down):
    import concourse.bacc as bacc
    from concourse.bass_utils import run_bass_kernel_spmd

    f = [np.asarray(a) for a in (x, norm_mix, norm_ffn, norm_final, ab_w_in, ab_w_gate2, ab_b_gate, ab_gla_norm,
                                 ab_w_out, c_w_qkv, c_sinks, c_w_out, rel_bias, ffn_w_up, ffn_conv_w, ffn_conv_b,
                                 ffn_w_down)]
    (x, norm_mix, norm_ffn, norm_final, w_in, w_gate2, b_gate, gla_norm, w_out0, w_qkv, sinks, w_out1,
     rel_bias, w_up, conv_w, conv_b, w_down) = f

    sizes = [GH * GK, GH * GK, GH * GV, GH * GV, RANK, SH * SD, SH * SD, SH * SD]
    qa, ka, va, ra, ga, qb, kb, vb = np.split(w_in[0], np.cumsum(sizes)[:-1], axis=1)
    ga = np.concatenate([ga, np.zeros((D, P - RANK), ga.dtype)], axis=1)
    parts = {"qa": stationary(qa), "ra": stationary(ra), "ga": stationary(ga), "qb": stationary(qb),
             "kb": stationary(kb), "ka": moving(ka), "va": moving(va), "vb": moving(vb)}
    w_mix0 = np.concatenate([np.stack([parts[n][i] for n, i in MIX0]), stationary(w_out0[0])])

    q_heads = [h for a in range(4) for h in (a, 4 + a)] + [h for a in range(4) for h in (8 + a, 12 + a)]
    wq, wk, wv = np.split(w_qkv[0], [CH * CD, CH * CD + CKV * CD], axis=1)
    wq = wq.reshape(D, CH, CD)[:, q_heads].reshape(D, CH * CD)
    parts = {"q": stationary(wq), "k": stationary(wk), "v": moving(wv)}
    wo = w_out1[0].reshape(CH, CD, D)[q_heads].reshape(CH * CD, D)
    w_mix1 = np.concatenate([np.stack([parts[n][i] for n, i in MIX1]), stationary(wo)])

    turns = [t for i in range(FC) for t in (i, FC + i)]
    up = np.concatenate([stationary(w_up[layer])[turns] for layer in range(LAYERS)])
    down = np.concatenate([stationary(w_down[layer]) for layer in range(LAYERS)])
    conv = np.concatenate([conv_w, conv_b[:, None]], axis=1)
    conv = conv.reshape(LAYERS, 4, UP, P)[:, :, turns].transpose(3, 0, 2, 1).reshape(P, -1)

    pairs = [8 * (n // 4) + 4 * (n % 2) + 2 * ((n // 2) % 2) for n in range(CH // 2)]
    sink_cols = np.stack([np.repeat(sinks[0, [h, h + 1]], CHUNK) for h in pairs], axis=1)
    rel = np.arange(2 * CHUNK)[None, :] - (CHUNK + np.arange(CHUNK)[:, None])
    by_head = rel_bias[t5_bucket(rel)]
    bias = np.stack([np.concatenate([by_head[:, :, h], by_head[:, :, h + 1]]) for h in pairs], axis=1).reshape(P, -1)

    gains = np.concatenate([columns(norm_mix[0]), columns(norm_ffn[0]), columns(norm_mix[1]),
                            columns(norm_ffn[1]), columns(norm_final)], axis=1)
    small = np.concatenate([gains, columns(gla_norm[0]), conv, sink_cols], axis=1)
    arrays = {
        "xT": columns_of_tokens(x[0]),
        "w_mix0": w_mix0, "w_mix1": w_mix1, "w_up": up, "w_down": down, "small": small,
        "wg2": np.concatenate([w_gate2[0], b_gate]), "bias": bias,
    }
    arrays = {n: np.ascontiguousarray(a) for n, a in arrays.items()}

    nc = bacc.Bacc("TRN2", target_bir_lowering=False, num_devices=1)
    aps = {n: nc.dram_tensor(n, a.shape, F32, kind="ExternalInput").ap() for n, a in arrays.items()}
    out = nc.dram_tensor("out", (P, KC * T), F32, kind="ExternalOutput").ap()
    trunk(nc, *aps.values(), out)
    got = run_bass_kernel_spmd(nc, [arrays], core_ids=[0]).results[0]["out"]
    return np.ascontiguousarray(got.reshape(P, KC, T).transpose(2, 1, 0).reshape(1, T, D))


def columns_of_tokens(a):
    return a.T.reshape(KC, P, T).transpose(1, 0, 2).reshape(P, KC * T)
```

```python
from contextlib import ExitStack

import numpy as np

import concourse.bass as bass
from concourse import mybir

F32 = mybir.dt.float32
F32R = mybir.dt.float32r
BF16 = mybir.dt.bfloat16
ACT = mybir.ActivationFunctionType
ALU = mybir.AluOpType
AX = mybir.AxisListType

P = 128
T = 512
D = 1024
KC = D // P
TT = T // P
LAYERS = 2
CHUNK = 64
NCH = T // CHUNK
GH, GK, GV = 4, 64, 128
RANK = 16
TAU = 16.0
SH, SD = 8, 64
CH, CKV, CD = 16, 4, 64
DFF = 2816
FC = DFF // P
EPS = 1e-6
NEG = -1e30
RAW = 4
SPL = 2
UC = KC * P

MIX0 = ([("qb", 0), ("kb", 0)] + [("vb", i) for i in range(4)]
        + [("qb", 1), ("kb", 1), ("ga", 0), ("ka", 0), ("ka", 1), ("qb", 2), ("kb", 2), ("qb", 3)]
        + [("va", i) for i in range(4)] + [("kb", 3), ("qa", 0), ("qa", 1)] + [("ra", i) for i in range(4)])
N0 = len(MIX0)
MIX1 = [("k", 0), ("k", 1), ("v", 0), ("v", 1)] + [("q", i) for i in range(8)]
N1 = len(MIX1)
UP = 2 * FC
DN = (6, 6, 5, 5)
DOFF = (0, 6, 12, 17)
U_OUT0 = N0
U_UP0 = U_OUT0 + KC
U_DN0 = U_UP0 + UP
U_MIX1 = U_DN0 + 4 * KC
U_OUT1 = U_MIX1 + N1
U_UP1 = U_OUT1 + KC
U_DN1 = U_UP1 + UP
U_END = U_DN1 + 4 * KC

def parts_of(units):
    return [("unit", u, (q, q + 1)) for u in units for q in range(8)]


def joined(seq):
    out = []
    for step in seq:
        if out and step[0] == "unit" == out[-1][0] and step[1] == out[-1][1]:
            out[-1] = ("unit", step[1], (out[-1][2][0], step[2][1]))
        else:
            out.append(step)
    return out


def mix0_order():
    def unit(name, i=0):
        return parts_of([MIX0.index((name, i))])

    def ev(name, i=0):
        return [(name, i, None)]

    def cut(name, i, *steps):
        parts, at = [], 0
        for q, step in zip(steps[::2], steps[1::2]):
            parts += unit(name, i)[at:q] + ev(step.rstrip("1"), int(step[-1] == "1"))
            at = q
        return parts + unit(name, i)[at:]

    q, k = unit("qb"), unit("kb")
    seq = q[:4] + k[:4] + ev("sq", 0) + q[4:] + ev("sq", 1) + k[4:]
    seq += unit("vb", 0) + ev("ssq") + cut("vb", 1, 6, "rinv")
    seq += cut("vb", 2, 4, "z", 6, "z_exp") + ev("z_ln") + cut("vb", 3, 4, "z_soft")
    fill = (unit("qb", 1) + unit("kb", 1) + unit("ga") + unit("ka", 0) + unit("ka", 1)
            + cut("qb", 2, 3, "gz") + cut("kb", 2, 2, "gz_v", 6, "gs") + cut("qb", 3, 3, "gd") + ev("gd_v")
            + sum((unit("va", i) for i in range(4)), [])
            + cut("kb", 3, 2, "gkv", 6, "gkv_v") + unit("qa", 0) + ev("gkv", 1) + cut("qa", 1, 4, "gkv_v1")
            + cut("ra", 0, 3, "go", 7, "go_v") + cut("ra", 1, 0, "go1", 5, "go_v1", 6, "gn") + ev("silu", 0)
            + cut("ra", 2, 3, "gn_v", 4, "gn1") + ev("gout", 0) + cut("ra", 3, 3, "gn_v1")
            + ev("silu", 1) + ev("gout", 1))

    def take(n):
        got = []
        while fill and (n or fill[0][0] != "unit"):
            n -= fill[0][0] == "unit"
            got.append(fill.pop(0))
        return got

    seq += take(2) + ev("sfx")
    for h in range(1, SH):
        seq += take(5) + ev("z", h) + ev("pv", h - 1) + take(2) + ev("z_exp", h) + take(2) + ev("z_ln", h)
        seq += take(3) + ev("z_soft", h) + take(8) + ev("sfx", h)
    seq += take(4) + ev("pv", SH - 1) + take(len(fill))
    seq += [("out", 0, (4, 5, 6)), ("out", 1, (4, 5, 6)), ("out", 0, (7,)), ("out", 1, (7,)),
            ("out", 0, (0, 1, 2, 3)), ("out", 1, (0, 1, 2, 3))]
    return joined(seq)


def mix1_order():
    def unit(u):
        return parts_of([u])

    def ev(name, i=0):
        return [(name, i, None)]

    def whole(u):
        return unit(u) + ev("split", u)

    seq = whole(0) + ev("ssq") + whole(1) + ev("rinv")
    for u in range(2, 6):
        seq += whole(u)
    seq += ev("s", 0) + ev("s_exp", 0) + whole(6) + ev("s_norm", 0)
    for n in range(CH // 2):
        if n + 1 < CH // 2:
            seq += ev("s", n + 1)
        if 7 + n < N1:
            fill = unit(7 + n)
        elif n == 5:
            fill = [("out", 0, (0, 1)), ("out", 0, (2, 3))]
        elif n == 6:
            fill = [("out", 1, (0, 1, 2, 3)), ("out", 0, (4, 5))]
        else:
            fill = [("out", 1, (4, 5))]
        half = len(fill) // 2
        if n + 1 == CH // 2:
            seq += fill + ev("t", n)
        else:
            seq += fill[:half] + ev("t", n) + ev("s_exp", n + 1) + fill[half:] + ev("s_norm", n + 1)
        if 7 + n < N1:
            seq += ev("split", 7 + n)
        seq += ev("o", n)
    return joined(seq + [("out", 0, (6, 7)), ("out", 1, (6, 7))])


SEQ0, SEQ1 = mix0_order(), mix1_order()


S_GAIN = 0
S_GLA = S_GAIN + 5 * KC
S_CONV = S_GLA + GH
S_SINK = S_CONV + LAYERS * UP * 4
S_END = S_SINK + CH // 2

ZOFF = (0, 512, 1024, 896)
ZW = (512, 384, 256, 128)
ZN = 1280


def trunk(nc, xT, w_mix0, w_mix1, w_up, w_down, small, wg2, bias, out):
    ctx = ExitStack()
    with ctx:
        def sb(name, shape, dt=F32, where=ctx):
            return where.enter_context(nc.sbuf_tensor(name, shape, dt))

        def sem(name):
            return ctx.enter_context(nc.semaphore(name))

        x = sb("x", [P, KC, T])
        h_hi = sb("h_hi", [P, KC, T], F32R)
        h_lo = sb("h_lo", [P, KC, T], F32R)
        w_raw = [sb(f"w_raw{r}", [P, UC]) for r in range(RAW)]
        w_hi = [sb(f"w_hi{s}", [P, UC], F32R) for s in range(SPL)]
        w_lo = [sb(f"w_lo{s}", [P, UC], F32R) for s in range(SPL)]
        par = sb("par", [P, S_END])
        rinv = sb("rinv", [P, T])
        rinv_col = sb("rinv_col", [P, TT])
        var_col = sb("var_col", [P, TT])
        mhalf = sb("mhalf", [P, TT])
        eps_col = sb("eps_col", [P, 1])
        gelu_warm = sb("gelu_warm", [P, 1])
        ssq = sb("ssq", [P, T])
        sq = sb("sq", [P, T])
        ident = sb("ident", [P, P])
        ones = sb("ones", [P, P])
        diag = sq

        m0 = ExitStack()

        def s0(name, shape, dt=F32):
            return sb(name, shape, dt, m0)

        ident_bf = s0("ident_bf", [P, P], BF16)
        negmask = s0("negmask", [P, P], BF16)
        negtri = s0("negtri", [P, P], F32R)
        negones = s0("negones", [P, P], F32R)
        tri_f = s0("tri_f", [P, P])
        tri16 = s0("tri16", [P, P])
        ind16 = s0("ind16", [P, 2])
        raT = s0("raT", [P, GH, T])
        qbT = s0("qbT", [P, SH // 2, T])
        kbT = s0("kbT", [P, SH // 2, T])
        vb = s0("vb", [P, TT, SH * SD])
        va = s0("va", [P, TT, GH * GV])
        ka = s0("ka", [P, TT, GH * GK])
        qaT = s0("qaT", [P, GH // 2, T])
        gaT = s0("gaT", [RANK + 1, T])
        wg2_sb = s0("wg2_sb", [RANK + 1, GH * GK])
        sbE = s0("sbE", [P, ZN])
        sbS = s0("sbS", [P, ZN])
        sbH = s0("sbH", [P, ZN], F32R)
        sbL = s0("sbL", [P, ZN], F32R)
        gE = s0("gE", [P, TT * GH * GK])
        gL = s0("gL", [P, TT * GH * GK])
        sq0 = [b[:, c, :] for b in (va, raT) for c in range(4)]
        dec = s0("dec", [P, GH // 2, NCH])
        oc_hi = s0("oc_hi", [P, KC, T], F32R)
        oc_lo = s0("oc_lo", [P, KC, T], F32R)
        m0.close()
        st = [b[:, 0:2, :].rearrange("p a t -> p (a t)").rearrange("p (c v) -> p c v", c=NCH)
              for b in (qbT, kbT)]
        oF = va
        gq = [b[:, :].rearrange("p (a t) -> p a t", a=2) for b in (gE, gL)]

        m1 = ExitStack()

        def s1(name, shape, dt=F32):
            return sb(name, shape, dt, m1)

        q1 = s1("q1", [P, KC // 2, NCH, 2, CHUNK])
        k1 = s1("k1", [P, 2, CHUNK + T])
        v1 = s1("v1", [P, TT, CKV * CD])
        v1s = s1("v1s", [P, TT, CKV * CD])
        bias_sb = s1("bias_sb", [P, CH // 2, P])
        scs = [s1(f"sc{k}", [P, NCH, P]) for k in range(2)]
        prs = [s1(f"pr{k}", [P, NCH, P]) for k in range(2)]
        prT = s1("prT", [P, NCH, P])
        mx = s1("mx", [P, NCH])
        nms = [s1(f"nm{k}", [P, NCH]) for k in range(2)]
        rss = [s1(f"rs{k}", [P, NCH]) for k in range(2)]
        ess = [s1(f"es{k}", [P, NCH]) for k in range(2)]
        den = s1("den", [P, NCH])
        rd = s1("rd", [P, NCH])
        o1_hi = s1("o1_hi", [P, KC, T], F32R)
        o1_lo = s1("o1_lo", [P, KC, T], F32R)
        m1.close()

        y_hi = sb("y_hi", [P, FC, T], F32R)
        y_lo = sb("y_lo", [P, FC, T], F32R)
        us = [sb(f"us{k}", [P, 2 + T]) for k in range(2)]
        cv = [sb(f"cv{k}", [P, T]) for k in range(2)]

        ps = ctx.enter_context(nc.psum_tensor("ps", [P, 8, T], F32))
        zs = ps[:, 4:7, :].rearrange("p b t -> p (b t)")
        B_O = 7
        B_RES = 4
        B_G = 2
        B_Z = 4
        g_banks = ps[:, B_G:B_G + 2, :].rearrange("p b t -> p (b t)")
        B_SSQ, B_RINV = 6, 7
        B_SC, B_T, B_PV = 2, 4, 6

        w_loaded = [sem(f"w_loaded{r}") for r in range(RAW)]
        w_hi_ready = sem("w_hi_ready")
        w_lo_ready = sem("w_lo_ready")
        unit_done = sem("unit_done")
        x_loaded = [sem(f"x_loaded{i}") for i in range(4)]
        par_loaded = sem("par_loaded")
        wg2_loaded = sem("wg2_loaded")
        bias_loaded = sem("bias_loaded")
        consts = sem("consts")
        consts_dve = sem("consts_dve")
        sq_ready = sem("sq_ready")
        ssq_added = sem("ssq_added")
        hi_ready = sem("hi_ready")
        lo_ready = sem("lo_ready")
        x_updated = sem("x_updated")
        ssq_col = sem("ssq_col")
        var_ready = sem("var_ready")
        rcol_ready = sem("rcol_ready")
        diag_ready = sem("diag_ready")
        rbc_done = sem("rbc_done")
        rinv_ready = sem("rinv_ready")
        a_taken = sem("a_taken")
        b_taken = sem("b_taken")
        sb_z = sem("sb_z")
        sb_abs = sem("sb_abs")
        sb_e = sem("sb_e")
        sb_ln = sem("sb_ln")
        sb_sp = sem("sb_sp")
        sb_hi = sem("sb_hi")
        sb_lo = sem("sb_lo")
        sb_sum = sem("sb_sum")
        sb_w = sem("sb_w")
        sb_pv = sem("sb_pv")
        oc_hi_ready = sem("oc_hi_ready")
        oc_lo_ready = sem("oc_lo_ready")
        silu_done = sem("silu_done")
        g_z = sem("g_z")
        g_abs = sem("g_abs")
        g_e = sem("g_e")
        g_ln = sem("g_ln")
        g_log = sem("g_log")
        g_sum = sem("g_sum")
        g_total = sem("g_total")
        g_exp = sem("g_exp")
        g_kd = sem("g_kd")
        g_kv = sem("g_kv")
        g_state = sem("g_state")
        g_o = sem("g_o")
        g_ocopy = sem("g_ocopy")
        g_osq = sem("g_osq")
        g_osum = sem("g_osum")
        g_lnv = sem("g_lnv")
        g_rms = sem("g_rms")
        g_norm = sem("g_norm")
        g_out = sem("g_out")
        gla_hi_ready = sem("gla_hi_ready")
        gla_lo_ready = sem("gla_lo_ready")
        c_pad = sem("c_pad")
        vs_loaded = [sem(f"vs_loaded{i}") for i in range(2)]
        c_s = sem("c_s")
        c_bias = sem("c_bias")
        c_mask = sem("c_mask")
        c_mx = sem("c_mx")
        c_nm = sem("c_nm")
        c_exp = sem("c_exp")
        c_den = sem("c_den")
        c_rd = sem("c_rd")
        c_p = sem("c_p")
        c_t = sem("c_t")
        c_tc = sem("c_tc")
        c_pv = sem("c_pv")
        o1_hi_ready = sem("o1_hi_ready")
        o1_lo_ready = sem("o1_lo_ready")
        u_scaled = sem("u_scaled")
        u_mid = sem("u_mid")
        conv1 = sem("conv1")
        conv2 = sem("conv2")
        gelu_done = sem("gelu_done")
        y_mul = sem("y_mul")
        yhi_ready = sem("yhi_ready")
        ylo_ready = sem("ylo_ready")
        halo = sem("halo")
        warmed = sem("warmed")
        out_ready = sem("out_ready")
        out_written = sem("out_written")

        def gain_at(n, c):
            return par[:, bass.ds(S_GAIN + n * KC + c, 1)]

        def blk(t, c):
            return t[:, bass.ds(c, 1), :].rearrange("p o t -> p (o t)")

        B_PARTS = {"vb": 4, "va": 4, "ka": 2, "v": 2}

        def a_before(units, u):
            return sum(n not in B_PARTS for n, _ in units[:u])

        def a_bank0(a):
            return B_Z + a if a < 2 else a % 2

        def out_bank(c, units):
            return (a_before(units, len(units)) + c) % 2 if c < 2 else B_RES + c % 2

        def b_before(units, u):
            return TT * sum(n in B_PARTS and i == B_PARTS[n] - 1 for n, i in units[:u])

        B_ORDER = (0, 1, 2, 3)
        A_MIX0, B_MIX0 = a_before(MIX0, N0), b_before(MIX0, N0)
        N_CONSTS = 16
        WARM = 14
        NADD = KC + 1

        def x_pair(i):
            return xT[:, 2 * i * T:(2 * i + 2) * T].rearrange("p (c t) -> p c t", t=T)

        o1_psum = ps[:, B_PV:B_PV + 2, :].rearrange("p b (c e q) -> p e (b c) q", e=2, q=CHUNK)

        def o1_tiles(t, g):
            return t[:, 2 * g:2 * g + 2, :].rearrange("p e (c q) -> p e c q", q=CHUNK)

        block = ctx.enter_context(nc.Block())

        @block.sync
        def _(sp):
            def unit(u, r, src, cols=UC):
                sp.wait_ge(w_lo_ready, u - (RAW - 1))
                sp.dma_start(w_raw[r][:, 0:cols], src).then_inc(w_loaded[r], 16)

            def one(t, i):
                return t[bass.ds(i, 1)].rearrange("o p c -> (o p) c")

            for u in range(RAW):
                sp.dma_start(w_raw[u][:, :], w_mix0[u]).then_inc(w_loaded[u], 16)
                if u < 2:
                    i = 3 * u
                    sp.dma_start(x[:, 2 * i:2 * i + 2, :], x_pair(i)).then_inc(x_loaded[i], 16)
            sp.dma_start(wg2_sb[:, :], wg2).then_inc(wg2_loaded, 16)
            with sp.Fori(1, U_UP0 // RAW) as i:
                for k in range(RAW):
                    unit(RAW * i + k, k, one(w_mix0, RAW * i + k))
            for u in range(U_UP0 // RAW * RAW, U_UP0):
                unit(u, u % RAW, w_mix0[u])

            def ffn(layer, u_up, u_dn):
                with sp.Fori(0, UP // RAW) as i:
                    for k in range(RAW):
                        unit(u_up + k + RAW * i, (u_up + k) % RAW, one(w_up, layer * UP + k + RAW * i))
                with sp.Fori(0, KC) as i:
                    for k in range(len(DN)):
                        src = w_down[bass.ds(layer * KC + i, 1), :, DOFF[k] * P:(DOFF[k] + DN[k]) * P]
                        unit(u_dn + k + RAW * i, (u_dn + k) % RAW,
                             src.rearrange("o p c -> (o p) c"), DN[k] * P)

            ffn(0, U_UP0, U_DN0)
            with sp.Fori(0, (N1 + KC) // RAW) as i:
                for k in range(RAW):
                    unit(U_MIX1 + k + RAW * i, (U_MIX1 + k) % RAW, one(w_mix1, k + RAW * i))
            ffn(1, U_UP1, U_DN1)
            for c in range(KC):
                sp.wait_ge(out_ready, c + 1)
                sp.dma_start(out[:, c * T:(c + 1) * T], x[:, c, :]).then_inc(out_written, 16)
            sp.wait_ge(out_written, 16 * KC)

        @block.gpsimd
        def _(pool):
            n = [0]

            def step(ins):
                ins.then_inc(consts, 1)
                n[0] += 1
                pool.wait_ge(consts, n[0])

            g = nc.gpsimd
            step(g.memset(mhalf[:, :], -0.5))
            step(g.memset(eps_col[:, :], EPS))
            step(g.memset(ones[:, :], 1.0))
            step(g.memset(ident[:, :], 0.0))
            step(g.affine_select(out=ident[:, :], in_=ident[:, :], compare_op=ALU.not_equal, fill=1.0,
                                 base=0, pattern=[[-1, P]], channel_multiplier=1))
            step(g.memset(gaT[:, :], 1.0))
            step(g.memset(negmask[:, :], NEG))
            step(g.affine_select(out=negmask[:, :], in_=negmask[:, :], compare_op=ALU.is_ge, fill=0.0,
                                 base=0, pattern=[[-1, P]], channel_multiplier=1))
            step(g.memset(tri_f[:, :], -1.0))
            step(g.affine_select(out=tri_f[:, :], in_=tri_f[:, :], compare_op=ALU.is_ge, fill=0.0,
                                 base=0, pattern=[[-1, P]], channel_multiplier=1))
            step(g.memset(tri16[:, :], 1.0 / TAU))
            step(g.affine_select(out=tri16[:, :], in_=tri16[:, :], compare_op=ALU.is_gt, fill=0.0,
                                 base=0, pattern=[[-1, P]], channel_multiplier=1))
            step(g.memset(tri16[CHUNK:P, 0:CHUNK], 0.0))
            step(g.memset(ind16[:, :], 0.0))
            step(g.memset(ind16[0:CHUNK, 0:1], 1.0 / TAU))
            step(g.memset(ind16[CHUNK:P, 1:2], 1.0 / TAU))
            assert n[0] == N_CONSTS

            for norm in range(2 * LAYERS + 1):
                pool.wait_ge(var_ready, norm + 1)
                g.tensor_tensor(rinv_col[:, :], var_col[:, :], mhalf[:, :], ALU.pow).then_inc(rcol_ready, 1)

        @block.scalar
        def _(act):
            s = nc.scalar

            def hi(u, gen, r, cols=UC):
                act.wait_ge(w_loaded[r], 16 * gen + 16)
                act.wait_ge(unit_done, u - (SPL - 1))
                s.activation(w_hi[r % SPL][:, 0:cols], w_raw[r][:, 0:cols], ACT.Copy).then_inc(w_hi_ready, 1)

            def hi_static(u, cols=UC):
                if u < U_END:
                    hi(u, u // RAW, u % RAW, cols)

            def norm_tile(norm, c, r, last=False):
                act.wait_ge(x_updated, r + 1)
                act.wait_ge(ssq_added, norm * NADD + 1 + c)
                s.activation(sq[:, :], blk(x, c), ACT.Square).then_inc(sq_ready, 1)
                if not last:
                    s.activation(blk(h_hi, c), blk(x, c), ACT.Copy, scale=gain_at(norm, c)).then_inc(hi_ready, 1)

            def rinv_copy(norm):
                act.wait_ge(rbc_done, norm + 1)
                s.activation(rinv[:, :], ps[:, B_RINV, :], ACT.Copy).then_inc(rinv_ready, 1)

            act.dma_start(par[:, :], small).then_inc(par_loaded, 16)
            for i in (1, 2):
                act.dma_start(x[:, 2 * i:2 * i + 2, :], x_pair(i)).then_inc(x_loaded[i], 16)

            for c in range(KC):
                if c % 4 == 0:
                    act.wait_ge(w_loaded[c // 4], 16)
                    s.activation(w_hi[c // 4][:, :], w_raw[c // 4][:, :], ACT.Copy).then_inc(w_hi_ready, 1)
                if c == 0:
                    act.wait_ge(par_loaded, 16)
                if c % 2 == 0:
                    act.wait_ge(x_loaded[c // 2], 16)
                s.activation(h_hi[:, c, :], x[:, c, :], ACT.Copy, scale=gain_at(0, c)).then_inc(hi_ready, 1)

            def b_evac(dst, bank0, n_cols):
                for tt in B_ORDER:
                    s.activation(dst[:, tt, :], ps[:, bank0 + tt, 0:n_cols], ACT.Copy,
                                 scale=rinv_col[:, tt:tt + 1]).then_inc(b_taken, 1)

            for name, i, span in SEQ0:
                if name == "unit" and span[1] == 8:
                    n, part = MIX0[i]
                    if n in B_PARTS and part == B_PARTS[n] - 1:
                        act.wait_ge(unit_done, i + 1)
                        b_evac({"vb": vb, "va": va, "ka": ka}[n], 0, {"vb": SH * SD, "va": GH * GV, "ka": GH * GK}[n])
                    hi_static(i + SPL)
                elif name == "sq":
                    for c in range(4 * i, 4 * i + 4):
                        s.activation(sq0[c], x[:, c, :], ACT.Square).then_inc(sq_ready, 1)
                elif name == "rinv":
                    rinv_copy(0)
                elif name == "z":
                    act.wait_ge(sb_z, i + 1)
                    act.wait_ge(sb_sp, i)
                    s.activation(sbE[:, :], zs[:, 0:ZN], ACT.Abs).then_inc(sb_abs, 1)
                elif name == "z_exp":
                    act.wait_ge(sb_abs, i + 1)
                    s.activation(sbE[:, :], sbE[:, :], ACT.Exp, scale=-1.0).then_inc(sb_e, 1)
                elif name == "z_ln":
                    act.wait_ge(sb_e, i + 1)
                    s.activation(sbE[:, :], sbE[:, :], ACT.Ln, bias=1.0).then_inc(sb_ln, 1)
                elif name == "sfx":
                    act.wait_ge(sb_sum, i + 1)
                    s.activation(sbS[:, :], zs[:, 0:ZN], ACT.Exp).then_inc(sb_w, 1)
                elif name == "pv" and i % 2 == 1:
                    act.wait_ge(sb_pv, i + 1)
                    s.activation(oc_hi[:, GH + i // 2, :], ps[:, B_O, :], ACT.Copy).then_inc(oc_hi_ready, 1)
                elif name == "gz":
                    act.wait_ge(g_z, 1)
                    s.activation(gE[:, :], g_banks, ACT.Abs).then_inc(g_abs, 1)
                    act.wait_ge(g_abs, 1)
                    s.activation(gE[:, :], gE[:, :], ACT.Exp, scale=-1.0).then_inc(g_e, 1)
                    act.wait_ge(g_e, 1)
                    s.activation(gE[:, :], gE[:, :], ACT.Ln, bias=1.0).then_inc(g_ln, 1)
                elif name == "gs":
                    act.wait_ge(g_sum, 1)
                    s.activation(gE[:, :], g_banks, ACT.Exp).then_inc(g_exp, 1)
                elif name == "gd":
                    act.wait_ge(g_total, 1)
                    s.activation(dec[:, :, :].rearrange("p a c -> p (a c)"), ps[:, B_G, 0:2 * NCH], ACT.Exp).then_inc(g_exp, 1)
                elif name == "go":
                    act.wait_ge(g_o, i + 1)
                    s.activation(oF[:, 2 * i:2 * i + 2, :].rearrange("p a t -> p (a t)"), g_banks, ACT.Copy).then_inc(g_ocopy, 1)
                elif name == "gn":
                    act.wait_ge(g_osum, i + 1)
                    act.wait_ge(consts, 2)
                    s.activation(gq[i].rearrange("p a t -> p (a t)"), g_banks, ACT.Ln, scale=1.0 / GV,
                                 bias=eps_col[:, 0:1]).then_inc(g_lnv, 1)
                    act.wait_ge(g_lnv, i + 1)
                    s.activation(gq[i], gq[i], ACT.Exp, scale=-0.5).then_inc(g_rms, 1)
                elif name == "silu":
                    act.wait_ge(a_taken, a_before(MIX0, MIX0.index(("ra", 2 * i + 1))) + 1)
                    s.activation(raT[:, 2 * i:2 * i + 2, :], raT[:, 2 * i:2 * i + 2, :], ACT.Silu).then_inc(silu_done, 1)
                elif name == "gout":
                    for h in (2 * i, 2 * i + 1):
                        act.wait_ge(g_out, h + 1)
                        s.activation(oc_hi[:, h, :], oF[:, h, :], ACT.Copy).then_inc(gla_hi_ready, 1)

            def w_out(norm, u0, r0):
                for c in range(KC):
                    hi_static(u0 + c + SPL)
                    norm_tile(norm, c, r0 + c)

            def ffn(layer, norm, u_up, u_dn, r0, next_cols, last):
                act.wait_ge(warmed, layer)
                s.activation(gelu_warm[:, :], par[:, 0:1], ACT.Gelu_apprx_tanh).then_inc(warmed, 1)

                def up_hi(i, k, cols=UC):
                    hi(u_up + k + SPL + 4 * i, (u_up + k + SPL) // RAW + i, (u_up + k + SPL) % RAW, cols)

                def up_tile(i, k):
                    m = layer * UP + k + 4 * i
                    pair = layer * FC + k // 2 + 2 * i
                    taps = S_CONV + (layer * UP + k) * 4 + 16 * i
                    act.wait_ge(ylo_ready, pair)
                    act.wait_ge(u_scaled, m + 1)
                    s.activation(cv[k % 2][:, :], us[k % 2][:, 2:2 + T], ACT.Identity,
                                 bias=par[:, bass.ds(taps + 3, 1)],
                                 scale=par[:, bass.ds(taps + 2, 1)]).then_inc(u_mid, 1)
                    if k % 2 == 0:
                        act.wait_ge(conv2, m + 1)
                        s.activation(cv[0][:, :], cv[0][:, :], ACT.Gelu_apprx_tanh).then_inc(gelu_done, 1)
                    else:
                        act.wait_ge(y_mul, pair + 1)
                        s.activation(blk(y_hi, k // 2 + 2 * i), cv[1][:, :], ACT.Copy).then_inc(yhi_ready, 1)

                up_hi(0, 0)
                up_hi(0, 1)
                rinv_copy(norm)
                up_tile(0, 0)
                up_tile(0, 1)
                for k in (2, 3):
                    up_hi(0, k)
                    up_tile(0, k)
                with act.Fori(1, UP // 4 - 1) as i:
                    for k in range(4):
                        up_hi(i, k)
                        up_tile(i, k)
                for k in range(4):
                    up_hi(UP // 4 - 1, k, UC if k < 4 - SPL else DN[k - 4 + SPL] * P)
                    up_tile(UP // 4 - 1, k)

                def down_pair(i, ahead):
                    for j in range(2):
                        for kk in range(4 * j, 4 * j + 4):
                            if kk + SPL < 8 or ahead is not None:
                                cols = DN[(kk + SPL) % 4] * P if kk + SPL < 8 else ahead[kk + SPL - 8]
                                hi(u_dn + kk + SPL + 8 * i, (u_dn + kk + SPL) // RAW + 2 * i,
                                   (u_dn + kk + SPL) % RAW, cols)
                        norm_tile(norm + 1, j + 2 * i, r0 + j + 2 * i, last)

                with act.Fori(0, KC // 2 - 1) as i:
                    down_pair(i, [DN[k] * P for k in range(SPL)])
                down_pair(KC // 2 - 1, next_cols)

            w_out(1, U_OUT0, 0)
            ffn(0, 1, U_UP0, U_DN0, KC, [UC] * SPL, False)

            for name, i, span in SEQ1:
                if name == "split":
                    hi_static(U_MIX1 + i + SPL)
                elif name == "unit" and span[1] == 8:
                    if i == 0:
                        act.dma_start(bias_sb[:, :, :], bias.rearrange("p (n k) -> p n k", k=P)).then_inc(bias_loaded, 16)
                    if MIX1[i] == ("v", 1):
                        act.wait_ge(unit_done, U_MIX1 + i + 1)
                        b_evac(v1, B_SC, CKV * CD)
                        act.wait_ge(b_taken, B_MIX0 + TT)
                        act.dma_start(v1s[0:CHUNK, 1:TT, :], v1[CHUNK:P, 0:TT - 1, :]).then_inc(vs_loaded[0], 16)
                        act.dma_start(v1s[CHUNK:P, :, :], v1[0:CHUNK, :, :]).then_inc(vs_loaded[1], 16)
                elif name == "rinv":
                    rinv_copy(2)
                elif name == "s_exp":
                    sc, pr, nm, rs, es = (t[i % 2] for t in (scs, prs, nms, rss, ess))
                    act.wait_ge(c_nm, i + 1)
                    if i >= 2:
                        act.wait_ge(c_den, i - 1)
                        act.wait_ge(c_t, i - 1)
                    s.activation(es[:, :], nm[:, :], ACT.Exp, bias=par[:, S_SINK + i:S_SINK + i + 1])
                    for c in range(NCH):
                        ins = s.activation(pr[:, c, :], sc[:, c, :], ACT.Exp, bias=nm[:, c:c + 1],
                                           accum_out=rs[:, c:c + 1])
                    ins.then_inc(c_exp, 1)
                elif name == "t":
                    act.wait_ge(c_t, i + 1)
                    act.wait_ge(c_pv, i)
                    s.activation(prT[:, :, :].rearrange("p c k -> p (c k)"),
                                 ps[:, B_T:B_T + 2, :].rearrange("p b t -> p (b t)"), ACT.Copy).then_inc(c_tc, 1)
                elif name == "o" and i % 2 == 1:
                    act.wait_ge(c_pv, i + 1)
                    s.activation(o1_tiles(o1_hi, i // 2), o1_psum, ACT.Copy).then_inc(o1_hi_ready, 1)
            w_out(3, U_OUT1, 2 * KC)
            ffn(1, 3, U_UP1, U_DN1, 3 * KC, None, True)
            rinv_copy(2 * LAYERS)

        @block.vector
        def _(dve):
            v = nc.vector

            def lo(u, r, cols=UC):
                dve.wait_ge(w_hi_ready, u + 1)
                v.tensor_tensor(w_lo[r % SPL][:, 0:cols], w_raw[r][:, 0:cols],
                                w_hi[r % SPL][:, 0:cols].bitcast(F32), ALU.subtract).then_inc(w_lo_ready, 1)

            def lo_static(u, cols=UC):
                lo(u, u % RAW, cols)

            def add_sq(norm, c, squares=sq[:, :]):
                dve.wait_ge(sq_ready, norm * KC + 1 + c)
                dve.wait_ge(ssq_added, norm * NADD + 1 + c)
                v.tensor_tensor(ssq[:, :], ssq[:, :], squares, ALU.add).then_inc(ssq_added, 1)

            def h_lo_part(norm, c):
                dve.wait_ge(hi_ready, norm * KC + 1 + c)
                v.scalar_tensor_tensor(blk(h_lo, c), blk(x, c), gain_at(norm, c),
                                       blk(h_hi, c).bitcast(F32), ALU.mult, ALU.subtract).then_inc(lo_ready, 1)

            def res_tile(norm, c, bank, r, units, last=False):
                dve.wait_ge(unit_done, units)
                v.tensor_tensor(blk(x, c), ps[:, bank, :], blk(x, c), ALU.add).then_inc(x_updated, 1)
                if not last:
                    dve.wait_ge(x_updated, r + 1)
                    h_lo_part(norm, c)
                add_sq(norm, c)

            def rms(norm):
                dve.wait_ge(ssq_col, norm + 1)
                v.tensor_scalar(var_col[:, :], ps[:, B_SSQ, 0:TT], 1.0 / D, EPS, ALU.mult, ALU.add).then_inc(var_ready, 1)
                if norm < 2 * LAYERS:
                    v.memset(ssq[:, :], 0.0).then_inc(ssq_added, 1)
                dve.wait_ge(rcol_ready, norm + 1)
                v.tensor_tensor(diag[:, :].rearrange("p (a t) -> p a t", a=TT),
                                ident[:, :].unsqueeze(1).broadcast_to([P, TT, P]),
                                rinv_col[:, :].unsqueeze(2).broadcast_to([P, TT, P]), ALU.mult).then_inc(diag_ready, 1)

            v.memset(ssq[:, :], 0.0).then_inc(ssq_added, 1)
            for c in range(KC):
                if c % 4 == 0:
                    lo_static(c // 4)
                h_lo_part(0, c)
            dve.wait_ge(consts, N_CONSTS)
            v.tensor_copy(ident_bf[:, :], ident[:, :]).then_inc(consts_dve, 1)
            v.tensor_copy(negtri[:, :], tri_f[:, :]).then_inc(consts_dve, 1)
            v.tensor_scalar(negones[:, :], ones[:, :], -1.0, None, ALU.mult).then_inc(consts_dve, 1)

            def a_evac0(u):
                (n, i), a = MIX0[u], a_before(MIX0, u)
                dve.wait_ge(unit_done, u + 1)
                src = ps[:, a_bank0(a), :]
                if n in ("ra", "kb"):
                    dst = (raT if n == "ra" else kbT)[:, i, :]
                    ins = v.tensor_tensor(dst, src, rinv[:, :], ALU.mult)
                elif n in ("qb", "qa"):
                    dst, width = (qbT, SD) if n == "qb" else (qaT, GK)
                    ins = v.scalar_tensor_tensor(dst[:, i, :], src, width ** -0.5, rinv[:, :], ALU.mult, ALU.mult)
                else:
                    ins = v.tensor_tensor(gaT[0:RANK, :], ps[0:RANK, a_bank0(a), :], rinv[0:RANK, :], ALU.mult)
                ins.then_inc(a_taken, 1)

            for name, i, span in SEQ0:
                if name == "unit" and span[1] == 8:
                    if i >= 2 and MIX0[i][0] not in B_PARTS:
                        a_evac0(i)
                    lo_static(i + SPL)
                elif name == "sq":
                    for c in range(4 * i, 4 * i + 4):
                        add_sq(0, c, sq0[c])
                elif name == "ssq":
                    rms(0)
                elif name == "rinv":
                    dve.wait_ge(rinv_ready, 1)
                    a_evac0(0)
                    a_evac0(1)
                elif name == "z_soft":
                    dve.wait_ge(sb_ln, i + 1)
                    dve.wait_ge(sb_pv, i)
                    v.scalar_tensor_tensor(sbS[:, :], zs[:, 0:ZN], 0.0, sbE[:, :], ALU.max, ALU.add).then_inc(sb_sp, 1)
                    dve.wait_ge(sb_sp, i + 1)
                    v.tensor_copy(sbH[:, :], sbS[:, :]).then_inc(sb_hi, 1)
                    dve.wait_ge(sb_hi, i + 1)
                    v.tensor_tensor(sbL[:, :], sbS[:, :], sbH[:, :].bitcast(F32), ALU.subtract).then_inc(sb_lo, 1)
                elif name == "pv" and i % 2 == 1:
                    dve.wait_ge(oc_hi_ready, i // 2 + 1)
                    v.tensor_tensor(oc_lo[:, GH + i // 2, :], ps[:, B_O, :],
                                    oc_hi[:, GH + i // 2, :].bitcast(F32), ALU.subtract).then_inc(oc_lo_ready, 1)
                elif name == "gz_v":
                    dve.wait_ge(g_ln, 1)
                    v.scalar_tensor_tensor(gL[:, :], g_banks, 0.0, gE[:, :], ALU.min, ALU.subtract).then_inc(g_log, 1)
                elif name == "gd_v":
                    dve.wait_ge(g_exp, 1)
                    dve.wait_ge(b_taken, b_before(MIX0, MIX0.index(("ka", 1)) + 1))
                    k_all = ka[:, :, :].rearrange("p a n -> p (a n)")
                    v.tensor_tensor(k_all, gE[:, :], k_all, ALU.mult).then_inc(g_kd, 1)
                elif name == "gkv_v":
                    dve.wait_ge(g_kv, i + 1)
                    dve.wait_ge(g_exp, 2)
                    for c in range(NCH):
                        kv = ps[:, B_G + c % 2, (c // 2) * GV:(c // 2 + 1) * GV]
                        if c == 0:
                            v.tensor_copy(st[i][:, 0, :], kv).then_inc(g_state, 1)
                        else:
                            dve.wait_ge(g_state, NCH * i + c)
                            v.scalar_tensor_tensor(st[i][:, c, :], st[i][:, c - 1, :], dec[:, i, c:c + 1], kv,
                                                   ALU.mult, ALU.add).then_inc(g_state, 1)
                elif name == "go_v":
                    dve.wait_ge(g_ocopy, i + 1)
                    o_pair = oF[:, 2 * i:2 * i + 2, :]
                    v.tensor_tensor(gq[i], o_pair, o_pair, ALU.mult).then_inc(g_osq, 1)
                elif name == "gn_v":
                    dve.wait_ge(g_rms, i + 1)
                    o_pair = oF[:, 2 * i:2 * i + 2, :]
                    v.tensor_tensor(o_pair, o_pair, gq[i], ALU.mult).then_inc(g_norm, 1)
                elif name == "gout":
                    dve.wait_ge(g_norm, i + 1)
                    dve.wait_ge(silu_done, i + 1)
                    for h in (2 * i, 2 * i + 1):
                        v.scalar_tensor_tensor(oF[:, h, :], oF[:, h, :], par[:, S_GLA + h:S_GLA + h + 1],
                                               raT[:, h, :], ALU.mult, ALU.mult).then_inc(g_out, 1)
                    for h in (2 * i, 2 * i + 1):
                        dve.wait_ge(gla_hi_ready, h + 1)
                        v.tensor_tensor(oc_lo[:, h, :], oF[:, h, :], oc_hi[:, h, :].bitcast(F32),
                                        ALU.subtract).then_inc(gla_lo_ready, 1)

            def w_out(norm, u0, r0, units):
                for c in range(KC):
                    lo_static(u0 + c + SPL)
                    res_tile(norm, c, out_bank(c, units), r0 + c, u0 + c + 1)

            def ffn(layer, norm, u_up, u_dn, r0, next_cols, last):
                def up_lo(i, k, cols=UC):
                    lo(u_up + k + SPL + 4 * i, (u_up + k + SPL) % RAW, cols)

                def up_scale(i, k):
                    dve.wait_ge(unit_done, u_up + k + 1 + 4 * i)
                    v.tensor_tensor(us[k % 2][:, 2:2 + T], ps[:, k, :], rinv[:, :], ALU.mult).then_inc(u_scaled, 1)

                def up_conv(i, k):
                    m = layer * UP + k + 4 * i
                    pair = layer * FC + k // 2 + 2 * i
                    taps = S_CONV + (layer * UP + k) * 4 + 16 * i
                    dve.wait_ge(u_mid, m + 1)
                    v.scalar_tensor_tensor(cv[k % 2][:, :], us[k % 2][:, 1:1 + T], par[:, bass.ds(taps + 1, 1)],
                                           cv[k % 2][:, :], ALU.mult, ALU.add).then_inc(conv1, 1)
                    dve.wait_ge(conv1, m + 1)
                    v.scalar_tensor_tensor(cv[k % 2][:, :], us[k % 2][:, 0:T], par[:, bass.ds(taps, 1)],
                                           cv[k % 2][:, :], ALU.mult, ALU.add).then_inc(conv2, 1)
                    if k % 2 == 1:
                        dve.wait_ge(conv2, m + 1)
                        dve.wait_ge(gelu_done, pair + 1)
                        v.tensor_tensor(cv[1][:, :], cv[1][:, :], cv[0][:, :], ALU.mult).then_inc(y_mul, 1)
                        dve.wait_ge(yhi_ready, pair + 1)
                        p = k // 2 + 2 * i
                        v.tensor_tensor(blk(y_lo, p), cv[1][:, :], blk(y_hi, p).bitcast(F32),
                                        ALU.subtract).then_inc(ylo_ready, 1)

                up_lo(0, 0)
                for k in range(2):
                    v.memset(us[k][:, 0:2], 0.0).then_inc(halo, 1)
                rms(norm)
                up_lo(0, 1)
                dve.wait_ge(halo, 2 * (layer + 1))
                dve.wait_ge(rinv_ready, norm + 1)
                for k in range(2):
                    up_scale(0, k)
                    up_conv(0, k)
                for k in (2, 3):
                    up_scale(0, k)
                    up_lo(0, k)
                    up_conv(0, k)
                with dve.Fori(1, UP // 4 - 1) as i:
                    for k in range(4):
                        up_scale(i, k)
                        up_lo(i, k)
                        up_conv(i, k)
                for k in range(4):
                    up_scale(UP // 4 - 1, k)
                    up_lo(UP // 4 - 1, k, UC if k < 4 - SPL else DN[k - 4 + SPL] * P)
                    up_conv(UP // 4 - 1, k)

                def down_pair(i, ahead):
                    for j in range(2):
                        for kk in range(4 * j, 4 * j + 4):
                            if kk + SPL < 8 or ahead is not None:
                                cols = DN[(kk + SPL) % 4] * P if kk + SPL < 8 else ahead[kk + SPL - 8]
                                lo(u_dn + kk + SPL + 8 * i, (u_dn + kk + SPL) % RAW, cols)
                        res_tile(norm + 1, j + 2 * i, B_RES + j, r0 + j + 2 * i, u_dn + 4 * j + 4 + 8 * i, last)

                with dve.Fori(0, KC // 2 - 1) as i:
                    down_pair(i, [DN[k] * P for k in range(SPL)])
                down_pair(KC // 2 - 1, next_cols)

            w_out(1, U_OUT0, 0, MIX0)
            ffn(0, 1, U_UP0, U_DN0, KC, [UC] * SPL, False)

            def a_evac1(i):
                n, part = MIX1[i]
                dve.wait_ge(unit_done, U_MIX1 + i + 1)
                src, scale = ps[:, a_before(MIX1, i) % 2, :], rinv[:, :]
                if n == "k":
                    dst = k1[:, part, CHUNK:CHUNK + T]
                else:
                    dst = q1[:, part // 2, :, part % 2, :]
                    src, scale = (t.rearrange("p (c q) -> p c q", q=CHUNK) for t in (src, scale))
                v.tensor_tensor(dst, src, scale, ALU.mult).then_inc(a_taken, 1)

            for name, i, span in SEQ1:
                if name == "unit" and span[1] == 8:
                    if i >= 2 and MIX1[i][0] not in B_PARTS:
                        a_evac1(i)
                elif name == "split":
                    lo_static(U_MIX1 + i + SPL)
                elif name == "ssq":
                    rms(2)
                    v.memset(k1[:, :, 0:CHUNK], 0.0).then_inc(c_pad, 1)
                    v.memset(v1s[0:CHUNK, 0, :], 0.0).then_inc(c_pad, 1)
                elif name == "rinv":
                    dve.wait_ge(rinv_ready, 3)
                    a_evac1(0)
                    a_evac1(1)
                elif name == "s":
                    sc, nm = scs[i % 2], nms[i % 2]
                    dve.wait_ge(c_s, i + 1)
                    if i == 0:
                        dve.wait_ge(bias_loaded, 16)
                    if i >= 2:
                        dve.wait_ge(c_exp, i - 1)
                    v.scalar_tensor_tensor(sc[:, :, :], ps[:, B_SC:B_SC + 2, :].rearrange("p b (c k) -> p (b c) k", k=P),
                                           CD ** -0.5, bias_sb[:, i, :].unsqueeze(1).broadcast_to([P, NCH, P]),
                                           ALU.mult, ALU.add).then_inc(c_bias, 1)
                    dve.wait_ge(c_bias, i + 1)
                    v.memset(sc[:, 0, 0:CHUNK], NEG).then_inc(c_mask, 1)
                    dve.wait_ge(c_mask, i + 1)
                    v.tensor_reduce(mx[:, :], sc[:, :, :], AX.X, ALU.max).then_inc(c_mx, 1)
                    dve.wait_ge(c_mx, i + 1)
                    v.tensor_scalar(nm[:, :], mx[:, :], par[:, S_SINK + i:S_SINK + i + 1], -1.0,
                                    ALU.max, ALU.mult).then_inc(c_nm, 1)
                elif name == "s_norm":
                    pr, rs, es = prs[i % 2], rss[i % 2], ess[i % 2]
                    dve.wait_ge(c_exp, i + 1)
                    v.tensor_tensor(den[:, :], rs[:, :], es[:, :], ALU.add).then_inc(c_den, 1)
                    dve.wait_ge(c_den, i + 1)
                    v.reciprocal(rd[:, :], den[:, :]).then_inc(c_rd, 1)
                    dve.wait_ge(c_rd, i + 1)
                    v.tensor_tensor(pr[:, :, :], pr[:, :, :], rd[:, :].unsqueeze(2).broadcast_to([P, NCH, P]),
                                    ALU.mult).then_inc(c_p, 1)
                elif name == "o" and i % 2 == 1:
                    dve.wait_ge(o1_hi_ready, i // 2 + 1)
                    v.tensor_tensor(o1_tiles(o1_lo, i // 2), o1_psum, o1_tiles(o1_hi, i // 2).bitcast(F32),
                                    ALU.subtract).then_inc(o1_lo_ready, 1)
            w_out(3, U_OUT1, 2 * KC, MIX1)
            ffn(1, 3, U_UP1, U_DN1, 3 * KC, None, True)

            rms(2 * LAYERS)
            dve.wait_ge(rinv_ready, 2 * LAYERS + 1)
            for c in range(KC):
                v.scalar_tensor_tensor(x[:, c, :], x[:, c, :], gain_at(2 * LAYERS, c), rinv[:, :],
                                       ALU.mult, ALU.mult).then_inc(out_ready, 1)

        @block.tensor
        def _(pe):
            mm = nc.tensor.matmul

            def three(dst, w, m, first, last):
                mm(dst, w[0], m[0], start=first, stop=False)
                mm(dst, w[0], m[1], start=False, stop=False)
                return mm(dst, w[1], m[0], start=False, stop=last)

            def w_blocks(r, c, n=P):
                return tuple(t[r % SPL][:, c * n:(c + 1) * n] for t in (w_hi, w_lo))

            def a_unit(u, r, bank, h_blocks=None, span=(0, KC)):
                if span[0] == 0:
                    pe.wait_ge(w_lo_ready, u + 1)
                for c in range(*span):
                    if h_blocks is not None:
                        pe.wait_ge(lo_ready, h_blocks + c + 1)
                    ins = three(ps[:, bank, :], w_blocks(r, c), (h_hi[:, c, :], h_lo[:, c, :]),
                                c == 0, c == KC - 1)
                if span[1] == KC:
                    ins.then_inc(unit_done, 1)

            def b_unit(u, part, parts, bank0, n_cols, span=(0, 8), a_taken_by=None):
                if span[0] == 0:
                    pe.wait_ge(w_lo_ready, u + 1)
                blocks = KC // parts
                for step in range(span[0] * blocks * TT // 8, span[1] * blocks * TT // 8):
                    k, tt = step // TT, TT - 1 - step % TT
                    c = part * blocks + k
                    if a_taken_by is not None and c == 0 and tt == 1:
                        pe.wait_ge(a_taken, a_taken_by)
                    tok = slice(tt * P, (tt + 1) * P)
                    ins = three(ps[:, bank0 + tt, 0:n_cols], (h_hi[:, c, tok], h_lo[:, c, tok]),
                                w_blocks(u % RAW, k, n_cols), c == 0, c == KC - 1)
                if span[1] == 8:
                    ins.then_inc(unit_done, 1)

            def ssq_mm(norm):
                if norm == 0:
                    pe.wait_ge(consts, N_CONSTS)
                pe.wait_ge(ssq_added, NADD * (norm + 1))
                for tt in range(TT):
                    ins = mm(ps[:, B_SSQ, tt:tt + 1], ssq[:, tt * P:(tt + 1) * P], ones[:, 0:1],
                             start=True, stop=True)
                ins.then_inc(ssq_col, 1)

            def rinv_mm(norm):
                pe.wait_ge(diag_ready, norm + 1)
                mm(ps[:, B_RINV, :], ones[:, :], diag[:, :], start=True, stop=True).then_inc(rbc_done, 1)

            def out_blocks(units, u0, c, blocks, first, last, o_hi, o_lo, ready):
                if first:
                    pe.wait_ge(w_lo_ready, u0 + c + 1)
                for k in blocks:
                    ready(k)
                    ins = three(ps[:, out_bank(c, units), :], w_blocks((u0 + c) % RAW, k),
                                (o_hi[:, k, :], o_lo[:, k, :]), first and k == blocks[0], last and k == blocks[-1])
                if last:
                    ins.then_inc(unit_done, 1)

            def out_tiles(units, u0, r0, o_hi, o_lo):
                for c in range(2, KC):
                    if c >= 4:
                        pe.wait_ge(x_updated, r0 + c - 1)
                    out_blocks(units, u0, c, range(KC), True, True, o_hi, o_lo, lambda k: None)

            def is_first(seq, at):
                return all(step[:2] != seq[at][:2] for step in seq[:at])

            def is_last(seq, at):
                return all(step[:2] != seq[at][:2] for step in seq[at + 1:])

            def ffn(layer, norm, u_up, u_dn, r0):
                def up(i, k):
                    pe.wait_ge(u_scaled, layer * UP + k - 3 + 4 * i)
                    a_unit(u_up + k + 4 * i, u_up + k, k)

                a_unit(u_up, u_up, 0, norm * KC)
                ssq_mm(norm)
                a_unit(u_up + 1, u_up + 1, 1)
                rinv_mm(norm)
                a_unit(u_up + 2, u_up + 2, 2)
                a_unit(u_up + 3, u_up + 3, 3)
                with pe.Fori(1, UP // 4) as i:
                    for k in range(4):
                        up(i, k)

                def down_pair(i, first):
                    for j in range(2):
                        if not (first and r0 == 0):
                            pe.wait_ge(x_updated, r0 + j - 1 + 2 * i)
                        for k in range(4):
                            kk = u_dn + 4 * j + k
                            pe.wait_ge(w_lo_ready, kk + 1 + 8 * i)
                            if first and j == 0:
                                pe.wait_ge(ylo_ready, layer * FC + DOFF[k] + DN[k])
                            for b in range(DN[k]):
                                c = DOFF[k] + b
                                ins = three(ps[:, B_RES + j, :], w_blocks(kk, b),
                                            (y_hi[:, c, :], y_lo[:, c, :]), c == 0, c == FC - 1)
                            ins.then_inc(unit_done, 1)

                down_pair(0, True)
                with pe.Fori(1, KC // 2) as i:
                    down_pair(i, False)

            pe.wait_ge(consts, 3)
            for _ in range(WARM):
                mm(ps[:, B_RINV, 0:P], ones[:, :], ones[:, :], start=True, stop=True)

            for at, (name, i, span) in enumerate(SEQ0):
                if name == "unit":
                    n, part = MIX0[i]
                    a, b_done = a_before(MIX0, i), b_before(MIX0, i)
                    if n in B_PARTS:
                        if part == 0 and span[0] == 0:
                            if b_done:
                                pe.wait_ge(b_taken, b_done)
                            if n == "va":
                                pe.wait_ge(g_exp, 2)
                        b_unit(i, part, B_PARTS[n], 0, {"vb": SH * SD, "va": GH * GV, "ka": GH * GK}[n], span,
                               a if a > 2 else None)
                    else:
                        if a >= 4 and span[0] == 0:
                            pe.wait_ge(a_taken, a - 1)
                        if b_done and span[0] == 0:
                            pe.wait_ge(b_taken, b_done - TT + 1 + B_ORDER.index(a % 2))
                        a_unit(i, i, a_bank0(a), 0 if i < 2 else None, span)
                elif name == "ssq":
                    ssq_mm(0)
                elif name == "rinv":
                    rinv_mm(0)
                elif name == "z":
                    j, rows = i // 2, slice(SD * (i % 2), SD * (i % 2) + SD)
                    pe.wait_ge(a_taken, a_before(MIX0, MIX0.index(("kb", j))) + 1)
                    pe.wait_ge(consts_dve, 3)
                    pe.wait_ge(sb_w, i)
                    for b in (0, 1, 3, 2):
                        mm(zs[:, ZOFF[b]:ZOFF[b] + ZW[b]], kbT[rows, j, b * P:(b + 1) * P],
                           qbT[rows, j, b * P:T], start=b != 3, stop=False, skip_group_check=True)
                    for b in range(TT):
                        ins = mm(zs[:, ZOFF[b]:ZOFF[b] + P], ident_bf[:, :], negmask[:, :],
                                 start=False, stop=False, skip_group_check=True)
                    ins.then_inc(sb_z, 1)
                elif name == "sfx":
                    pe.wait_ge(sb_lo, i + 1)
                    for b in range(TT):
                        for c in range(b, TT):
                            lhs = negtri if c == b else negones
                            dst = zs[:, ZOFF[b] + (c - b) * P:ZOFF[b] + ZW[b]]
                            for part in (sbH, sbL):
                                ins = mm(dst, lhs[:, :], part[:, ZOFF[c]:ZOFF[c] + ZW[c]],
                                         start=False, stop=c == TT - 1 and part is sbL, skip_group_check=True)
                    ins.then_inc(sb_sum, 1)
                elif name == "pv":
                    j, rows = i // 2, slice(SD * (i % 2), SD * (i % 2) + SD)
                    pe.wait_ge(sb_w, i + 1)
                    pe.wait_ge(oc_lo_ready, j)
                    for b in range(TT):
                        ins = mm(ps[rows, B_O, b * P:T], vb[:, b, i * SD:(i + 1) * SD],
                                 sbS[:, ZOFF[b]:ZOFF[b] + ZW[b]], start=b == 0, stop=b == TT - 1)
                    ins.then_inc(sb_pv, 1)
                elif name == "gz":
                    pe.wait_ge(wg2_loaded, 16)
                    pe.wait_ge(a_taken, a_before(MIX0, MIX0.index(("ga", 0))) + 1)
                    pe.wait_ge(b_taken, b_before(MIX0, MIX0.index(("ka", 1)) + 1))
                    for tt in range(TT):
                        ins = mm(ps[:, B_G + tt // 2, (tt % 2) * 256:(tt % 2) * 256 + GH * GK],
                                 gaT[:, tt * P:(tt + 1) * P], wg2_sb[:, :], start=True, stop=True)
                    ins.then_inc(g_z, 1)
                elif name == "gs":
                    pe.wait_ge(g_log, 1)
                    for tt in range(TT):
                        ins = mm(ps[:, B_G + tt // 2, (tt % 2) * 256:(tt % 2) * 256 + GH * GK], tri16[:, :],
                                 gL[:, tt * GH * GK:(tt + 1) * GH * GK], start=True, stop=True)
                    ins.then_inc(g_sum, 1)
                elif name == "gd":
                    pe.wait_ge(g_exp, 1)
                    for tt in range(TT):
                        for p in range(GH // 2):
                            col = p * NCH + 2 * tt
                            ins = mm(ps[:, B_G, col:col + 2], gL[:, tt * GH * GK + p * P:tt * GH * GK + (p + 1) * P],
                                     ind16[:, :], start=True, stop=True)
                    ins.then_inc(g_total, 1)
                elif name == "gkv":
                    pe.wait_ge(g_kd, 1)
                    pe.wait_ge(b_taken, B_MIX0)
                    if i:
                        pe.wait_ge(g_state, NCH * i)
                    for h in (2 * i, 2 * i + 1):
                        for c in range(NCH):
                            tok = slice(CHUNK * (c % 2), CHUNK * (c % 2) + CHUNK)
                            ins = mm(ps[GK * (h % 2):GK * (h % 2) + GK, B_G + c % 2, (c // 2) * GV:(c // 2 + 1) * GV],
                                     ka[tok, c // 2, h * GK:(h + 1) * GK], va[tok, c // 2, h * GV:(h + 1) * GV],
                                     start=True, stop=True)
                    ins.then_inc(g_kv, 1)
                elif name == "go":
                    pe.wait_ge(a_taken, a_before(MIX0, MIX0.index(("qa", 1))) + 1)
                    pe.wait_ge(g_state, 2 * NCH)
                    if i:
                        pe.wait_ge(g_ocopy, i)
                    for h in (2 * i, 2 * i + 1):
                        rows = slice(GK * (h % 2), GK * (h % 2) + GK)
                        for c in range(NCH):
                            ins = mm(ps[:, B_G + h % 2, c * CHUNK:(c + 1) * CHUNK], st[i][rows, c, :],
                                     qaT[rows, i, c * CHUNK:(c + 1) * CHUNK], start=True, stop=True)
                    ins.then_inc(g_o, 1)
                elif name == "gn":
                    pe.wait_ge(g_osq, i + 1)
                    pe.wait_ge(g_ocopy, 2)
                    if i:
                        pe.wait_ge(g_lnv, i)
                    for a in range(2):
                        ins = mm(ps[:, B_G + a, :], ones[:, :], gq[i][:, a, :], start=True, stop=True)
                    ins.then_inc(g_osum, 1)
                elif name == "out":
                    if is_first(SEQ0, at):
                        pe.wait_ge(a_taken, A_MIX0 - 1 + i)

                    def ready(k):
                        pe.wait_ge(*((gla_lo_ready, k + 1) if k < GH else (oc_lo_ready, k - GH + 1)))
                    out_blocks(MIX0, U_OUT0, i, span, is_first(SEQ0, at), is_last(SEQ0, at), oc_hi, oc_lo, ready)
            out_tiles(MIX0, U_OUT0, 0, oc_hi, oc_lo)
            ffn(0, 1, U_UP0, U_DN0, KC)

            for at, (name, i, span) in enumerate(SEQ1):
                if name == "unit":
                    n, part = MIX1[i]
                    a = a_before(MIX1, i)
                    if n == "v":
                        b_unit(U_MIX1 + i, part, B_PARTS[n], B_SC, CKV * CD, span)
                    else:
                        if a >= 2 and span[0] == 0:
                            pe.wait_ge(a_taken, A_MIX0 + a - 1)
                        a_unit(U_MIX1 + i, U_MIX1 + i, a % 2, 2 * KC if i == 0 else None, span)
                elif name == "ssq":
                    ssq_mm(2)
                elif name == "rinv":
                    rinv_mm(2)
                elif name == "s":
                    g, hh = i // 2, i % 2
                    rows = slice(CD * hh, CD * hh + CD)
                    pe.wait_ge(a_taken, A_MIX0 + 2 + 2 * g + 2)
                    pe.wait_ge(c_pad, 2)
                    pe.wait_ge(b_taken, B_MIX0 + TT)
                    pe.wait_ge(c_bias, i)
                    for c in range(NCH):
                        ins = mm(ps[:, B_SC + c // 4, (c % 4) * P:(c % 4 + 1) * P],
                                 q1[rows, g, c, :, :].rearrange("k e q -> k (e q)"),
                                 k1[rows, g // 2, c * CHUNK:c * CHUNK + P], start=True, stop=True)
                    ins.then_inc(c_s, 1)
                elif name == "t":
                    pe.wait_ge(c_p, i + 1)
                    pe.wait_ge(c_tc, i)
                    for c in range(NCH):
                        ins = nc.tensor.transpose(ps[:, B_T + c // 4, (c % 4) * P:(c % 4 + 1) * P],
                                                  prs[i % 2][:, c, :], ident[:, :])
                    ins.then_inc(c_t, 1)
                elif name == "o":
                    g, hh = i // 2, i % 2
                    kv = 2 * (g // 2) + hh
                    pe.wait_ge(c_tc, i + 1)
                    pe.wait_ge(o1_lo_ready, g)
                    for sem_v in vs_loaded:
                        pe.wait_ge(sem_v, 16)
                    for c in range(NCH):
                        vals = v1 if c % 2 else v1s
                        ins = mm(ps[CD * hh:CD * hh + CD, B_PV + c // 4, (c % 4) * P:(c % 4 + 1) * P],
                                 vals[:, c // 2, kv * CD:(kv + 1) * CD], prT[:, c, :], start=True, stop=True)
                    ins.then_inc(c_pv, 1)
                elif name == "out":
                    if is_first(SEQ1, at):
                        pe.wait_ge(a_taken, A_MIX0 + a_before(MIX1, N1) - 1 + i)

                    def ready(k):
                        pe.wait_ge(o1_lo_ready, k // 2 + 1)
                    out_blocks(MIX1, U_OUT1, i, span, is_first(SEQ1, at), is_last(SEQ1, at), o1_hi, o1_lo, ready)
            out_tiles(MIX1, U_OUT1, 2 * KC, o1_hi, o1_lo)
            ffn(1, 3, U_UP1, U_DN1, 3 * KC)
            ssq_mm(2 * LAYERS)
            rinv_mm(2 * LAYERS)


def t5_bucket(rel):
    buckets, far = 32, 128
    nb = buckets // 2
    exact = nb // 2
    n = np.abs(rel)
    large = exact + (np.log(np.maximum(n, 1) / exact) / np.log(far / exact) * (nb - exact)).astype(np.int32)
    return (np.where(rel > 0, nb, 0) + np.where(n < exact, n, np.minimum(large, nb - 1))).astype(np.int32)


def stationary(w):
    k, n = w.shape
    return w.reshape(k // P, P, n // P, P).transpose(2, 1, 0, 3).reshape(n // P, P, k)


def moving(w):
    k, n = w.shape
    per = UC // n
    return w.reshape(k // (P * per), per, P, n).transpose(0, 2, 1, 3).reshape(-1, P, UC)


def columns(a):
    a = np.asarray(a)
    return np.moveaxis(a.reshape(*a.shape[:-1], a.shape[-1] // P, P), -1, 0).reshape(P, -1)


def kernel(x, norm_mix, norm_ffn, norm_final, ab_w_in, ab_w_gate2, ab_b_gate, ab_gla_norm, ab_w_out,
           c_w_qkv, c_sinks, c_w_out, rel_bias, ffn_w_up, ffn_conv_w, ffn_conv_b, ffn_w_down):
    import concourse.bacc as bacc
    from concourse.bass_utils import run_bass_kernel_spmd

    f = [np.asarray(a) for a in (x, norm_mix, norm_ffn, norm_final, ab_w_in, ab_w_gate2, ab_b_gate, ab_gla_norm,
                                 ab_w_out, c_w_qkv, c_sinks, c_w_out, rel_bias, ffn_w_up, ffn_conv_w, ffn_conv_b,
                                 ffn_w_down)]
    (x, norm_mix, norm_ffn, norm_final, w_in, w_gate2, b_gate, gla_norm, w_out0, w_qkv, sinks, w_out1,
     rel_bias, w_up, conv_w, conv_b, w_down) = f

    sizes = [GH * GK, GH * GK, GH * GV, GH * GV, RANK, SH * SD, SH * SD, SH * SD]
    qa, ka, va, ra, ga, qb, kb, vb = np.split(w_in[0], np.cumsum(sizes)[:-1], axis=1)
    ga = np.concatenate([ga, np.zeros((D, P - RANK), ga.dtype)], axis=1)
    parts = {"qa": stationary(qa), "ra": stationary(ra), "ga": stationary(ga), "qb": stationary(qb),
             "kb": stationary(kb), "ka": moving(ka), "va": moving(va), "vb": moving(vb)}
    w_mix0 = np.concatenate([np.stack([parts[n][i] for n, i in MIX0]), stationary(w_out0[0])])

    q_heads = [h for a in range(4) for h in (a, 4 + a)] + [h for a in range(4) for h in (8 + a, 12 + a)]
    wq, wk, wv = np.split(w_qkv[0], [CH * CD, CH * CD + CKV * CD], axis=1)
    wq = wq.reshape(D, CH, CD)[:, q_heads].reshape(D, CH * CD)
    parts = {"q": stationary(wq), "k": stationary(wk), "v": moving(wv)}
    wo = w_out1[0].reshape(CH, CD, D)[q_heads].reshape(CH * CD, D)
    w_mix1 = np.concatenate([np.stack([parts[n][i] for n, i in MIX1]), stationary(wo)])

    turns = [t for i in range(FC) for t in (i, FC + i)]
    up = np.concatenate([stationary(w_up[layer])[turns] for layer in range(LAYERS)])
    down = np.concatenate([stationary(w_down[layer]) for layer in range(LAYERS)])
    conv = np.concatenate([conv_w, conv_b[:, None]], axis=1)
    conv = conv.reshape(LAYERS, 4, UP, P)[:, :, turns].transpose(3, 0, 2, 1).reshape(P, -1)

    pairs = [8 * (n // 4) + 4 * (n % 2) + 2 * ((n // 2) % 2) for n in range(CH // 2)]
    sink_cols = np.stack([np.repeat(sinks[0, [h, h + 1]], CHUNK) for h in pairs], axis=1)
    rel = np.arange(2 * CHUNK)[None, :] - (CHUNK + np.arange(CHUNK)[:, None])
    by_head = rel_bias[t5_bucket(rel)]
    bias = np.stack([np.concatenate([by_head[:, :, h], by_head[:, :, h + 1]]) for h in pairs], axis=1).reshape(P, -1)

    gains = np.concatenate([columns(norm_mix[0]), columns(norm_ffn[0]), columns(norm_mix[1]),
                            columns(norm_ffn[1]), columns(norm_final)], axis=1)
    small = np.concatenate([gains, columns(gla_norm[0]), conv, sink_cols], axis=1)
    arrays = {
        "xT": columns_of_tokens(x[0]),
        "w_mix0": w_mix0, "w_mix1": w_mix1, "w_up": up, "w_down": down, "small": small,
        "wg2": np.concatenate([w_gate2[0], b_gate]), "bias": bias,
    }
    arrays = {n: np.ascontiguousarray(a) for n, a in arrays.items()}

    nc = bacc.Bacc("TRN2", target_bir_lowering=False, num_devices=1)
    aps = {n: nc.dram_tensor(n, a.shape, F32, kind="ExternalInput").ap() for n, a in arrays.items()}
    out = nc.dram_tensor("out", (P, KC * T), F32, kind="ExternalOutput").ap()
    trunk(nc, *aps.values(), out)
    got = run_bass_kernel_spmd(nc, [arrays], core_ids=[0]).results[0]["out"]
    return np.ascontiguousarray(got.reshape(P, KC, T).transpose(2, 1, 0).reshape(1, T, D))


def columns_of_tokens(a):
    return a.T.reshape(KC, P, T).transpose(1, 0, 2).reshape(P, KC * T)
```

```python
from contextlib import ExitStack

import numpy as np

import concourse.bass as bass
from concourse import mybir

F32 = mybir.dt.float32
F32R = mybir.dt.float32r
BF16 = mybir.dt.bfloat16
ACT = mybir.ActivationFunctionType
ALU = mybir.AluOpType
AX = mybir.AxisListType

P = 128
T = 512
D = 1024
KC = D // P
TT = T // P
LAYERS = 2
CHUNK = 64
NCH = T // CHUNK
GH, GK, GV = 4, 64, 128
RANK = 16
TAU = 16.0
SH, SD = 8, 64
CH, CKV, CD = 16, 4, 64
DFF = 2816
FC = DFF // P
EPS = 1e-6
NEG = -1e30
RAW = 4
SPL = 2
UC = KC * P

MIX0 = ([("qb", 0), ("kb", 0)] + [("vb", i) for i in range(4)]
        + [("qb", 1), ("kb", 1), ("kg", 0), ("kg", 1), ("kg", 2), ("qb", 2), ("kb", 2), ("qb", 3)]
        + [("va", i) for i in range(4)] + [("kb", 3), ("qa", 0), ("qa", 1)] + [("ra", i) for i in range(4)])
KG = GH * GK + RANK
N0 = len(MIX0)
MIX1 = [("k", 0), ("q", 0), ("q", 1), ("k", 1)] + [("q", i) for i in range(2, 7)] + [("v", 0), ("v", 1), ("q", 7)]
N1 = len(MIX1)
UP = 2 * FC
DRAIN = 3
DN = (6, 6, 5, 5)
DOFF = (0, 6, 12, 17)
U_OUT0 = N0
U_UP0 = U_OUT0 + KC
U_DN0 = U_UP0 + UP
U_MIX1 = U_DN0 + 4 * KC
U_OUT1 = U_MIX1 + N1
U_UP1 = U_OUT1 + KC
U_DN1 = U_UP1 + UP
U_END = U_DN1 + 4 * KC

def parts_of(units):
    return [("unit", u, (q, q + 1)) for u in units for q in range(8)]


def joined(seq):
    out = []
    for step in seq:
        if out and step[0] == "unit" == out[-1][0] and step[1] == out[-1][1]:
            out[-1] = ("unit", step[1], (out[-1][2][0], step[2][1]))
        else:
            out.append(step)
    return out


SB_PARTS = ((4,), (5, 2, 2, 2, 8), (3, 2, 5, 2, 8), (8, 2, 0, 2, 8), (5, 2, 2, 3, 8), (2, 1, 1, 7, 8),
            (3, 5, 0, 3, 9), (5, 3, 2, 2, 8), (9,))
GLA_AT = ((42, "gt", 0), (45, "gz", 0), (49, "gz_v", 0), (56, "gs", 0), (60, "gd", 0), (62, "gd_v", 0),
          (98, "gkv", 0), (100, "gkv_v", 0), (112, "gkv", 1), (116, "gkv_v", 1), (123, "go", 0),
          (128, "go_v", 0), (131, "go", 1), (131, "go_v", 1), (134, "gn", 0), (137, "silu", 0),
          (139, "gn_v", 0), (140, "gn", 1), (150, "gout", 0), (152, "gn_v", 1), (152, "silu", 1),
          (152, "gout", 1))


def mix0_order():
    def unit(name, i=0):
        return parts_of([MIX0.index((name, i))])

    def ev(name, i=0):
        return [(name, i, None)]

    def cut(name, i, *steps):
        parts, at = [], 0
        for q, step in zip(steps[::2], steps[1::2]):
            parts += unit(name, i)[at:q] + ev(step)
            at = q
        return parts + unit(name, i)[at:]

    q, k = unit("qb"), unit("kb")
    seq = q[:4] + k[:4] + ev("sq", 0) + q[4:] + ev("sq", 1) + k[4:]
    seq += unit("vb", 0) + ev("ssq") + cut("vb", 1, 6, "rinv")
    seq += cut("vb", 2, 4, "z", 6, "z_exp") + ev("z_ln") + cut("vb", 3, 4, "z_soft")
    fill = sum((parts_of([u]) for u in range(6, N0)), [])
    for at, name, i in reversed(GLA_AT):
        fill[at:at] = ev(name, i)

    def take(n):
        got = []
        while fill and (n or fill[0][0] != "unit"):
            n -= fill[0][0] == "unit"
            got.append(fill.pop(0))
        return got

    seq += take(SB_PARTS[0][0]) + ev("sfx")
    for h in range(1, SH):
        before, to_exp, to_ln, to_soft, to_sfx = SB_PARTS[h]
        seq += take(before) + ev("z", h) + ev("pv", h - 1) + take(to_exp) + ev("z_exp", h) + take(to_ln) + ev("z_ln", h)
        seq += take(to_soft) + ev("z_soft", h) + take(to_sfx) + ev("sfx", h)
    seq += take(SB_PARTS[SH][0]) + ev("pv", SH - 1) + take(len(fill))
    seq = with_splits(seq)
    seq += [("out", 0, (4, 5, 6)), ("out", 1, (4, 5, 6)), ("out", 0, (7,)), ("out", 1, (7,)),
            ("out", 0, (0, 1, 2, 3)), ("out", 1, (0, 1, 2, 3))]
    return joined(seq)


def with_splits(seq):
    out = []
    for step in seq:
        out.append(step)
        if step[0] == "unit" and step[2][1] == 8:
            out.append(("split", step[1], None))
    return out


SW_SPLIT = (4, 4, 4, 4, 4, 4, 4, 4, 4)
SW_PARTS = ((2, 2, 1, 8), (0, 2, 1, 9), (0, 2, 1, 6), (0, 2, 1, 6), (0, 2, 1, 7), (0, 2, 1, 6), (4, 2))


def mix1_order():
    def ev(name, i=0):
        return [(name, i, None)]

    def whole(u):
        return parts_of([u]) + ev("split", u)

    seq = whole(0) + ev("ssq") + whole(1) + parts_of([2])[:3] + ev("rinv") + parts_of([2])[3:]
    fill = []
    for u in range(3, N1):
        fill += parts_of([u])[:SW_SPLIT[u - 3]] + ev("split", u - 1) + parts_of([u])[SW_SPLIT[u - 3]:]
    fill += ev("split", N1 - 1)

    def take(n):
        got = []
        while fill and (n or fill[0][0] != "unit"):
            n -= fill[0][0] == "unit"
            got.append(fill.pop(0))
        return got

    for n in range(6):
        before, to_t, to_exp, to_norm = SW_PARTS[n]
        seq += take(before) + ev("s", n) + take(to_t) + (ev("t", n - 1) if n else []) + take(to_exp) + ev("s_exp", n)
        seq += take(to_norm) + ev("s_norm", n)
    seq += take(SW_PARTS[6][0]) + ev("t", 5) + take(SW_PARTS[6][1]) + ev("o", 0) + ev("o", 1) + take(len(fill))
    seq += ev("o", 2) + ev("s", 6) + ev("o", 3) + ev("s_exp", 6) + ev("s", 7)
    seq += [("out", 0, (0, 1)), ("out", 1, (0, 1))] + ev("s_norm", 6) + ev("o", 4) + ev("o", 5) + ev("s_exp", 7)
    seq += [("out", 0, (2, 3))] + ev("t", 6) + [("out", 0, (4, 5))] + ev("s_norm", 7) + ev("o", 6) + ev("t", 7)
    seq += [("out", 1, (2, 3))] + ev("o", 7) + [("out", 1, (4, 5))]
    return joined(seq + [("out", 0, (6, 7)), ("out", 1, (6, 7))])


SEQ0, SEQ1 = mix0_order(), mix1_order()


S_GAIN = 0
S_GLA = S_GAIN + 5 * KC
S_CONV = S_GLA + GH
S_SINK = S_CONV + LAYERS * UP * 4
S_END = S_SINK + CH // 2

ZOFF = (0, 512, 1024, 896)
ZW = (512, 384, 256, 128)
ZN = 1280


def trunk(nc, xT, w_mix0, w_mix1, w_up, w_down, small, wg2, bias, out):
    ctx = ExitStack()
    with ctx:
        def sb(name, shape, dt=F32, where=ctx):
            return where.enter_context(nc.sbuf_tensor(name, shape, dt))

        def sem(name):
            return ctx.enter_context(nc.semaphore(name))

        x = sb("x", [P, KC, T])
        h_hi = sb("h_hi", [P, KC, T], F32R)
        h_lo = sb("h_lo", [P, KC, T], F32R)
        w_raw = [sb(f"w_raw{r}", [P, UC]) for r in range(RAW)]
        w_hi = [sb(f"w_hi{s}", [P, UC], F32R) for s in range(SPL)]
        w_lo = [sb(f"w_lo{s}", [P, UC], F32R) for s in range(SPL)]
        par = sb("par", [P, S_END])
        rinv = sb("rinv", [P, T])
        rinv_col = sb("rinv_col", [P, TT])
        var_col = sb("var_col", [P, TT])
        mhalf = sb("mhalf", [P, TT])
        eps_col = sb("eps_col", [P, 1])
        gelu_warm = sb("gelu_warm", [P, 1])
        ssq = sb("ssq", [P, T])
        sq = sb("sq", [P, T])
        ident = sb("ident", [P, P])
        ones = sb("ones", [P, P])
        diag = sq

        m0 = ExitStack()

        def s0(name, shape, dt=F32):
            return sb(name, shape, dt, m0)

        ident_bf = s0("ident_bf", [P, P], BF16)
        negmask = s0("negmask", [P, P], BF16)
        negtri = s0("negtri", [P, P], F32R)
        negones = s0("negones", [P, P], F32R)
        tri_f = s0("tri_f", [P, P])
        tri16 = s0("tri16", [P, P])
        ind16 = s0("ind16", [P, 2])
        raT = s0("raT", [P, GH, T])
        qbT = s0("qbT", [P, SH // 2, T])
        kbT = s0("kbT", [P, SH // 2, T])
        vb = s0("vb", [P, TT, SH * SD])
        va = s0("va", [P, TT, GH * GV])
        kg = s0("kg", [P, TT, KG])
        qaT = s0("qaT", [P, GH // 2, T])
        gaT = s0("gaT", [RANK + 1, T])
        wg2_sb = s0("wg2_sb", [RANK + 1, GH * GK])
        sbE = s0("sbE", [P, ZN])
        sbS = s0("sbS", [P, ZN])
        sbH = s0("sbH", [P, ZN], F32R)
        sbL = s0("sbL", [P, ZN], F32R)
        gE = s0("gE", [P, TT * GH * GK])
        gL = s0("gL", [P, TT * GH * GK])
        sq0 = [b[:, c, :] for b in (va, raT) for c in range(4)]
        dec = s0("dec", [P, GH // 2, NCH])
        oc_hi = s0("oc_hi", [P, KC, T], F32R)
        oc_lo = s0("oc_lo", [P, KC, T], F32R)
        m0.close()
        st = [b[:, 0:2, :].rearrange("p a t -> p (a t)").rearrange("p (c v) -> p c v", c=NCH)
              for b in (qbT, kbT)]
        oF = va
        gq = [b[:, :].rearrange("p (a t) -> p a t", a=2) for b in (gE, gL)]

        m1 = ExitStack()

        def s1(name, shape, dt=F32):
            return sb(name, shape, dt, m1)

        q1 = s1("q1", [P, KC // 2, NCH, 2, CHUNK])
        k1 = s1("k1", [P, 2, CHUNK + T])
        v1 = s1("v1", [P, TT, CKV * CD])
        v1s = s1("v1s", [P, TT, CKV * CD])
        bias_sb = s1("bias_sb", [P, CH // 2, P])
        scs = [s1(f"sc{k}", [P, NCH, P]) for k in range(2)]
        prs = [s1(f"pr{k}", [P, NCH, P]) for k in range(2)]
        prTs = [s1(f"prT{n}", [P, NCH, P]) for n in range(CH // 2)]
        mx = s1("mx", [P, NCH])
        nms = [s1(f"nm{k}", [P, NCH]) for k in range(2)]
        rss = [s1(f"rs{k}", [P, NCH]) for k in range(2)]
        ess = [s1(f"es{k}", [P, NCH]) for k in range(2)]
        den = s1("den", [P, NCH])
        rd = s1("rd", [P, NCH])
        o1_hi = s1("o1_hi", [P, KC, T], F32R)
        o1_lo = s1("o1_lo", [P, KC, T], F32R)
        m1.close()

        y_hi = sb("y_hi", [P, FC, T], F32R)
        y_lo = sb("y_lo", [P, FC, T], F32R)
        us = [sb(f"us{k}", [P, 2 + T]) for k in range(2)]
        cv = [sb(f"cv{k}", [P, T]) for k in range(4)]

        ps = ctx.enter_context(nc.psum_tensor("ps", [P, 8, T], F32))
        zs = ps[:, 4:7, :].rearrange("p b t -> p (b t)")
        B_O = 7
        B_RES = 4
        B_G = 2
        B_Z = 4
        g_banks = ps[:, B_G:B_G + 2, :].rearrange("p b t -> p (b t)")
        B_SSQ, B_RINV = 6, 7
        B_SC, B_T, B_PV = 2, 4, 6

        w_loaded = [sem(f"w_loaded{r}") for r in range(RAW)]
        w_hi_ready = sem("w_hi_ready")
        w_lo_ready = sem("w_lo_ready")
        unit_done = sem("unit_done")
        x_loaded = [sem(f"x_loaded{i}") for i in range(4)]
        par_loaded = sem("par_loaded")
        wg2_loaded = sem("wg2_loaded")
        bias_loaded = sem("bias_loaded")
        consts = sem("consts")
        consts_dve = sem("consts_dve")
        sq_ready = sem("sq_ready")
        ssq_added = sem("ssq_added")
        hi_ready = sem("hi_ready")
        lo_ready = sem("lo_ready")
        x_updated = sem("x_updated")
        ssq_col = sem("ssq_col")
        var_ready = sem("var_ready")
        rcol_ready = sem("rcol_ready")
        diag_ready = sem("diag_ready")
        rbc_done = sem("rbc_done")
        rinv_ready = sem("rinv_ready")
        a_taken = sem("a_taken")
        b_taken = sem("b_taken")
        sb_z = sem("sb_z")
        sb_abs = sem("sb_abs")
        sb_e = sem("sb_e")
        sb_ln = sem("sb_ln")
        sb_sp = sem("sb_sp")
        sb_hi = sem("sb_hi")
        sb_lo = sem("sb_lo")
        sb_sum = sem("sb_sum")
        sb_w = sem("sb_w")
        sb_pv = sem("sb_pv")
        oc_hi_ready = sem("oc_hi_ready")
        oc_lo_ready = sem("oc_lo_ready")
        silu_done = sem("silu_done")
        g_t = sem("g_t")
        g_tcopy = sem("g_tcopy")
        g_z = sem("g_z")
        g_abs = sem("g_abs")
        g_e = sem("g_e")
        g_ln = sem("g_ln")
        g_log = sem("g_log")
        g_sum = sem("g_sum")
        g_total = sem("g_total")
        g_exp = sem("g_exp")
        g_kd = sem("g_kd")
        g_kv = sem("g_kv")
        g_state = sem("g_state")
        g_o = sem("g_o")
        g_ocopy = sem("g_ocopy")
        g_osq = sem("g_osq")
        g_osum = sem("g_osum")
        g_lnv = sem("g_lnv")
        g_rms = sem("g_rms")
        g_norm = sem("g_norm")
        g_out = sem("g_out")
        gla_hi_ready = sem("gla_hi_ready")
        gla_lo_ready = sem("gla_lo_ready")
        c_pad = sem("c_pad")
        vs_loaded = [sem(f"vs_loaded{i}") for i in range(2)]
        c_s = sem("c_s")
        c_bias = sem("c_bias")
        c_mask = sem("c_mask")
        c_mx = sem("c_mx")
        c_nm = sem("c_nm")
        c_exp = sem("c_exp")
        c_den = sem("c_den")
        c_rd = sem("c_rd")
        c_p = sem("c_p")
        c_t = sem("c_t")
        c_tc = sem("c_tc")
        c_pv = sem("c_pv")
        o1_hi_ready = sem("o1_hi_ready")
        o1_lo_ready = sem("o1_lo_ready")
        u_scaled = sem("u_scaled")
        u_mid = sem("u_mid")
        conv1 = sem("conv1")
        conv2 = sem("conv2")
        gelu_done = sem("gelu_done")
        y_mul = sem("y_mul")
        yhi_ready = sem("yhi_ready")
        ylo_ready = sem("ylo_ready")
        halo = sem("halo")
        warmed = sem("warmed")
        out_ready = sem("out_ready")
        out_written = sem("out_written")

        def gain_at(n, c):
            return par[:, bass.ds(S_GAIN + n * KC + c, 1)]

        def blk(t, c):
            return t[:, bass.ds(c, 1), :].rearrange("p o t -> p (o t)")

        B_PARTS = {"vb": 4, "va": 4, "kg": 3, "v": 2}
        B_COLS = {"vb": SH * SD, "va": GH * GV, "kg": KG, "v": CKV * CD}

        def a_before(units, u):
            return sum(n not in B_PARTS for n, _ in units[:u])

        def a_bank0(a):
            return B_Z + a if a < 2 else a % 2

        def a_bank1(a):
            return a % 2 + (B_T if a in (2, 3) else 0)

        def out_bank(c, units):
            return (a_before(units, len(units)) + c) % 2 if c < 2 else B_RES + c % 2

        def b_tile(tt, n_cols):
            return ps[:, tt, 0:n_cols]

        def v_tile(tt, n_cols):
            return ps[:, B_PV + tt // 2, (tt % 2) * n_cols:(tt % 2 + 1) * n_cols]

        def b_before(units, u):
            return TT * sum(n in B_PARTS and i == B_PARTS[n] - 1 for n, i in units[:u])


        def b_order(a):
            return (a % 2, 1 - a % 2, 2, 3)

        A_MIX0, B_MIX0 = a_before(MIX0, N0), b_before(MIX0, N0)
        N_CONSTS = 16
        WARM = 14
        NADD = KC + 1

        def x_pair(i):
            return xT[:, 2 * i * T:(2 * i + 2) * T].rearrange("p (c t) -> p c t", t=T)

        def o1_psum(b):
            return ps[:, B_PV + b, :].rearrange("p (c e q) -> p e c q", e=2, q=CHUNK)

        def o1_half(t, g, b):
            return t[:, 2 * g:2 * g + 2, b * T // 2:(b + 1) * T // 2].rearrange("p e (c q) -> p e c q", q=CHUNK)

        block = ctx.enter_context(nc.Block())

        @block.sync
        def _(sp):
            def unit(u, r, src, cols=UC):
                sp.wait_ge(w_lo_ready, u - (RAW - 1))
                sp.dma_start(w_raw[r][:, 0:cols], src).then_inc(w_loaded[r], 16)

            def one(t, i):
                return t[bass.ds(i, 1)].rearrange("o p c -> (o p) c")

            for u in range(RAW):
                sp.dma_start(w_raw[u][:, :], w_mix0[u]).then_inc(w_loaded[u], 16)
                if u < 2:
                    i = 3 * u
                    sp.dma_start(x[:, 2 * i:2 * i + 2, :], x_pair(i)).then_inc(x_loaded[i], 16)
            sp.dma_start(wg2_sb[:, :], wg2).then_inc(wg2_loaded, 16)
            with sp.Fori(1, U_UP0 // RAW) as i:
                for k in range(RAW):
                    unit(RAW * i + k, k, one(w_mix0, RAW * i + k))
            for u in range(U_UP0 // RAW * RAW, U_UP0):
                unit(u, u % RAW, w_mix0[u])

            def ffn(layer, u_up, u_dn):
                with sp.Fori(0, UP // RAW) as i:
                    for k in range(RAW):
                        unit(u_up + k + RAW * i, (u_up + k) % RAW, one(w_up, layer * UP + k + RAW * i))
                with sp.Fori(0, KC) as i:
                    for k in range(len(DN)):
                        src = w_down[bass.ds(layer * KC + i, 1), :, DOFF[k] * P:(DOFF[k] + DN[k]) * P]
                        unit(u_dn + k + RAW * i, (u_dn + k) % RAW,
                             src.rearrange("o p c -> (o p) c"), DN[k] * P)

            ffn(0, U_UP0, U_DN0)
            with sp.Fori(0, (N1 + KC) // RAW) as i:
                for k in range(RAW):
                    unit(U_MIX1 + k + RAW * i, (U_MIX1 + k) % RAW, one(w_mix1, k + RAW * i))
            ffn(1, U_UP1, U_DN1)
            for c in range(KC):
                sp.wait_ge(out_ready, c + 1)
                sp.dma_start(out[:, c * T:(c + 1) * T], x[:, c, :]).then_inc(out_written, 16)
            sp.wait_ge(out_written, 16 * KC)

        @block.gpsimd
        def _(pool):
            n = [0]

            def step(ins):
                ins.then_inc(consts, 1)
                n[0] += 1
                pool.wait_ge(consts, n[0])

            g = nc.gpsimd
            step(g.memset(mhalf[:, :], -0.5))
            step(g.memset(eps_col[:, :], EPS))
            step(g.memset(ones[:, :], 1.0))
            step(g.memset(ident[:, :], 0.0))
            step(g.affine_select(out=ident[:, :], in_=ident[:, :], compare_op=ALU.not_equal, fill=1.0,
                                 base=0, pattern=[[-1, P]], channel_multiplier=1))
            step(g.memset(gaT[:, :], 1.0))
            step(g.memset(negmask[:, :], NEG))
            step(g.affine_select(out=negmask[:, :], in_=negmask[:, :], compare_op=ALU.is_ge, fill=0.0,
                                 base=0, pattern=[[-1, P]], channel_multiplier=1))
            step(g.memset(tri_f[:, :], -1.0))
            step(g.affine_select(out=tri_f[:, :], in_=tri_f[:, :], compare_op=ALU.is_ge, fill=0.0,
                                 base=0, pattern=[[-1, P]], channel_multiplier=1))
            step(g.memset(tri16[:, :], 1.0 / TAU))
            step(g.affine_select(out=tri16[:, :], in_=tri16[:, :], compare_op=ALU.is_gt, fill=0.0,
                                 base=0, pattern=[[-1, P]], channel_multiplier=1))
            step(g.memset(tri16[CHUNK:P, 0:CHUNK], 0.0))
            step(g.memset(ind16[:, :], 0.0))
            step(g.memset(ind16[0:CHUNK, 0:1], 1.0 / TAU))
            step(g.memset(ind16[CHUNK:P, 1:2], 1.0 / TAU))
            assert n[0] == N_CONSTS

            for norm in range(2 * LAYERS + 1):
                pool.wait_ge(var_ready, norm + 1)
                g.tensor_tensor(rinv_col[:, :], var_col[:, :], mhalf[:, :], ALU.pow).then_inc(rcol_ready, 1)

        @block.scalar
        def _(act):
            s = nc.scalar

            def hi(u, gen, r, cols=UC):
                act.wait_ge(w_loaded[r], 16 * gen + 16)
                act.wait_ge(unit_done, u - (SPL - 1))
                s.activation(w_hi[r % SPL][:, 0:cols], w_raw[r][:, 0:cols], ACT.Copy).then_inc(w_hi_ready, 1)

            def hi_static(u, cols=UC):
                if u < U_END:
                    hi(u, u // RAW, u % RAW, cols)

            def norm_tile(norm, c, r, last=False):
                act.wait_ge(x_updated, r + 1)
                act.wait_ge(ssq_added, norm * NADD + 1 + c)
                if not last:
                    s.activation(blk(h_hi, c), blk(x, c), ACT.Copy, scale=gain_at(norm, c)).then_inc(hi_ready, 1)
                s.activation(sq[:, :], blk(x, c), ACT.Square).then_inc(sq_ready, 1)

            def rinv_copy(norm):
                act.wait_ge(rbc_done, norm + 1)
                s.activation(rinv[:, :], ps[:, B_RINV, :], ACT.Copy).then_inc(rinv_ready, 1)

            act.dma_start(par[:, :], small).then_inc(par_loaded, 16)
            for i in (1, 2):
                act.dma_start(x[:, 2 * i:2 * i + 2, :], x_pair(i)).then_inc(x_loaded[i], 16)

            for c in range(KC):
                if c % 4 == 0:
                    act.wait_ge(w_loaded[c // 4], 16)
                    s.activation(w_hi[c // 4][:, :], w_raw[c // 4][:, :], ACT.Copy).then_inc(w_hi_ready, 1)
                if c == 0:
                    act.wait_ge(par_loaded, 16)
                if c % 2 == 0:
                    act.wait_ge(x_loaded[c // 2], 16)
                s.activation(h_hi[:, c, :], x[:, c, :], ACT.Copy, scale=gain_at(0, c)).then_inc(hi_ready, 1)

            def b_evac(dst, n_cols, src, next_a=0):
                for tt in b_order(next_a):
                    s.activation(dst[:, tt, :], src(tt, n_cols), ACT.Copy,
                                 scale=rinv_col[:, tt:tt + 1]).then_inc(b_taken, 1)

            for name, i, span in SEQ0:
                if name == "unit" and span[1] == 8:
                    n, part = MIX0[i]
                    if n in B_PARTS and part == B_PARTS[n] - 1:
                        act.wait_ge(unit_done, i + 1)
                        b_evac({"vb": vb, "va": va, "kg": kg}[n], B_COLS[n], b_tile, a_before(MIX0, i))
                elif name == "split":
                    hi_static(i + SPL)
                elif name == "sq":
                    for c in range(4 * i, 4 * i + 4):
                        s.activation(sq0[c], x[:, c, :], ACT.Square).then_inc(sq_ready, 1)
                elif name == "rinv":
                    rinv_copy(0)
                elif name == "z":
                    act.wait_ge(sb_z, i + 1)
                    act.wait_ge(sb_sp, i)
                    s.activation(sbE[:, :], zs[:, 0:ZN], ACT.Abs).then_inc(sb_abs, 1)
                elif name == "z_exp":
                    act.wait_ge(sb_abs, i + 1)
                    s.activation(sbE[:, :], sbE[:, :], ACT.Exp, scale=-1.0).then_inc(sb_e, 1)
                elif name == "z_ln":
                    act.wait_ge(sb_e, i + 1)
                    s.activation(sbE[:, :], sbE[:, :], ACT.Ln, bias=1.0).then_inc(sb_ln, 1)
                elif name == "sfx":
                    act.wait_ge(sb_sum, i + 1)
                    s.activation(sbS[:, :], zs[:, 0:ZN], ACT.Exp).then_inc(sb_w, 1)
                elif name == "pv" and i % 2 == 1:
                    act.wait_ge(sb_pv, i + 1)
                    s.activation(oc_hi[:, GH + i // 2, :], ps[:, B_O, :], ACT.Copy).then_inc(oc_hi_ready, 1)
                elif name == "gz":
                    act.wait_ge(g_z, 1)
                    s.activation(gE[:, :], g_banks, ACT.Abs).then_inc(g_abs, 1)
                    act.wait_ge(g_abs, 1)
                    s.activation(gE[:, :], gE[:, :], ACT.Exp, scale=-1.0).then_inc(g_e, 1)
                    act.wait_ge(g_e, 1)
                    s.activation(gE[:, :], gE[:, :], ACT.Ln, bias=1.0).then_inc(g_ln, 1)
                elif name == "gs":
                    act.wait_ge(g_sum, 1)
                    s.activation(gE[:, :], g_banks, ACT.Exp).then_inc(g_exp, 1)
                elif name == "gd":
                    act.wait_ge(g_total, 1)
                    s.activation(dec[:, :, :].rearrange("p a c -> p (a c)"), ps[:, B_G, 0:2 * NCH], ACT.Exp).then_inc(g_exp, 1)
                elif name == "go":
                    act.wait_ge(g_o, i + 1)
                    s.activation(oF[:, 2 * i:2 * i + 2, :].rearrange("p a t -> p (a t)"), g_banks, ACT.Copy).then_inc(g_ocopy, 1)
                elif name == "gn":
                    act.wait_ge(g_osum, i + 1)
                    act.wait_ge(consts, 2)
                    s.activation(gq[i].rearrange("p a t -> p (a t)"), g_banks, ACT.Ln, scale=1.0 / GV,
                                 bias=eps_col[:, 0:1]).then_inc(g_lnv, 1)
                    act.wait_ge(g_lnv, i + 1)
                    s.activation(gq[i], gq[i], ACT.Exp, scale=-0.5).then_inc(g_rms, 1)
                elif name == "silu":
                    act.wait_ge(a_taken, a_before(MIX0, MIX0.index(("ra", 2 * i + 1))) + 1)
                    s.activation(raT[:, 2 * i:2 * i + 2, :], raT[:, 2 * i:2 * i + 2, :], ACT.Silu).then_inc(silu_done, 1)
                elif name == "gout":
                    for h in (2 * i, 2 * i + 1):
                        act.wait_ge(g_out, h + 1)
                        s.activation(oc_hi[:, h, :], oF[:, h, :], ACT.Copy).then_inc(gla_hi_ready, 1)

            def w_out(norm, u0, r0):
                for c in range(KC):
                    hi_static(u0 + c + SPL)
                    norm_tile(norm, c, r0 + c)

            def ffn(layer, norm, u_up, u_dn, r0, next_cols, last):
                act.wait_ge(warmed, layer)
                s.activation(gelu_warm[:, :], par[:, 0:1], ACT.Gelu_apprx_tanh).then_inc(warmed, 1)

                def up_hi(i, k, cols=UC):
                    hi(u_up + k + SPL + 4 * i, (u_up + k + SPL) // RAW + i, (u_up + k + SPL) % RAW, cols)

                def mid(i, k):
                    m, pair = layer * UP + k + 4 * i, layer * FC + k // 2 + 2 * i
                    taps = S_CONV + (layer * UP + k) * 4 + 16 * i
                    if k >= 4 or not isinstance(i, int) or pair >= 2:
                        act.wait_ge(ylo_ready if k % 2 else y_mul, pair - 1)
                    act.wait_ge(u_scaled, m + 1)
                    s.activation(cv[k % 4][:, :], us[k % 2][:, 2:2 + T], ACT.Identity,
                                 bias=par[:, bass.ds(taps + 3, 1)],
                                 scale=par[:, bass.ds(taps + 2, 1)]).then_inc(u_mid, 1)

                def gelu(i, k):
                    act.wait_ge(conv2, layer * UP + k + 4 * i + 1)
                    s.activation(cv[k % 4][:, :], cv[k % 4][:, :], ACT.Gelu_apprx_tanh).then_inc(gelu_done, 1)

                def y_hi_part(i, k):
                    act.wait_ge(y_mul, layer * FC + k // 2 + 2 * i + 1)
                    s.activation(blk(y_hi, k // 2 + 2 * i), cv[(k + 1) % 4][:, :], ACT.Copy).then_inc(yhi_ready, 1)

                def later_stages(i, k):
                    static = isinstance(i, int)
                    if k % 2 == 0 and not (static and 4 * i + k < 2) and not (static and 4 * i + k > UP):
                        gelu(i, k - 2)
                    if k % 2 == 0 and not (static and 4 * i + k < 4):
                        y_hi_part(i, k - 4)

                up_hi(0, 0)
                up_hi(0, 1)
                rinv_copy(norm)
                mid(0, 0)
                mid(0, 1)
                for k in (2, 3):
                    up_hi(0, k)
                    mid(0, k)
                    later_stages(0, k)
                with act.Fori(1, UP // 4 - 1) as i:
                    for k in range(4):
                        up_hi(i, k)
                        mid(i, k)
                        later_stages(i, k)
                for k in range(4):
                    up_hi(UP // 4 - 1, k, UC if k < 4 - SPL else DN[k - 4 + SPL] * P)
                    mid(UP // 4 - 1, k)
                    later_stages(UP // 4 - 1, k)
                def down_hi(i, kk, cols):
                    hi(u_dn + kk + SPL + 8 * i, (u_dn + kk + SPL) // RAW + 2 * i, (u_dn + kk + SPL) % RAW, cols)

                for k in range(4, 4 + DRAIN):
                    if k == 3 + DRAIN:
                        down_hi(0, 0, DN[SPL] * P)
                    later_stages(UP // 4 - 1, k)

                def down_pair(i, final):
                    for kk in range(1, 9):
                        if not final or kk + SPL < 8:
                            down_hi(i, kk, DN[(kk + SPL) % 4] * P)
                        elif next_cols is not None and kk < 8:
                            down_hi(i, kk, next_cols[kk + SPL - 8])
                        if kk in (3, 7):
                            norm_tile(norm + 1, kk // 4 + 2 * i, r0 + kk // 4 + 2 * i, last)

                with act.Fori(0, KC // 2 - 1) as i:
                    down_pair(i, False)
                down_pair(KC // 2 - 1, True)

            w_out(1, U_OUT0, 0)
            ffn(0, 1, U_UP0, U_DN0, KC, [UC] * SPL, False)

            for name, i, span in SEQ1:
                if name == "split":
                    hi_static(U_MIX1 + i + SPL)
                elif name == "unit" and span[1] == 8:
                    if i == 0:
                        act.dma_start(bias_sb[:, :, :], bias.rearrange("p (n k) -> p n k", k=P)).then_inc(bias_loaded, 16)
                    if MIX1[i] == ("v", 1):
                        act.wait_ge(unit_done, U_MIX1 + i + 1)
                        b_evac(v1, CKV * CD, v_tile)
                        act.wait_ge(b_taken, B_MIX0 + TT)
                        act.dma_start(v1s[0:CHUNK, 1:TT, :], v1[CHUNK:P, 0:TT - 1, :]).then_inc(vs_loaded[0], 16)
                        act.dma_start(v1s[CHUNK:P, :, :], v1[0:CHUNK, :, :]).then_inc(vs_loaded[1], 16)
                elif name == "rinv":
                    rinv_copy(2)
                elif name == "s_exp":
                    sc, pr, nm, rs, es = (t[i % 2] for t in (scs, prs, nms, rss, ess))
                    act.wait_ge(c_nm, i + 1)
                    if i >= 2:
                        act.wait_ge(c_den, i - 1)
                        act.wait_ge(c_t, i - 1)
                    s.activation(es[:, :], nm[:, :], ACT.Exp, bias=par[:, S_SINK + i:S_SINK + i + 1])
                    for c in range(NCH):
                        ins = s.activation(pr[:, c, :], sc[:, c, :], ACT.Exp, bias=nm[:, c:c + 1],
                                           accum_out=rs[:, c:c + 1])
                    ins.then_inc(c_exp, 1)
                elif name == "t":
                    act.wait_ge(c_t, i + 1)
                    s.activation(prTs[i][:, :, :].rearrange("p c k -> p (c k)"),
                                 ps[:, B_T:B_T + 2, :].rearrange("p b t -> p (b t)"), ACT.Copy).then_inc(c_tc, 1)
                elif name == "o" and i % 2 == 1:
                    act.wait_ge(c_pv, i + 1)
                    for b in range(2):
                        s.activation(o1_half(o1_hi, i // 2, b), o1_psum(b), ACT.Copy).then_inc(o1_hi_ready, 1)
            w_out(3, U_OUT1, 2 * KC)
            ffn(1, 3, U_UP1, U_DN1, 3 * KC, None, True)

        @block.vector
        def _(dve):
            v = nc.vector

            def lo(u, r, cols=UC):
                dve.wait_ge(w_hi_ready, u + 1)
                v.tensor_tensor(w_lo[r % SPL][:, 0:cols], w_raw[r][:, 0:cols],
                                w_hi[r % SPL][:, 0:cols].bitcast(F32), ALU.subtract).then_inc(w_lo_ready, 1)

            def lo_static(u, cols=UC):
                lo(u, u % RAW, cols)

            def add_sq(norm, c, squares=sq[:, :]):
                dve.wait_ge(sq_ready, norm * KC + 1 + c)
                dve.wait_ge(ssq_added, norm * NADD + 1 + c)
                v.tensor_tensor(ssq[:, :], ssq[:, :], squares, ALU.add).then_inc(ssq_added, 1)

            def h_lo_part(norm, c):
                dve.wait_ge(hi_ready, norm * KC + 1 + c)
                v.scalar_tensor_tensor(blk(h_lo, c), blk(x, c), gain_at(norm, c),
                                       blk(h_hi, c).bitcast(F32), ALU.mult, ALU.subtract).then_inc(lo_ready, 1)

            def res_add(c, bank, units):
                dve.wait_ge(unit_done, units)
                v.tensor_tensor(blk(x, c), ps[:, bank, :], blk(x, c), ALU.add).then_inc(x_updated, 1)

            def res_split(norm, c, r, last=False):
                if not last:
                    dve.wait_ge(x_updated, r + 1)
                    h_lo_part(norm, c)
                add_sq(norm, c)

            def rms(norm):
                dve.wait_ge(ssq_col, norm + 1)
                v.tensor_scalar(var_col[:, :], ps[:, B_SSQ, 0:TT], 1.0 / D, EPS, ALU.mult, ALU.add).then_inc(var_ready, 1)
                if norm < 2 * LAYERS:
                    v.memset(ssq[:, :], 0.0).then_inc(ssq_added, 1)
                dve.wait_ge(rcol_ready, norm + 1)
                v.tensor_tensor(diag[:, :].rearrange("p (a t) -> p a t", a=TT),
                                ident[:, :].unsqueeze(1).broadcast_to([P, TT, P]),
                                rinv_col[:, :].unsqueeze(2).broadcast_to([P, TT, P]), ALU.mult).then_inc(diag_ready, 1)

            v.memset(ssq[:, :], 0.0).then_inc(ssq_added, 1)
            for c in range(KC):
                if c % 4 == 0:
                    lo_static(c // 4)
                h_lo_part(0, c)
            dve.wait_ge(consts, N_CONSTS)
            v.tensor_copy(ident_bf[:, :], ident[:, :]).then_inc(consts_dve, 1)
            v.tensor_copy(negtri[:, :], tri_f[:, :]).then_inc(consts_dve, 1)
            v.tensor_scalar(negones[:, :], ones[:, :], -1.0, None, ALU.mult).then_inc(consts_dve, 1)

            def a_evac0(u):
                (n, i), a = MIX0[u], a_before(MIX0, u)
                dve.wait_ge(unit_done, u + 1)
                src = ps[:, a_bank0(a), :]
                if n in ("ra", "kb"):
                    dst = (raT if n == "ra" else kbT)[:, i, :]
                    ins = v.tensor_tensor(dst, src, rinv[:, :], ALU.mult)
                else:
                    dst, width = (qbT, SD) if n == "qb" else (qaT, GK)
                    ins = v.scalar_tensor_tensor(dst[:, i, :], src, width ** -0.5, rinv[:, :], ALU.mult, ALU.mult)
                ins.then_inc(a_taken, 1)

            for name, i, span in SEQ0:
                if name == "unit" and span[1] == 8:
                    if i >= 2 and MIX0[i][0] not in B_PARTS:
                        a_evac0(i)
                elif name == "split":
                    lo_static(i + SPL)
                elif name == "sq":
                    for c in range(4 * i, 4 * i + 4):
                        add_sq(0, c, sq0[c])
                elif name == "ssq":
                    rms(0)
                elif name == "rinv":
                    dve.wait_ge(rinv_ready, 1)
                    a_evac0(0)
                    a_evac0(1)
                elif name == "z_soft":
                    dve.wait_ge(sb_ln, i + 1)
                    dve.wait_ge(sb_pv, i)
                    v.scalar_tensor_tensor(sbS[:, :], zs[:, 0:ZN], 0.0, sbE[:, :], ALU.max, ALU.add).then_inc(sb_sp, 1)
                    dve.wait_ge(sb_sp, i + 1)
                    v.tensor_copy(sbH[:, :], sbS[:, :]).then_inc(sb_hi, 1)
                    dve.wait_ge(sb_hi, i + 1)
                    v.tensor_tensor(sbL[:, :], sbS[:, :], sbH[:, :].bitcast(F32), ALU.subtract).then_inc(sb_lo, 1)
                elif name == "pv" and i % 2 == 1:
                    dve.wait_ge(oc_hi_ready, i // 2 + 1)
                    v.tensor_tensor(oc_lo[:, GH + i // 2, :], ps[:, B_O, :],
                                    oc_hi[:, GH + i // 2, :].bitcast(F32), ALU.subtract).then_inc(oc_lo_ready, 1)
                elif name == "gz":
                    dve.wait_ge(g_t, 1)
                    v.tensor_copy(gaT[0:RANK, :], ps[0:RANK, B_G, :]).then_inc(g_tcopy, 1)
                elif name == "gz_v":
                    dve.wait_ge(g_ln, 1)
                    v.scalar_tensor_tensor(gL[:, :], g_banks, 0.0, gE[:, :], ALU.min, ALU.subtract).then_inc(g_log, 1)
                elif name == "gd_v":
                    dve.wait_ge(g_exp, 1)
                    keys = kg[:, :, 0:GH * GK]
                    v.tensor_tensor(keys, gE[:, :].rearrange("p (a n) -> p a n", a=TT), keys, ALU.mult).then_inc(g_kd, 1)
                elif name == "gkv_v":
                    dve.wait_ge(g_kv, i + 1)
                    dve.wait_ge(g_exp, 2)
                    for c in range(NCH):
                        kv = ps[:, B_G + c % 2, (c // 2) * GV:(c // 2 + 1) * GV]
                        if c == 0:
                            v.tensor_copy(st[i][:, 0, :], kv).then_inc(g_state, 1)
                        else:
                            dve.wait_ge(g_state, NCH * i + c)
                            v.scalar_tensor_tensor(st[i][:, c, :], st[i][:, c - 1, :], dec[:, i, c:c + 1], kv,
                                                   ALU.mult, ALU.add).then_inc(g_state, 1)
                elif name == "go_v":
                    dve.wait_ge(g_ocopy, i + 1)
                    o_pair = oF[:, 2 * i:2 * i + 2, :]
                    v.tensor_tensor(gq[i], o_pair, o_pair, ALU.mult).then_inc(g_osq, 1)
                elif name == "gn_v":
                    dve.wait_ge(g_rms, i + 1)
                    o_pair = oF[:, 2 * i:2 * i + 2, :]
                    v.tensor_tensor(o_pair, o_pair, gq[i], ALU.mult).then_inc(g_norm, 1)
                elif name == "gout":
                    dve.wait_ge(g_norm, i + 1)
                    dve.wait_ge(silu_done, i + 1)
                    for h in (2 * i, 2 * i + 1):
                        v.scalar_tensor_tensor(oF[:, h, :], oF[:, h, :], par[:, S_GLA + h:S_GLA + h + 1],
                                               raT[:, h, :], ALU.mult, ALU.mult).then_inc(g_out, 1)
                    for h in (2 * i, 2 * i + 1):
                        dve.wait_ge(gla_hi_ready, h + 1)
                        v.tensor_tensor(oc_lo[:, h, :], oF[:, h, :], oc_hi[:, h, :].bitcast(F32),
                                        ALU.subtract).then_inc(gla_lo_ready, 1)

            def w_out(norm, u0, r0, units):
                for c in range(KC):
                    res_add(c, out_bank(c, units), u0 + c + 1)
                    lo_static(u0 + c + SPL)
                    res_split(norm, c, r0 + c)

            def ffn(layer, norm, u_up, u_dn, r0, next_cols, last):
                def up_lo(i, k, cols=UC):
                    lo(u_up + k + SPL + 4 * i, (u_up + k + SPL) % RAW, cols)

                def up_scale(i, k):
                    dve.wait_ge(unit_done, u_up + k + 1 + 4 * i)
                    if not isinstance(i, int) or 4 * i + k >= 2:
                        dve.wait_ge(conv2, layer * UP + k - 1 + 4 * i)
                    v.tensor_tensor(us[k % 2][:, 2:2 + T], ps[:, k, :], rinv[:, :], ALU.mult).then_inc(u_scaled, 1)

                def up_conv(i, k):
                    m = layer * UP + k + 4 * i
                    taps = S_CONV + (layer * UP + k) * 4 + 16 * i
                    dve.wait_ge(u_mid, m + 1)
                    v.scalar_tensor_tensor(cv[k % 4][:, :], us[k % 2][:, 1:1 + T], par[:, bass.ds(taps + 1, 1)],
                                           cv[k % 4][:, :], ALU.mult, ALU.add).then_inc(conv1, 1)
                    dve.wait_ge(conv1, m + 1)
                    v.scalar_tensor_tensor(cv[k % 4][:, :], us[k % 2][:, 0:T], par[:, bass.ds(taps, 1)],
                                           cv[k % 4][:, :], ALU.mult, ALU.add).then_inc(conv2, 1)

                def y_product(i, k):
                    dve.wait_ge(conv2, layer * UP + k + 4 * i + 2)
                    dve.wait_ge(gelu_done, layer * FC + k // 2 + 2 * i + 1)
                    v.tensor_tensor(cv[(k + 1) % 4][:, :], cv[(k + 1) % 4][:, :], cv[k % 4][:, :],
                                    ALU.mult).then_inc(y_mul, 1)

                def y_lo_part(i, k):
                    dve.wait_ge(yhi_ready, layer * FC + k // 2 + 2 * i + 1)
                    p = k // 2 + 2 * i
                    v.tensor_tensor(blk(y_lo, p), cv[(k + 1) % 4][:, :], blk(y_hi, p).bitcast(F32),
                                    ALU.subtract).then_inc(ylo_ready, 1)

                def later_stages(i, k):
                    static = isinstance(i, int)
                    if not (static and 4 * i + k > UP):
                        up_conv(i, k - 1)
                    if k % 2 == 1 and not (static and 4 * i + k < 3):
                        y_product(i, k - 3)
                    if k % 2 == 0 and not (static and 4 * i + k < 4):
                        y_lo_part(i, k - 4)

                up_lo(0, 0)
                for k in range(2):
                    v.memset(us[k][:, 0:2], 0.0).then_inc(halo, 1)
                rms(norm)
                up_lo(0, 1)
                dve.wait_ge(halo, 2 * (layer + 1))
                dve.wait_ge(rinv_ready, norm + 1)
                up_scale(0, 0)
                up_scale(0, 1)
                later_stages(0, 1)
                for k in (2, 3):
                    up_scale(0, k)
                    up_lo(0, k)
                    later_stages(0, k)
                with dve.Fori(1, UP // 4 - 1) as i:
                    for k in range(4):
                        up_scale(i, k)
                        up_lo(i, k)
                        later_stages(i, k)
                for k in range(4):
                    up_scale(UP // 4 - 1, k)
                    up_lo(UP // 4 - 1, k, UC if k < 4 - SPL else DN[k - 4 + SPL] * P)
                    later_stages(UP // 4 - 1, k)
                def down_lo(i, kk, cols):
                    lo(u_dn + kk + SPL + 8 * i, (u_dn + kk + SPL) % RAW, cols)

                for k in range(4, 4 + DRAIN):
                    if k == 3 + DRAIN:
                        down_lo(0, 0, DN[SPL] * P)
                    later_stages(UP // 4 - 1, k)

                def down_pair(i, final):
                    for kk in range(1, 9):
                        j = kk // 4
                        if kk in (3, 7):
                            res_add(j + 2 * i, B_RES + j, u_dn + kk + 1 + 8 * i)
                        if not final or kk + SPL < 8:
                            down_lo(i, kk, DN[(kk + SPL) % 4] * P)
                        elif next_cols is not None and kk < 8:
                            down_lo(i, kk, next_cols[kk + SPL - 8])
                        if kk in (3, 7):
                            res_split(norm + 1, j + 2 * i, r0 + j + 2 * i, last)

                with dve.Fori(0, KC // 2 - 1) as i:
                    down_pair(i, False)
                down_pair(KC // 2 - 1, True)

            w_out(1, U_OUT0, 0, MIX0)
            ffn(0, 1, U_UP0, U_DN0, KC, [UC] * SPL, False)

            def a_evac1(i):
                n, part = MIX1[i]
                dve.wait_ge(unit_done, U_MIX1 + i + 1)
                src, scale = ps[:, a_bank1(a_before(MIX1, i)), :], rinv[:, :]
                if n == "k":
                    dst = k1[:, part, CHUNK:CHUNK + T]
                else:
                    dst = q1[:, part // 2, :, part % 2, :]
                    src, scale = (t.rearrange("p (c q) -> p c q", q=CHUNK) for t in (src, scale))
                v.tensor_tensor(dst, src, scale, ALU.mult).then_inc(a_taken, 1)

            for name, i, span in SEQ1:
                if name == "unit" and span[1] == 8:
                    if i >= 2 and MIX1[i][0] not in B_PARTS:
                        a_evac1(i)
                elif name == "split":
                    lo_static(U_MIX1 + i + SPL)
                elif name == "ssq":
                    rms(2)
                    v.memset(k1[:, :, 0:CHUNK], 0.0).then_inc(c_pad, 1)
                    v.memset(v1s[0:CHUNK, 0, :], 0.0).then_inc(c_pad, 1)
                elif name == "rinv":
                    dve.wait_ge(rinv_ready, 3)
                    a_evac1(0)
                    a_evac1(1)
                elif name == "s":
                    sc, nm = scs[i % 2], nms[i % 2]
                    dve.wait_ge(c_s, i + 1)
                    if i == 0:
                        dve.wait_ge(bias_loaded, 16)
                    if i >= 2:
                        dve.wait_ge(c_exp, i - 1)
                    v.scalar_tensor_tensor(sc[:, :, :], ps[:, B_SC:B_SC + 2, :].rearrange("p b (c k) -> p (b c) k", k=P),
                                           CD ** -0.5, bias_sb[:, i, :].unsqueeze(1).broadcast_to([P, NCH, P]),
                                           ALU.mult, ALU.add).then_inc(c_bias, 1)
                    dve.wait_ge(c_bias, i + 1)
                    v.memset(sc[:, 0, 0:CHUNK], NEG).then_inc(c_mask, 1)
                    dve.wait_ge(c_mask, i + 1)
                    v.tensor_reduce(mx[:, :], sc[:, :, :], AX.X, ALU.max).then_inc(c_mx, 1)
                    dve.wait_ge(c_mx, i + 1)
                    v.tensor_scalar(nm[:, :], mx[:, :], par[:, S_SINK + i:S_SINK + i + 1], -1.0,
                                    ALU.max, ALU.mult).then_inc(c_nm, 1)
                elif name == "s_norm":
                    pr, rs, es = prs[i % 2], rss[i % 2], ess[i % 2]
                    dve.wait_ge(c_exp, i + 1)
                    v.tensor_tensor(den[:, :], rs[:, :], es[:, :], ALU.add).then_inc(c_den, 1)
                    dve.wait_ge(c_den, i + 1)
                    v.reciprocal(rd[:, :], den[:, :]).then_inc(c_rd, 1)
                    dve.wait_ge(c_rd, i + 1)
                    v.tensor_tensor(pr[:, :, :], pr[:, :, :], rd[:, :].unsqueeze(2).broadcast_to([P, NCH, P]),
                                    ALU.mult).then_inc(c_p, 1)
                elif name == "o" and i % 2 == 1:
                    for b in range(2):
                        dve.wait_ge(o1_hi_ready, i + b)
                        v.tensor_tensor(o1_half(o1_lo, i // 2, b), o1_psum(b), o1_half(o1_hi, i // 2, b).bitcast(F32),
                                        ALU.subtract).then_inc(o1_lo_ready, 1)
            w_out(3, U_OUT1, 2 * KC, MIX1)
            ffn(1, 3, U_UP1, U_DN1, 3 * KC, None, True)

            rms(2 * LAYERS)
            dve.wait_ge(rbc_done, 2 * LAYERS + 1)
            for c in range(KC):
                v.scalar_tensor_tensor(x[:, c, :], x[:, c, :], gain_at(2 * LAYERS, c), ps[:, B_RINV, :],
                                       ALU.mult, ALU.mult).then_inc(out_ready, 1)

        @block.tensor
        def _(pe):
            mm = nc.tensor.matmul

            def three(dst, w, m, first, last, shared=False):
                mm(dst, w[0], m[0], start=first, stop=False, skip_group_check=shared)
                mm(dst, w[0], m[1], start=False, stop=False, skip_group_check=shared)
                return mm(dst, w[1], m[0], start=False, stop=last, skip_group_check=shared)

            def w_blocks(r, c, n=P):
                return tuple(t[r % SPL][:, c * n:(c + 1) * n] for t in (w_hi, w_lo))

            def a_unit(u, r, bank, h_blocks=None, span=(0, KC)):
                if span[0] == 0:
                    pe.wait_ge(w_lo_ready, u + 1)
                for c in range(*span):
                    if h_blocks is not None:
                        pe.wait_ge(lo_ready, h_blocks + c + 1)
                    ins = three(ps[:, bank, :], w_blocks(r, c), (h_hi[:, c, :], h_lo[:, c, :]),
                                c == 0, c == KC - 1)
                if span[1] == KC:
                    ins.then_inc(unit_done, 1)

            def b_unit(u, part, parts, tile, n_cols, span=(0, 8), a_taken_by=None):
                if span[0] == 0:
                    pe.wait_ge(w_lo_ready, u + 1)
                blocks = -(-KC // parts)
                steps = (min(KC, (part + 1) * blocks) - part * blocks) * TT
                for step in range(span[0] * steps // 8, span[1] * steps // 8):
                    half, rest = divmod(step, steps // 2)
                    k, tt = rest // 2, 3 - 2 * half - rest % 2
                    c = part * blocks + k
                    if a_taken_by is not None and c == 0 and tt == 1:
                        pe.wait_ge(a_taken, a_taken_by)
                    tok = slice(tt * P, (tt + 1) * P)
                    ins = three(tile(tt, n_cols), (h_hi[:, c, tok], h_lo[:, c, tok]), w_blocks(u % RAW, k, n_cols),
                                c == 0 and (tile is b_tile or tt % 2 == 1), c == KC - 1, tile is v_tile)
                if span[1] == 8:
                    ins.then_inc(unit_done, 1)

            def ssq_mm(norm):
                if norm == 0:
                    pe.wait_ge(consts, N_CONSTS)
                pe.wait_ge(ssq_added, NADD * (norm + 1))
                for tt in range(TT):
                    ins = mm(ps[:, B_SSQ, tt:tt + 1], ssq[:, tt * P:(tt + 1) * P], ones[:, 0:1],
                             start=True, stop=True)
                ins.then_inc(ssq_col, 1)

            def rinv_mm(norm):
                pe.wait_ge(diag_ready, norm + 1)
                mm(ps[:, B_RINV, :], ones[:, :], diag[:, :], start=True, stop=True).then_inc(rbc_done, 1)

            def out_blocks(units, u0, c, blocks, first, last, o_hi, o_lo, ready):
                if first:
                    pe.wait_ge(w_lo_ready, u0 + c + 1)
                for k in blocks:
                    ready(k)
                    ins = three(ps[:, out_bank(c, units), :], w_blocks((u0 + c) % RAW, k),
                                (o_hi[:, k, :], o_lo[:, k, :]), first and k == blocks[0], last and k == blocks[-1])
                if last:
                    ins.then_inc(unit_done, 1)

            def out_tiles(units, u0, r0, o_hi, o_lo):
                for c in range(2, KC):
                    if c >= 4:
                        pe.wait_ge(x_updated, r0 + c - 1)
                    out_blocks(units, u0, c, range(KC), True, True, o_hi, o_lo, lambda k: None)

            def is_first(seq, at):
                return all(step[:2] != seq[at][:2] for step in seq[:at])

            def is_last(seq, at):
                return all(step[:2] != seq[at][:2] for step in seq[at + 1:])

            def ffn(layer, norm, u_up, u_dn, r0):
                def up(i, k):
                    pe.wait_ge(u_scaled, layer * UP + k - 3 + 4 * i)
                    a_unit(u_up + k + 4 * i, u_up + k, k)

                a_unit(u_up, u_up, 0, norm * KC)
                ssq_mm(norm)
                a_unit(u_up + 1, u_up + 1, 1)
                rinv_mm(norm)
                a_unit(u_up + 2, u_up + 2, 2)
                a_unit(u_up + 3, u_up + 3, 3)
                with pe.Fori(1, UP // 4) as i:
                    for k in range(4):
                        up(i, k)

                def down_pair(i, first):
                    for j in range(2):
                        if not (first and r0 == 0):
                            pe.wait_ge(x_updated, r0 + j - 1 + 2 * i)
                        for k in range(4):
                            kk = u_dn + 4 * j + k
                            pe.wait_ge(w_lo_ready, kk + 1 + 8 * i)
                            if first and j == 0:
                                pe.wait_ge(ylo_ready, layer * FC + DOFF[k] + DN[k])
                            for b in range(DN[k]):
                                c = DOFF[k] + b
                                ins = three(ps[:, B_RES + j, :], w_blocks(kk, b),
                                            (y_hi[:, c, :], y_lo[:, c, :]), c == 0, c == FC - 1)
                            ins.then_inc(unit_done, 1)

                down_pair(0, True)
                with pe.Fori(1, KC // 2) as i:
                    down_pair(i, False)

            pe.wait_ge(consts, 3)
            for _ in range(WARM):
                mm(ps[:, B_RINV, 0:P], ones[:, :], ones[:, :], start=True, stop=True)

            for at, (name, i, span) in enumerate(SEQ0):
                if name == "unit":
                    n, part = MIX0[i]
                    a, b_done = a_before(MIX0, i), b_before(MIX0, i)
                    if n in B_PARTS:
                        if part == 0 and span[0] == 0:
                            if b_done:
                                pe.wait_ge(b_taken, b_done)
                            if n == "va":
                                pe.wait_ge(g_exp, 2)
                        b_unit(i, part, B_PARTS[n], b_tile, B_COLS[n], span,
                               a if a > 2 else None)
                    else:
                        if a >= 4 and span[0] == 0:
                            pe.wait_ge(a_taken, a - 1)
                        if b_done and span[0] == 0:
                            after_group = MIX0[i - 1][0] in B_PARTS
                            pe.wait_ge(b_taken, b_done - TT + 1 if after_group else b_done)
                        a_unit(i, i, a_bank0(a), 0 if i < 2 else None, span)
                elif name == "ssq":
                    ssq_mm(0)
                elif name == "rinv":
                    rinv_mm(0)
                elif name == "z":
                    j, rows = i // 2, slice(SD * (i % 2), SD * (i % 2) + SD)
                    pe.wait_ge(a_taken, a_before(MIX0, MIX0.index(("kb", j))) + 1)
                    pe.wait_ge(consts_dve, 3)
                    pe.wait_ge(sb_w, i)
                    for b in (0, 1, 3, 2):
                        mm(zs[:, ZOFF[b]:ZOFF[b] + ZW[b]], kbT[rows, j, b * P:(b + 1) * P],
                           qbT[rows, j, b * P:T], start=b != 3, stop=False, skip_group_check=True)
                    for b in range(TT):
                        ins = mm(zs[:, ZOFF[b]:ZOFF[b] + P], ident_bf[:, :], negmask[:, :],
                                 start=False, stop=False, skip_group_check=True)
                    ins.then_inc(sb_z, 1)
                elif name == "sfx":
                    pe.wait_ge(sb_lo, i + 1)
                    for b in range(TT):
                        for c in range(b, TT):
                            lhs = negtri if c == b else negones
                            dst = zs[:, ZOFF[b] + (c - b) * P:ZOFF[b] + ZW[b]]
                            for part in (sbH, sbL):
                                ins = mm(dst, lhs[:, :], part[:, ZOFF[c]:ZOFF[c] + ZW[c]],
                                         start=False, stop=c == TT - 1 and part is sbL, skip_group_check=True)
                    ins.then_inc(sb_sum, 1)
                elif name == "pv":
                    j, rows = i // 2, slice(SD * (i % 2), SD * (i % 2) + SD)
                    pe.wait_ge(sb_w, i + 1)
                    pe.wait_ge(oc_lo_ready, j)
                    for b in range(TT):
                        ins = mm(ps[rows, B_O, b * P:T], vb[:, b, i * SD:(i + 1) * SD],
                                 sbS[:, ZOFF[b]:ZOFF[b] + ZW[b]], start=b == 0, stop=b == TT - 1)
                    ins.then_inc(sb_pv, 1)
                elif name == "gt":
                    pe.wait_ge(b_taken, b_before(MIX0, MIX0.index(("kg", 2)) + 1))
                    for tt in range(TT):
                        ins = nc.tensor.transpose(ps[0:RANK, B_G, tt * P:(tt + 1) * P], kg[:, tt, GH * GK:KG],
                                                  ident[:, :])
                    ins.then_inc(g_t, 1)
                elif name == "gz":
                    pe.wait_ge(wg2_loaded, 16)
                    pe.wait_ge(g_tcopy, 1)
                    for tt in range(TT):
                        ins = mm(ps[:, B_G + tt // 2, (tt % 2) * 256:(tt % 2) * 256 + GH * GK],
                                 gaT[:, tt * P:(tt + 1) * P], wg2_sb[:, :], start=True, stop=True)
                    ins.then_inc(g_z, 1)
                elif name == "gs":
                    pe.wait_ge(g_log, 1)
                    for tt in range(TT):
                        ins = mm(ps[:, B_G + tt // 2, (tt % 2) * 256:(tt % 2) * 256 + GH * GK], tri16[:, :],
                                 gL[:, tt * GH * GK:(tt + 1) * GH * GK], start=True, stop=True)
                    ins.then_inc(g_sum, 1)
                elif name == "gd":
                    pe.wait_ge(g_exp, 1)
                    for tt in range(TT):
                        for p in range(GH // 2):
                            col = p * NCH + 2 * tt
                            ins = mm(ps[:, B_G, col:col + 2], gL[:, tt * GH * GK + p * P:tt * GH * GK + (p + 1) * P],
                                     ind16[:, :], start=True, stop=True)
                    ins.then_inc(g_total, 1)
                elif name == "gkv":
                    pe.wait_ge(g_kd, 1)
                    pe.wait_ge(b_taken, B_MIX0)
                    if i:
                        pe.wait_ge(g_state, NCH * i)
                    for h in (2 * i, 2 * i + 1):
                        for c in range(NCH):
                            tok = slice(CHUNK * (c % 2), CHUNK * (c % 2) + CHUNK)
                            ins = mm(ps[GK * (h % 2):GK * (h % 2) + GK, B_G + c % 2, (c // 2) * GV:(c // 2 + 1) * GV],
                                     kg[tok, c // 2, h * GK:(h + 1) * GK], va[tok, c // 2, h * GV:(h + 1) * GV],
                                     start=True, stop=True)
                    ins.then_inc(g_kv, 1)
                elif name == "go":
                    pe.wait_ge(a_taken, a_before(MIX0, MIX0.index(("qa", 1))) + 1)
                    pe.wait_ge(g_state, 2 * NCH)
                    if i:
                        pe.wait_ge(g_ocopy, i)
                    for h in (2 * i, 2 * i + 1):
                        rows = slice(GK * (h % 2), GK * (h % 2) + GK)
                        for c in range(NCH):
                            ins = mm(ps[:, B_G + h % 2, c * CHUNK:(c + 1) * CHUNK], st[i][rows, c, :],
                                     qaT[rows, i, c * CHUNK:(c + 1) * CHUNK], start=True, stop=True)
                    ins.then_inc(g_o, 1)
                elif name == "gn":
                    pe.wait_ge(g_osq, i + 1)
                    pe.wait_ge(g_ocopy, 2)
                    if i:
                        pe.wait_ge(g_lnv, i)
                    for a in range(2):
                        ins = mm(ps[:, B_G + a, :], ones[:, :], gq[i][:, a, :], start=True, stop=True)
                    ins.then_inc(g_osum, 1)
                elif name == "out":
                    if is_first(SEQ0, at):
                        pe.wait_ge(a_taken, A_MIX0 - 1 + i)

                    def ready(k):
                        pe.wait_ge(*((gla_lo_ready, k + 1) if k < GH else (oc_lo_ready, k - GH + 1)))
                    out_blocks(MIX0, U_OUT0, i, span, is_first(SEQ0, at), is_last(SEQ0, at), oc_hi, oc_lo, ready)
            out_tiles(MIX0, U_OUT0, 0, oc_hi, oc_lo)
            ffn(0, 1, U_UP0, U_DN0, KC)

            for at, (name, i, span) in enumerate(SEQ1):
                if name == "unit":
                    n, part = MIX1[i]
                    a = a_before(MIX1, i)
                    if n == "v":
                        b_unit(U_MIX1 + i, part, B_PARTS[n], v_tile, CKV * CD, span)
                    else:
                        if a >= 4 and span[0] == 0:
                            pe.wait_ge(a_taken, A_MIX0 + a - 1)
                        a_unit(U_MIX1 + i, U_MIX1 + i, a_bank1(a), 2 * KC if i == 0 else None, span)
                elif name == "ssq":
                    ssq_mm(2)
                elif name == "rinv":
                    rinv_mm(2)
                elif name == "s":
                    g, hh = i // 2, i % 2
                    rows = slice(CD * hh, CD * hh + CD)
                    for unit in (("k", g // 2), ("q", 2 * g + 1)):
                        pe.wait_ge(a_taken, A_MIX0 + a_before(MIX1, MIX1.index(unit)) + 1)
                    pe.wait_ge(c_pad, 1)
                    pe.wait_ge(c_bias, i)
                    for c in range(NCH):
                        ins = mm(ps[:, B_SC + c // 4, (c % 4) * P:(c % 4 + 1) * P],
                                 q1[rows, g, c, :, :].rearrange("k e q -> k (e q)"),
                                 k1[rows, g // 2, c * CHUNK:c * CHUNK + P], start=True, stop=True)
                    ins.then_inc(c_s, 1)
                elif name == "t":
                    if i == 0:
                        pe.wait_ge(a_taken, A_MIX0 + 4)
                    pe.wait_ge(c_p, i + 1)
                    pe.wait_ge(c_tc, i)
                    for c in range(NCH):
                        ins = nc.tensor.transpose(ps[:, B_T + c // 4, (c % 4) * P:(c % 4 + 1) * P],
                                                  prs[i % 2][:, c, :], ident[:, :])
                    ins.then_inc(c_t, 1)
                elif name == "o":
                    g, hh = i // 2, i % 2
                    kv = 2 * (g // 2) + hh
                    pe.wait_ge(c_tc, i + 1)
                    pe.wait_ge(c_pad, 2)
                    pe.wait_ge(b_taken, B_MIX0 + TT)
                    pe.wait_ge(o1_lo_ready, 2 * g)
                    for sem_v in vs_loaded:
                        pe.wait_ge(sem_v, 16)
                    for c in range(NCH):
                        vals = v1 if c % 2 else v1s
                        ins = mm(ps[CD * hh:CD * hh + CD, B_PV + c // 4, (c % 4) * P:(c % 4 + 1) * P],
                                 vals[:, c // 2, kv * CD:(kv + 1) * CD], prTs[i][:, c, :], start=True, stop=True)
                    ins.then_inc(c_pv, 1)
                elif name == "out":
                    if is_first(SEQ1, at):
                        pe.wait_ge(a_taken, A_MIX0 + a_before(MIX1, N1) - 1 + i)

                    def ready(k):
                        pe.wait_ge(o1_lo_ready, 2 * (k // 2) + 2)
                    out_blocks(MIX1, U_OUT1, i, span, is_first(SEQ1, at), is_last(SEQ1, at), o1_hi, o1_lo, ready)
            out_tiles(MIX1, U_OUT1, 2 * KC, o1_hi, o1_lo)
            ffn(1, 3, U_UP1, U_DN1, 3 * KC)
            ssq_mm(2 * LAYERS)
            rinv_mm(2 * LAYERS)


def t5_bucket(rel):
    buckets, far = 32, 128
    nb = buckets // 2
    exact = nb // 2
    n = np.abs(rel)
    large = exact + (np.log(np.maximum(n, 1) / exact) / np.log(far / exact) * (nb - exact)).astype(np.int32)
    return (np.where(rel > 0, nb, 0) + np.where(n < exact, n, np.minimum(large, nb - 1))).astype(np.int32)


def stationary(w):
    k, n = w.shape
    return w.reshape(k // P, P, n // P, P).transpose(2, 1, 0, 3).reshape(n // P, P, k)


def moving(w):
    k, n = w.shape
    per = UC // n
    parts = -(-k // (P * per))
    w = np.concatenate([w, np.zeros((parts * per * P - k, n), w.dtype)])
    units = w.reshape(parts, per, P, n).transpose(0, 2, 1, 3).reshape(parts, P, per * n)
    return np.concatenate([units, np.zeros((parts, P, UC - per * n), w.dtype)], axis=2)


def columns(a):
    a = np.asarray(a)
    return np.moveaxis(a.reshape(*a.shape[:-1], a.shape[-1] // P, P), -1, 0).reshape(P, -1)


def kernel(x, norm_mix, norm_ffn, norm_final, ab_w_in, ab_w_gate2, ab_b_gate, ab_gla_norm, ab_w_out,
           c_w_qkv, c_sinks, c_w_out, rel_bias, ffn_w_up, ffn_conv_w, ffn_conv_b, ffn_w_down):
    import concourse.bacc as bacc
    from concourse.bass_utils import run_bass_kernel_spmd

    f = [np.asarray(a) for a in (x, norm_mix, norm_ffn, norm_final, ab_w_in, ab_w_gate2, ab_b_gate, ab_gla_norm,
                                 ab_w_out, c_w_qkv, c_sinks, c_w_out, rel_bias, ffn_w_up, ffn_conv_w, ffn_conv_b,
                                 ffn_w_down)]
    (x, norm_mix, norm_ffn, norm_final, w_in, w_gate2, b_gate, gla_norm, w_out0, w_qkv, sinks, w_out1,
     rel_bias, w_up, conv_w, conv_b, w_down) = f

    sizes = [GH * GK, GH * GK, GH * GV, GH * GV, RANK, SH * SD, SH * SD, SH * SD]
    qa, ka, va, ra, ga, qb, kb, vb = np.split(w_in[0], np.cumsum(sizes)[:-1], axis=1)
    parts = {"qa": stationary(qa), "ra": stationary(ra), "qb": stationary(qb),
             "kb": stationary(kb), "kg": moving(np.concatenate([ka, ga], axis=1)), "va": moving(va), "vb": moving(vb)}
    w_mix0 = np.concatenate([np.stack([parts[n][i] for n, i in MIX0]), stationary(w_out0[0])])

    q_heads = [h for a in range(4) for h in (a, 4 + a)] + [h for a in range(4) for h in (8 + a, 12 + a)]
    wq, wk, wv = np.split(w_qkv[0], [CH * CD, CH * CD + CKV * CD], axis=1)
    wq = wq.reshape(D, CH, CD)[:, q_heads].reshape(D, CH * CD)
    parts = {"q": stationary(wq), "k": stationary(wk), "v": moving(wv)}
    wo = w_out1[0].reshape(CH, CD, D)[q_heads].reshape(CH * CD, D)
    w_mix1 = np.concatenate([np.stack([parts[n][i] for n, i in MIX1]), stationary(wo)])

    turns = [t for i in range(FC) for t in (i, FC + i)]
    up = np.concatenate([stationary(w_up[layer])[turns] for layer in range(LAYERS)])
    down = np.concatenate([stationary(w_down[layer]) for layer in range(LAYERS)])
    conv = np.concatenate([conv_w, conv_b[:, None]], axis=1)
    conv = conv.reshape(LAYERS, 4, UP, P)[:, :, turns].transpose(3, 0, 2, 1).reshape(P, -1)

    pairs = [8 * (n // 4) + 4 * (n % 2) + 2 * ((n // 2) % 2) for n in range(CH // 2)]
    sink_cols = np.stack([np.repeat(sinks[0, [h, h + 1]], CHUNK) for h in pairs], axis=1)
    rel = np.arange(2 * CHUNK)[None, :] - (CHUNK + np.arange(CHUNK)[:, None])
    by_head = rel_bias[t5_bucket(rel)]
    bias = np.stack([np.concatenate([by_head[:, :, h], by_head[:, :, h + 1]]) for h in pairs], axis=1).reshape(P, -1)

    gains = np.concatenate([columns(norm_mix[0]), columns(norm_ffn[0]), columns(norm_mix[1]),
                            columns(norm_ffn[1]), columns(norm_final)], axis=1)
    small = np.concatenate([gains, columns(gla_norm[0]), conv, sink_cols], axis=1)
    arrays = {
        "xT": columns_of_tokens(x[0]),
        "w_mix0": w_mix0, "w_mix1": w_mix1, "w_up": up, "w_down": down, "small": small,
        "wg2": np.concatenate([w_gate2[0], b_gate]), "bias": bias,
    }
    arrays = {n: np.ascontiguousarray(a) for n, a in arrays.items()}

    nc = bacc.Bacc("TRN2", target_bir_lowering=False, num_devices=1)
    aps = {n: nc.dram_tensor(n, a.shape, F32, kind="ExternalInput").ap() for n, a in arrays.items()}
    out = nc.dram_tensor("out", (P, KC * T), F32, kind="ExternalOutput").ap()
    trunk(nc, *aps.values(), out)
    got = run_bass_kernel_spmd(nc, [arrays], core_ids=[0]).results[0]["out"]
    return np.ascontiguousarray(got.reshape(P, KC, T).transpose(2, 1, 0).reshape(1, T, D))


def columns_of_tokens(a):
    return a.T.reshape(KC, P, T).transpose(1, 0, 2).reshape(P, KC * T)
```
